# Optimizing a Trainium2 kernel written in Bass

```python
import math
import jax, jax.numpy as jnp
from jax import lax
import numpy as np

D_MODEL = 1024
BATCH = 1
SEQ = 1024
DEPTH = 1

GRID_W = 64
CTX_LEN = 256
EPS = 1e-6
MLA_HEADS = 8
MLA_Q_RANK = 256
MLA_KV_RANK = 128
MLA_NOPE = 64
MLA_ROPE = 32
MLA_V = 64
MLA_SCALE = (MLA_NOPE + MLA_ROPE) ** -0.5
ROPE_BASE = 10000.0
Q_BLOCK = 128
DN_HEADS = 4
DN_DK = 128
DN_DV = 128
DN_QKV = 2 * DN_HEADS * DN_DK + DN_HEADS * DN_DV
CONV_W = 5
CHUNK = 64
N_GROUPS = 4
EXPERTS_PER_GROUP = 8
N_EXPERTS = N_GROUPS * EXPERTS_PER_GROUP
TOP_K = 2
EXPERT_FF = 512
MOE_BLOCK = 128
MIX_WIDTH = MLA_HEADS * MLA_V + DN_HEADS * DN_DV
IN_SPLITS = (MLA_Q_RANK, MLA_KV_RANK, MLA_ROPE, DN_QKV, DN_HEADS * DN_DV, 2 * DN_HEADS, 2 * DN_HEADS)
IN_WIDTH = 2480

kernel_name = "hybrid_mla_gdn_hmoe_diffusion_block"

def rmsnorm(x, gain):
    xf = x.astype(jnp.float32)
    y = xf * lax.rsqrt(jnp.mean(xf * xf, axis=-1, keepdims=True) + EPS)
    return (y * gain.astype(jnp.float32)).astype(x.dtype)

def l2norm(t):
    tf = t.astype(jnp.float32)
    return tf * lax.rsqrt(jnp.sum(tf * tf, axis=-1, keepdims=True) + EPS)

def split_cols(t, sizes):
    return jnp.split(t, np.cumsum(sizes)[:-1].tolist(), axis=-1)

def axial_rope_angles(rows):
    row = jnp.repeat(jnp.arange(rows, dtype=jnp.float32), GRID_W)
    col = jnp.tile(jnp.arange(GRID_W, dtype=jnp.float32), rows)
    half = MLA_ROPE // 2
    inv_freq = ROPE_BASE ** (-jnp.arange(0, half, 2, dtype=jnp.float32) / half)
    ang = jnp.concatenate([row[:, None] * inv_freq, col[:, None] * inv_freq], axis=-1)
    return jnp.cos(ang), jnp.sin(ang)

def apply_rope(x, cos, sin):
    xp = x.astype(jnp.float32).reshape(*x.shape[:-1], MLA_ROPE // 2, 2)
    x0, x1 = xp[..., 0], xp[..., 1]
    out = jnp.stack([x0 * cos - x1 * sin, x0 * sin + x1 * cos], axis=-1)
    return out.reshape(x.shape).astype(x.dtype)

def mla_project(q_lat, kv_lat, k_rope, p):
    B, L, _ = q_lat.shape
    q = (rmsnorm(q_lat, p["mla_q_norm"]) @ p["w_q_up"]).reshape(B, L, MLA_HEADS, MLA_NOPE + MLA_ROPE)
    kv = (rmsnorm(kv_lat, p["mla_kv_norm"]) @ p["w_kv_up"]).reshape(B, L, MLA_HEADS, MLA_NOPE + MLA_V)
    return q[..., :MLA_NOPE], q[..., MLA_NOPE:], kv[..., :MLA_NOPE], k_rope, kv[..., MLA_NOPE:]

def mla_attend(qn, qr, kn, kr, v):
    s = jnp.einsum('bqhd,bkhd->bhqk', qn, kn) + jnp.einsum('bqhr,bkr->bhqk', qr, kr)
    prob = jax.nn.softmax(s.astype(jnp.float32) * MLA_SCALE, axis=-1).astype(v.dtype)
    return jnp.einsum('bhqk,bkhd->bqhd', prob, v)

def mla_latent_attention(qn, qr, kn, kr, v):
    B, L, H, _ = qn.shape
    nb = L // Q_BLOCK
    blocks = lambda t: t.reshape(B, nb, Q_BLOCK, *t.shape[2:]).swapaxes(0, 1)
    o = lax.map(lambda qs: mla_attend(qs[0], qs[1], kn, kr, v), (blocks(qn), blocks(qr)))
    return o.swapaxes(0, 1).reshape(B, L, H * MLA_V)

def short_conv(t, w):
    C = t.shape[-1]
    y = lax.conv_general_dilated(t, w[:, None, :], window_strides=(1,),
                                 padding=[(CONV_W // 2, CONV_W // 2)],
                                 dimension_numbers=('NWC', 'WIO', 'NWC'), feature_group_count=C)
    return jax.nn.silu(y)

def dn_inputs(qkv, b_logit, a_logit, p):
    B, L, _ = qkv.shape
    q, k, v = split_cols(short_conv(qkv, p["dn_conv"]), (DN_HEADS * DN_DK, DN_HEADS * DN_DK, DN_HEADS * DN_DV))
    q = l2norm(q.reshape(B, L, DN_HEADS, DN_DK)) * DN_DK ** -0.5
    k = l2norm(k.reshape(B, L, DN_HEADS, DN_DK))
    v = v.reshape(B, L, DN_HEADS, DN_DV).astype(jnp.float32)
    beta = jax.nn.sigmoid(b_logit.astype(jnp.float32).reshape(B, L, 2, DN_HEADS))
    g = -jnp.exp(p["dn_A_log"].astype(jnp.float32)) * jax.nn.softplus(
        a_logit.astype(jnp.float32).reshape(B, L, 2, DN_HEADS) + p["dn_dt_bias"].astype(jnp.float32))
    return q, k, v, g, beta

def gated_delta_chunked(q, k, v, g, beta, s0):
    B, L, H, DK = q.shape
    DV = v.shape[-1]
    n = L // CHUNK

    def to_chunks(t):
        t = jnp.moveaxis(t.astype(jnp.float32), 2, 1)
        return t.reshape(B, H, n, CHUNK, *t.shape[3:])

    q, k, v, g, beta = (to_chunks(t) for t in (q, k, v, g, beta))
    gc = jnp.cumsum(g, axis=-1)
    idx = jnp.arange(CHUNK)
    incl = idx[:, None] >= idx[None, :]
    strict = idx[:, None] > idx[None, :]
    decay = jnp.exp(jnp.where(incl, gc[..., :, None] - gc[..., None, :], -jnp.inf))
    kb = k * beta[..., None]
    lmat = jnp.where(strict, jnp.einsum('bhnid,bhnjd->bhnij', kb, k) * decay, 0.0)
    a = lmat + jnp.eye(CHUNK, dtype=jnp.float32)
    u = lax.linalg.triangular_solve(a, v * beta[..., None], left_side=True, lower=True, unit_diagonal=True)
    w = lax.linalg.triangular_solve(a, kb * jnp.exp(gc)[..., None], left_side=True, lower=True, unit_diagonal=True)
    intra = jnp.einsum('bhnid,bhnjd->bhnij', q, k) * decay
    q_dec = q * jnp.exp(gc)[..., None]
    k_dec = k * jnp.exp(gc[..., -1:] - gc)[..., None]
    g_last = jnp.exp(gc[..., -1])

    def step(S, xs):
        u_i, w_i, intra_i, qd_i, kd_i, gl_i = xs
        v_new = u_i - jnp.einsum('bhck,bhkv->bhcv', w_i, S)
        o_i = jnp.einsum('bhck,bhkv->bhcv', qd_i, S) + jnp.einsum('bhij,bhjv->bhiv', intra_i, v_new)
        S = S * gl_i[..., None, None] + jnp.einsum('bhck,bhcv->bhkv', kd_i, v_new)
        return S, o_i

    xs = tuple(jnp.moveaxis(t, 2, 0) for t in (u, w, intra, q_dec, k_dec, g_last))
    s_final, o = lax.scan(step, s0, xs)
    o = jnp.transpose(o, (1, 0, 3, 2, 4)).reshape(B, L, H, DV)
    return o, s_final

def bidir_scan(q, k, v, g, beta, s0_f, s0_b):
    flip = lambda t: jnp.flip(t, axis=1)
    o_f, s_f = gated_delta_chunked(q, k, v, g[:, :, 0], beta[:, :, 0], s0_f)
    o_b, s_b = gated_delta_chunked(flip(q), flip(k), flip(v), flip(g[:, :, 1]), flip(beta[:, :, 1]), s0_b)
    return o_f + flip(o_b), s_f, s_b

def dn_output(o, z, gain):
    B, L = o.shape[:2]
    zf = z.astype(jnp.float32).reshape(B, L, DN_HEADS, DN_DV)
    return (rmsnorm(o, gain) * jax.nn.silu(zf)).reshape(B, L, DN_HEADS * DN_DV)

def token_mixer(h, hc, cos, sin, p, with_ctx):
    B, L, _ = h.shape
    C = hc.shape[1]
    q_lat, kv_lat, k_rope, qkv, z, b_logit, a_logit = split_cols(h @ p["w_in"], IN_SPLITS)
    q_lat_c, kv_lat_c, k_rope_c, qkv_c, z_c, b_logit_c, a_logit_c = split_cols(hc @ p["w_in"], IN_SPLITS)

    qn, qr, kn, kr, v = mla_project(q_lat, kv_lat, k_rope, p)
    qr = apply_rope(qr, cos[None, :, None, :], sin[None, :, None, :])
    kr = apply_rope(kr, cos[None], sin[None])
    qn_c, qr_c, kn_c, kr_c, v_c = mla_project(q_lat_c, kv_lat_c, k_rope_c, p)
    mla_lat = mla_latent_attention(qn, qr, jnp.concatenate([kn, kn_c], axis=1),
                                   jnp.concatenate([kr, kr_c], axis=1), jnp.concatenate([v, v_c], axis=1))

    qd, kd, vd, gd, bd = dn_inputs(qkv, b_logit, a_logit, p)
    qd_c, kd_c, vd_c, gd_c, bd_c = dn_inputs(qkv_c, b_logit_c, a_logit_c, p)
    s0 = jnp.zeros((B, DN_HEADS, DN_DK, DN_DV), jnp.float32)
    o_c, s_ctx_f, s_ctx_b = bidir_scan(qd_c, kd_c, vd_c, gd_c, bd_c, s0, s0)
    o_l, _, _ = bidir_scan(qd, kd, vd, gd, bd, s_ctx_f, s_ctx_b)
    dn_lat = dn_output(o_l, z, p["dn_norm"]).astype(h.dtype)

    y_lat = jnp.concatenate([mla_lat, dn_lat], axis=-1) @ p["w_out"]
    if not with_ctx:
        return y_lat, None
    mla_ctx = mla_attend(qn_c, qr_c, kn_c, kr_c, v_c).reshape(B, C, MLA_HEADS * MLA_V)
    dn_ctx = dn_output(o_c, z_c, p["dn_norm"]).astype(hc.dtype)
    y_ctx = jnp.concatenate([mla_ctx, dn_ctx], axis=-1) @ p["w_out"]
    return y_lat, y_ctx

def moe_dispatch(h, expert_idx, combine_w, w1, w3, w2):
    N, D = h.shape
    NK = N * TOP_K
    flat_e = expert_idx.reshape(NK).astype(jnp.int32)
    order = jnp.argsort(flat_e)
    sorted_e = flat_e[order]
    counts = jnp.bincount(flat_e, length=N_EXPERTS).astype(jnp.int32)
    padded = (counts + MOE_BLOCK - 1) // MOE_BLOCK * MOE_BLOCK
    pad_end = jnp.cumsum(padded)
    pad_start = pad_end - padded
    start = jnp.cumsum(counts) - counts
    dest = pad_start[sorted_e] + jnp.arange(NK, dtype=jnp.int32) - start[sorted_e]
    n_blocks = -(-(NK + N_EXPERTS * (MOE_BLOCK - 1)) // MOE_BLOCK)
    rows = n_blocks * MOE_BLOCK
    row_token = jnp.full((rows,), N, jnp.int32).at[dest].set((order // TOP_K).astype(jnp.int32))
    block_expert = jnp.minimum(
        jnp.searchsorted(pad_end, jnp.arange(n_blocks, dtype=jnp.int32) * MOE_BLOCK, side='right'),
        N_EXPERTS - 1).astype(jnp.int32)
    h_pad = jnp.concatenate([h, jnp.zeros((1, D), h.dtype)], axis=0)
    xb = h_pad[row_token].reshape(n_blocks, MOE_BLOCK, D)

    def expert_block(args):
        xs, e = args
        return (jax.nn.silu(xs @ w1[e]) * (xs @ w3[e])) @ w2[e]

    yb = lax.map(expert_block, (xb, block_expert)).reshape(rows, D)
    slot = jnp.zeros((NK,), jnp.int32).at[order].set(dest)
    return jnp.einsum('nkd,nk->nd', yb[slot].reshape(N, TOP_K, D), combine_w)

def hier_moe(h, p):
    g_logits = (h @ p["w_router_group"] + p["b_router_group"]).astype(jnp.float32)
    grp = jnp.argmax(g_logits, axis=-1).astype(jnp.int32)
    p_grp = jnp.take_along_axis(jax.nn.softmax(g_logits, axis=-1), grp[:, None], axis=-1)
    e_all = (jnp.einsum('nd,gde->nge', h, p["w_router_expert"]) + p["b_router_expert"]).astype(jnp.float32)
    e_logits = jnp.take_along_axis(e_all, grp[:, None, None], axis=1)[:, 0]
    top_val, top_loc = lax.top_k(e_logits, TOP_K)
    combine = jax.nn.softmax(top_val, axis=-1) * p_grp
    expert_idx = grp[:, None] * EXPERTS_PER_GROUP + top_loc.astype(jnp.int32)
    return moe_dispatch(h, expert_idx, combine.astype(h.dtype), p["w_exp_gate"], p["w_exp_up"], p["w_exp_down"])

def layer_forward(x, xc, mod, mod_c, cos, sin, p, with_ctx):
    B, L, D = x.shape
    sh1, sc1, g1, sh2, sc2, g2 = jnp.split(mod[:, None, :], 6, axis=-1)
    csh1, csc1, cg1, csh2, csc2, cg2 = jnp.split(mod_c, 6, axis=-1)
    h = rmsnorm(x, p["norm_mix_pre"]) * (1 + sc1) + sh1
    hc = rmsnorm(xc, p["norm_mix_pre"]) * (1 + csc1) + csh1
    y, yc = token_mixer(h, hc, cos, sin, p, with_ctx)
    x = x + g1 * rmsnorm(y, p["norm_mix_post"])
    h = rmsnorm(x, p["norm_ffn_pre"]) * (1 + sc2) + sh2
    x = x + g2 * rmsnorm(hier_moe(h.reshape(B * L, D), p).reshape(B, L, D), p["norm_ffn_post"])
    if with_ctx:
        xc = xc + cg1 * rmsnorm(yc, p["norm_mix_post"])
        hc = rmsnorm(xc, p["norm_ffn_pre"]) * (1 + csc2) + csh2
        xc = xc + cg2 * rmsnorm(hier_moe(hc.reshape(-1, D), p).reshape(xc.shape), p["norm_ffn_post"])
    return x, xc

def setup_inputs(seed: int = 0) -> dict:
    key = jax.random.key(seed)
    ks = iter(jax.random.split(key, 40))
    nrm = lambda shape, scale: jax.random.normal(next(ks), shape, jnp.float32) * scale
    gain = lambda shape: 1.0 + nrm(shape, 0.02)
    L = DEPTH
    dt = jnp.exp(jax.random.uniform(next(ks), (L, 2, DN_HEADS), jnp.float32,
                                    minval=math.log(1e-3), maxval=math.log(1e-1)))
    a_init = jax.random.uniform(next(ks), (L, 2, DN_HEADS), jnp.float32, minval=1.0, maxval=16.0)
    return {
        "x": nrm((BATCH, SEQ, D_MODEL), 1.0),
        "c": nrm((BATCH, D_MODEL), 1.0),
        "ctx": nrm((BATCH, CTX_LEN, D_MODEL), 1.0),
        "c_ctx": nrm((D_MODEL,), 1.0),
        "w_ada": nrm((L, D_MODEL, 6 * D_MODEL), 0.5 * D_MODEL ** -0.5),
        "b_ada": nrm((L, 6 * D_MODEL), 0.02),
        "norm_mix_pre": gain((L, D_MODEL)),
        "norm_mix_post": gain((L, D_MODEL)),
        "norm_ffn_pre": gain((L, D_MODEL)),
        "norm_ffn_post": gain((L, D_MODEL)),
        "w_in": nrm((L, D_MODEL, IN_WIDTH), D_MODEL ** -0.5),
        "mla_q_norm": gain((L, MLA_Q_RANK)),
        "w_q_up": nrm((L, MLA_Q_RANK, MLA_HEADS * (MLA_NOPE + MLA_ROPE)), MLA_Q_RANK ** -0.5),
        "mla_kv_norm": gain((L, MLA_KV_RANK)),
        "w_kv_up": nrm((L, MLA_KV_RANK, MLA_HEADS * (MLA_NOPE + MLA_V)), MLA_KV_RANK ** -0.5),
        "dn_conv": nrm((L, CONV_W, DN_QKV), CONV_W ** -0.5),
        "dn_A_log": jnp.log(a_init),
        "dn_dt_bias": dt + jnp.log(-jnp.expm1(-dt)),
        "dn_norm": gain((L, DN_DV)),
        "w_out": nrm((L, MIX_WIDTH, D_MODEL), MIX_WIDTH ** -0.5),
        "w_router_group": nrm((L, D_MODEL, N_GROUPS), D_MODEL ** -0.5),
        "b_router_group": nrm((L, N_GROUPS), 0.01),
        "w_router_expert": nrm((L, N_GROUPS, D_MODEL, EXPERTS_PER_GROUP), D_MODEL ** -0.5),
        "b_router_expert": nrm((L, N_GROUPS, EXPERTS_PER_GROUP), 0.01),
        "w_exp_gate": nrm((L, N_EXPERTS, D_MODEL, EXPERT_FF), D_MODEL ** -0.5),
        "w_exp_up": nrm((L, N_EXPERTS, D_MODEL, EXPERT_FF), D_MODEL ** -0.5),
        "w_exp_down": nrm((L, N_EXPERTS, EXPERT_FF, D_MODEL), EXPERT_FF ** -0.5),
    }

def reference(x, c, ctx, c_ctx, w_ada, b_ada, norm_mix_pre, norm_mix_post, norm_ffn_pre, norm_ffn_post,
              w_in, mla_q_norm, w_q_up, mla_kv_norm, w_kv_up, dn_conv, dn_A_log, dn_dt_bias, dn_norm, w_out,
              w_router_group, b_router_group, w_router_expert, b_router_expert,
              w_exp_gate, w_exp_up, w_exp_down):
    ROWS = x.shape[1] // GRID_W
    cos, sin = axial_rope_angles(ROWS)
    silu_c = jax.nn.silu(c)
    silu_cc = jax.nn.silu(c_ctx)
    xc = ctx
    for layer in range(DEPTH):
        p = dict(w_in=w_in[layer], mla_q_norm=mla_q_norm[layer], w_q_up=w_q_up[layer],
                 mla_kv_norm=mla_kv_norm[layer], w_kv_up=w_kv_up[layer], dn_conv=dn_conv[layer],
                 dn_A_log=dn_A_log[layer], dn_dt_bias=dn_dt_bias[layer], dn_norm=dn_norm[layer],
                 w_out=w_out[layer], norm_mix_pre=norm_mix_pre[layer], norm_mix_post=norm_mix_post[layer],
                 norm_ffn_pre=norm_ffn_pre[layer], norm_ffn_post=norm_ffn_post[layer],
                 w_router_group=w_router_group[layer], b_router_group=b_router_group[layer],
                 w_router_expert=w_router_expert[layer], b_router_expert=b_router_expert[layer],
                 w_exp_gate=w_exp_gate[layer], w_exp_up=w_exp_up[layer], w_exp_down=w_exp_down[layer])
        mod = silu_c @ w_ada[layer] + b_ada[layer]
        mod_c = silu_cc @ w_ada[layer] + b_ada[layer]
        x, xc = layer_forward(x, xc, mod, mod_c, cos, sin, p, layer + 1 < DEPTH)
    return x


_drawn_inputs = setup_inputs


def setup_inputs(seed=0):
    import zlib

    import numpy as np

    out = dict(_drawn_inputs(seed))
    spreads = {}
    factors = {'norm_ffn_post': 8.0,
     'mla_q_norm': 5.366,
     'mla_kv_norm': 4.263,
     'b_router_group': 2.687,
     'b_router_expert': 3.29}
    for name, (base, spread) in spreads.items():
        noise = np.random.default_rng([zlib.crc32(name.encode()), seed]).standard_normal(out[name].shape)
        drawn = base * np.exp(spread * noise) if base else spread * noise
        out[name] = __import__('jax').numpy.asarray(drawn.astype(out[name].dtype))
    for name, factor in factors.items():
        out[name] = (out[name] * factor).astype(out[name].dtype)
    return out
```

```python
from contextlib import ExitStack

import numpy as np

import concourse.bass as bass
from concourse import mybir

ALU = mybir.AluOpType
ACT = mybir.ActivationFunctionType
AX_X = mybir.AxisListType.X
F32 = mybir.dt.float32
BF16 = mybir.dt.bfloat16
I32 = mybir.dt.int32
U32 = mybir.dt.uint32

P = 128
D = 1024
KT = D // P
SEQ = 1024
CTX = 256
TOK = SEQ + CTX
TT = TOK // P
LT = SEQ // P
EPS = 1e-6
CHUNKS = [(0, 512), (512, 512), (1024, 256)]

H = 8
NOPE, ROPE, VD = 64, 32, 64
QR, KVR = 256, 128
SCALE = (NOPE + ROPE) ** -0.5
WA = QR + KVR + 16
DH = 4
DK = 128
CONV = 5
HALO = CONV // 2
CW = SEQ + CTX + 2 * HALO
RAW = CW + 2 * HALO
LEVELS = [2, 4, 8, 16, 32, 64]

E = 32
EG = 8
G = 4
TOPK = 2
FF = 512
FT = FF // P
EXTRA = TOPK * SEQ // P - 1
COLS = 48
RW = G + E


def shape_constants():
    i = np.arange(P)
    c = {}
    ident = np.eye(P)
    tri_f = (i[:, None] <= i[None, :]).astype(float)
    tri_b = (i[:, None] >= i[None, :]).astype(float)
    strict = (i[:, None] < i[None, :]).astype(float)
    iota = np.tile(i[None, :], (P, 1)).astype(float)
    tok = (i[:, None] + P * np.arange(LT)[None, :]).astype(float)
    c["base"] = np.concatenate([ident, np.ones((P, P)), tri_f, tri_b], axis=1)
    steps = np.tile(P * np.arange(1.0, 9.0)[None, :], (P, 1))
    falling = np.tile(E - np.arange(float(E))[None, :], (P, 1))
    c["route"] = np.concatenate([strict, iota, tok, steps, falling], axis=1)
    low, neg = [], []
    for back in (False, True):
        for s in [1] + LEVELS:
            bi, bj = i[None, :] // s, i[:, None] // s
            m = (bi % 2 == 0) & (bj == bi + 1) if back else (bi % 2 == 1) & (bj == bi - 1)
            low.append(-m.astype(float))
        keep = i[:, None] >= i[None, :] if back else i[:, None] <= i[None, :]
        neg.append(np.where(keep, 0.0, -1e30))
    c["masks"] = np.concatenate(low + neg, axis=1)
    half = ROPE // 2
    inv = (10000.0 ** (-np.arange(0, half, 2, dtype=np.float32) / half)).astype(np.float32)
    rows, cols = np.arange(SEQ) // 64, np.arange(SEQ) % 64
    ang = np.concatenate([rows[:, None].astype(np.float32) * inv, cols[:, None].astype(np.float32) * inv], axis=1)
    cos, sin = np.cos(ang), np.sin(ang)
    rope = np.zeros((P, SEQ))
    rope[64:96] = np.repeat(cos, 2, axis=1).T
    rope[96:128] = np.stack([-sin, sin], axis=-1).reshape(SEQ, ROPE).T
    c["rope"] = rope
    return {k: np.ascontiguousarray(v.astype(np.float32)) for k, v in c.items()}


class Banks:

    def __init__(self, full, free):
        self.full_sem, self.free_sem = full, free
        self.uses = [0] * 8
        self.freed = [0] * 8
        self.jobs, self.parts = {}, {}

    def plan(self, key, bank, parts=1):
        self.jobs[key] = (bank, self.uses[bank] + 1, self.freed[bank])
        self.parts[key] = parts
        self.uses[bank] += 1
        self.freed[bank] += parts

    def bank(self, key):
        return self.jobs[key][0]

    def acquire(self, pe, key):
        bank, _, before = self.jobs[key]
        if before:
            pe.wait_ge(self.free_sem[bank], before)
        return bank

    def filled(self, ins, key):
        ins.then_inc(self.full_sem[self.jobs[key][0]], 1)

    def await_full(self, eng, key):
        bank, use, _ = self.jobs[key]
        eng.wait_ge(self.full_sem[bank], use)
        return bank

    def release(self, ins, key):
        ins.then_inc(self.free_sem[self.jobs[key][0]], 1)

    def await_read(self, eng, key):
        bank, _, before = self.jobs[key]
        eng.wait_ge(self.free_sem[bank], before + self.parts[key])


class Chain:

    def __init__(self, eng, sem):
        self.eng, self.sem, self.count = eng, sem, 0

    def __call__(self, ins):
        ins.then_inc(self.sem, 1)
        self.count += 1
        self.eng.wait_ge(self.sem, self.count)


class Arena:

    def __init__(self, tensor, size):
        self.tensor, self.size, self.top = tensor, size, 0

    def take(self, *dims):
        n = int(np.prod(dims))
        v = self.tensor[:, self.top:self.top + n]
        self.top += n
        assert self.top <= self.size, self.top
        if len(dims) == 2:
            v = v.rearrange("p (a b) -> p a b", b=dims[1])
        elif len(dims) == 3:
            v = v.rearrange("p (a b c) -> p a b c", b=dims[1], c=dims[2])
        return v


def bc(ap, shape):
    return ap.unsqueeze(2).to_broadcast(shape)


def mid(ap, n):
    return ap.unsqueeze(1).to_broadcast([P, n, ap.shape[-1]])


def hybrid_block_kernel(nc, io, stop=99):
    with ExitStack() as ctx:
        sem = lambda name: ctx.enter_context(nc.semaphore(name))
        size = 53200
        arena = Arena(ctx.enter_context(nc.sbuf_tensor("arena", [P, size], F32)), size)
        ps = ctx.enter_context(nc.psum_tensor("ps", [P, 8, 512], F32))
        banks = Banks([sem(f"bank_full{b}") for b in range(8)], [sem(f"bank_read{b}") for b in range(8)])
        dram = lambda name, *shape: nc.dram_tensor(name, shape, F32, kind="Internal").ap()

        take = arena.take
        ident, ones, tri_f, tri_b = (take(P) for _ in range(4))
        base = arena.tensor[:, 0:4 * P]
        b_ada = take(6, KT)
        gains = take(4, KT)
        q_gain, kv_gain, dn_gain = take(2), take(1), take(1)
        conv_w = take(12, CONV)
        c_col = take(2, KT)
        sc_col = take(KT, 2)
        modc = take(6, 2, KT)
        mix_scale = take(2, KT)
        ffn_scale = take(KT)
        eps_col = take(1)
        neg_a, dt_col = take(8), take(8)
        ssx, sdx, rx = take(TT), take(TT), take(TT)
        ss_a, sd_a, r_a = take(TT, 2), take(TT, 2), take(TT, 2)
        ba = take(TT, 16)
        rope = take(SEQ)
        zero = take(P)
        gate = [take(2 * TT * DH) for _ in range(9)]
        g_all, beta, gc, ngc, egc, bege, egl, kdc, gtmp = gate
        persistent_top = arena.top

        z = take(LT, DH * DK)
        qT = take(DH, SEQ)
        kT = take(DH, TOK)
        vT = take(DH, TOK)
        qnT = take(2, SEQ)
        kvnT = take(TOK)
        krT = take(TOK)
        mixer_top = arena.top

        hT = take(KT, TOK)
        w_a = take(KT, WA)
        w_r = take(KT, P)
        after_wr = arena.top
        arena.top = mixer_top + KT * TOK
        w_z = take(KT, DH * DK)
        arena.top = max(arena.top, after_wr)
        ring_top = arena.top
        x_ring = take(3, D)
        arena.top = ring_top
        w_c = take(3, KT, P)
        ada_top = arena.top
        w_ada = take(2, 4, D)
        arena.top = ada_top
        raw = take(2, RAW)
        acc = take(2, CW)
        sq, rn = take(CW), take(CW)
        raw_end = arena.top
        arena.top = max(ada_top + 8 * D, raw_end)
        an = take(2, QR + KVR)
        rope_tmp = an.rearrange("p a b -> p (a b)")
        junk = take(D // 2).bitcast(BF16)
        in_proj_top = arena.top
        gt_rows = rope_tmp[:, 0:2 * P]

        arena.top = mixer_top
        nlm = take(2, 6, DH * P)
        rows = take(2, DH, 2 * P)
        intra = take(2, 2, DH * P)
        assert arena.top == mixer_top + KT * TOK
        masks = take(16, P)
        et = take(2, DH * P)
        U = take(2, 2, DH * P)
        T = take(2, DH * P)
        Y = take(2, DH * P)
        R, kd, Vn, o1, S = (take(2, DH * P) for _ in range(5))
        ks = take(DH * P)
        oacc = take(LT, DH * DK)
        dn_top = arena.top

        z_at, qk_at, v_at = persistent_top, persistent_top + LT * DH * DK, persistent_top + LT * DH * DK + DH * (SEQ + TOK)
        arena.top = z_at
        atto = take(LT, H * VD)
        assert arena.top == qk_at
        mixT = take(KT, SEQ)
        arena.top = v_at
        w_q = take(2, H * P)
        w_k, w_v = take(H * NOPE), take(H * VD)
        qa = take(2, SEQ)
        assert arena.top == v_at + DH * TOK
        arena.top = mixer_top
        ka = take(2, TOK)
        V = take(TT * H, VD + 1)
        qb = take(SEQ).bitcast(BF16)
        kb = take(TOK).bitcast(BF16)
        PT = take(2, TT, 512)
        mx, rden = take(2, LT), take(LT, 4)
        ssd, rd = take(LT, DH), take(LT, DH)
        rot = take(512)
        assert arena.top <= dn_top - 4096 - 1536, arena.top

        WB = 3 * KT * FF
        wbuf = [arena.tensor[:, v_at:v_at + WB], arena.tensor[:, z_at:z_at + WB]]
        UP_AT, DOWN_AT = KT * FF, 2 * KT * FF

        def slot_of(n):
            return v_at - (n % 2) * (v_at - z_at)

        def weights(n, at, row, rows=1):
            return arena.tensor[:, bass.ds(slot_of(n) + (at + row * 512), rows * 512)]
        arena.top = v_at + WB
        wo1_at = arena.top
        wo1 = take(KT, 512)
        x2 = take(LT, D)
        gate2 = take(D)
        w_rt, b_rt, logits = take(KT, RW), take(RW), take(LT, RW)
        route = take(2 * P + LT + 8 + E)
        cw = take(TOPK, LT)
        dest = take(TOPK * LT).bitcast(I32)
        idx = take(COLS + 2).bitcast(I32)
        table = take(64).bitcast(I32)
        idx_cur = take(1).bitcast(I32)
        ssf, rf = take(LT), take(LT)
        tmp_at = arena.top
        h2T = take(2, KT, P)
        xr = take(2, D)
        gate1 = take(D)
        junk3 = take(512).bitcast(BF16)
        ssy, ry = take(LT, 2), take(LT)
        ssz, rz = take(LT), take(LT)
        y_top = arena.top
        arena.top = tmp_at
        og, gx = take(LT * G), take(LT * G)
        em, tmp = take(LT * E), take(TOPK * LT * E)
        oh = take(TOPK, LT * E)
        mark, before = take(LT * E), take(LT * E)
        marks_all = take(E)
        small = [take(TOPK * LT) for _ in range(8)]
        gsum, vtop, ktop = take(LT), take(TOPK, LT), take(LT)
        cmp8 = take(TOPK * LT, 8)
        ext_b, base_row, flags = take(P), take(E), take(16)
        ext, end_col, n_ext = take(1), take(1), take(1)
        hot_r, hot_c = take(4, P), take(4, COLS + 2)
        assert arena.top <= y_top, (arena.top, y_top)
        oacc_at = dn_top - LT * DH * DK
        assert y_top <= oacc_at
        arena.top = oacc_at
        wo0 = take(KT, 512)
        arena.top = oacc_at
        xg, yo = take(D), take(D)
        arena.top = wo1_at
        xT = take(KT, P)
        hh, hid, hidT = take(FF), take(FF), take(FT, P)
        f_out = take(D)

        def f_at(t, k):
            n = TOPK * t + k
            return wbuf[1][:, n * D:(n + 1) * D] if n < 12 else wbuf[0][:, (n - 12) * D:(n - 11) * D]

        dve_step, act_step, pool_step = sem("dve_step"), sem("act_step"), sem("pool_step")
        consts_in, small_in = sem("consts_in"), sem("small_in")
        x_in = [sem(f"x_in{i}") for i in range(3)]
        ada_in = [sem(f"ada_in{i}") for i in range(2)]
        wr_in, wa_in, wz_in = sem("wr_in"), sem("wa_in"), sem("wz_in")
        wc_in = [sem(f"wc_in{i}") for i in range(3)]
        silu_c, ada_used = sem("silu_c"), sem("ada_used")
        x_sd, xn_ready, mix_mod = sem("x_sd"), sem("xn_ready"), sem("mix_mod")
        a_sd, an_ready = sem("a_sd"), sem("an_ready")
        raw_edge, conv_done, silu_done, sq_done, norm_done = (
            sem("raw_edge"), sem("conv_done"), sem("silu_done"), sem("sq_done"), sem("norm_done"))
        eps_set = sem("eps_set")
        gate_a, gate_b, gate_c, gate_d, gate_e, gate_f, gate_g = (sem(f"gate_{x}") for x in "abcdefg")
        rows_out, masks_in, dn_start, s_zero = sem("rows_out"), sem("masks_in"), sem("dn_start"), sem("s_zero")
        two = lambda name: [sem(name + x) for x in ("_fwd", "_bwd")]
        rows_in, gm_ready, et_ready, lt_done, u0_ready, nlm_ready, r_ready, o_used = (
            two(x) for x in ("rows_in", "gm_ready", "et_ready", "lt_done", "u0_ready", "nlm_ready", "r_ready", "o_used"))
        att_in, att_set, dn_sq, dn_ss, dn_sd, dn_rn, dn_out = (
            sem(x) for x in ("att_in", "att_set", "dn_sq", "dn_ss", "dn_sd", "dn_rn", "dn_out"))
        q_rot, qb_ready, rden_step = sem("q_rot"), sem("qb_ready"), sem("rden_step")
        wo_in, xr_in, y_sd, y_ss, x2_ss, x2_sd, xn_out, xn2_ready, rt_in, gate1_set, diag_set = (
            sem(x) for x in ("wo_in", "xr_in", "y_sd", "y_ss", "x2_ss", "x2_sd", "xn_out", "xn2_ready", "rt_in", "gate1_set", "diag_set"))
        x2_ready, r_exp, r_expd, r_exp2, r_exp2d, marks_set, ext_set, base_set, flag_set, hot_set, route_set = (
            sem(x) for x in ("x2_ready", "r_exp", "r_expd", "r_exp2", "r_exp2d", "marks_set", "ext_set", "base_set", "flag_set",
                             "hot_set", "route_set"))
        gate_in, up_in, down_in, tok_in, y_out = (sem(x) for x in ("gate_in", "up_in", "down_in", "tok_in", "y_out"))
        xt_full, xt_done, g_full, u_full, hs_done, h_done, ht_full, ht_done, d_full, y_done, idx_set = (
            sem(x) for x in ("xt_full", "xt_done", "g_full", "u_full", "hs_done", "h_done", "ht_full", "ht_done", "d_full", "y_done", "idx_set"))
        zero_out = sem("zero_out")
        f_in = [sem(f"f_in{i}") for i in range(4)]
        pool_tick, sp_tick, f_y0, f_sum, f_ss, f_sd, f_done, all_in = (
            sem(x) for x in ("pool_tick", "sp_tick", "f_y0", "f_sum", "f_ss", "f_sd", "f_done", "all_in"))
        xn_dram, yb_dram = dram("xn_dram", SEQ, D), dram("yb_dram", COLS * P, D)
        gate_rows = dram("gate_rows", 2 * TT * DH, 2 * P)
        out_done = sem("out_done")

        def chans(n):
            return CHUNKS[:2] if n < DH else CHUNKS

        def chunk_of(i, d):
            order = [8, 9] + list(range(LT)) if d == 0 else [9, 8] + list(range(LT - 1, -1, -1))
            return order[i]

        def gate_cols(d, c):
            at = (d * TT + c) * DH
            return slice(at, at + DH)

        dn_order = []
        for i in range(TT + 1):
            def both(stage, step, level=0):
                if 0 <= step < TT:
                    dn_order.extend((stage, step, d, level) for d in range(2))
            if i == 0:
                both("gQ", 0)
                both("gK", 0)
                for level in range(6):
                    both("nlm", 0, level)
            both("tr", i - 1)
            both("t2", i)
            for level in range(6):
                both("Y", i, level)
                if level in (0, 1, 2):
                    both(("KS", "V", "OS")[level], i - 1)
                both("U", i, level)
                if level == 2:
                    both("gQ", i + 1)
                if level == 3:
                    both("gK", i + 1)
                    for lv in range(6):
                        both("nlm", i + 1, lv)
                if level < 5:
                    both("T", i, level)

        plan = banks.plan
        plan(("mod", 0), 6)
        plan(("mod", 1), 7)
        for t in range(TT):
            for half in range(2):
                plan(("xT", t, half), 2 * (t % 2) + half)
        for n in range(3):
            plan(("kr", n), 4 + n % 2)
        for t in range(TT + 1):
            if t < TT:
                plan(("A", t), 6 + t % 2)
            if t >= 1:
                plan(("AT", t - 1), 4 + (t - 1) % 2)
        for m in range(2, 6):
            plan(("mod", m), m % 4)
        plan(("gc",), 4)
        plan(("gT",), 5)
        for t in range(LT):
            plan(("z", t), 4 + t % 4)
        for n in range(13):
            if n < 12:
                for i in range(len(chans(n))):
                    plan(("qkv", n, i), i + 3 * (n % 2))
            if 1 <= n <= 8:
                for i in range(len(chans(n - 1))):
                    plan(("ss", n - 1, i), 6 + i % 2)

        for stage, i, d, level in dn_order:
            lat = i >= 2
            key, b = (stage, i, d), 4 * d
            if stage == "gK":
                plan(key, b + 3)
            elif stage == "gQ":
                if lat:
                    plan(key, b + 3)
            elif stage == "tr":
                plan(("tv", i, d), b + 3)
                plan(("tk", i, d), b + 2)
            elif stage == "t2":
                plan(key, b + 1)
            elif stage == "Y":
                plan(key + (level,), b)
            elif stage == "T":
                plan(key + (level,), b + 1)
            elif stage == "U":
                plan(key + (level,), b + 2)
            elif stage == "KS":
                plan(key, b + 3)
                if lat:
                    plan(("QS", i, d), b + 2)
            elif stage == "V":
                plan(key, b + 3)
            elif stage == "OS":
                if i < TT - 1:
                    plan(("SU", i, d), b + 3)
                if lat:
                    plan(("I", i, d), b + 1)

        att = [("v", k) for k in range(TT)] + [("ku", 0), ("qu", 0)] + [("mx", 0, j) for j in range(LT)] + [("nm", 0, 0), ("nm", 0, 1)]
        spread = {5 + 2 * j: j for j in range(LT)}
        for h in range(H):
            for n in range(2 * TT):
                att.append(("sc", h, n // TT, n % TT))
                if h + 1 < H:
                    if n == 0:
                        att.append(("ku", h + 1))
                        att.append(("qu", h + 1))
                    if n in spread:
                        att.append(("mx", h + 1, spread[n]))
                    if n == 15:
                        att.append(("nm", h + 1, 0))
                if n == 1 and h > 0:
                    att.append(("pv", h - 1, 1))
                if n == 12:
                    att.append(("pv", h, 0))
                if h == 1 and n % 2 == 1 and n < 2 * LT:
                    att.append(("dt", n // 2))
            if h + 1 < H:
                att.append(("nm", h + 1, 1))
        att.append(("pv", H - 1, 1))
        att_idle = list(banks.freed)
        misc = 0
        for item in att:
            if item[0] == "mx":
                plan(item, 0)
            elif item[0] == "sc":
                plan(item, 3 + (item[2] * TT + item[3]) % 3)
            else:
                for i in range({"ku": 3, "qu": 2}.get(item[0], 1)):
                    plan(item + (i,), 6 + misc % 2, parts=2 if item[0] == "qu" else 1)
                    misc += 1
        for t in range(LT):
            plan(("at", t), 6 + t % 2)
        for m in range(2):
            for half in range(2):
                plan(("gb", m, half), 4 + half)
        for u in range(LT + 3):
            if u < LT:
                for half in range(2):
                    plan(("y", u, half), 2 * (u % 2) + half)
            if 0 <= u - 2 < LT:
                for half in range(2):
                    plan(("x2T", u - 2, half), 4 + half)
            if 0 <= u - 3 < LT:
                plan(("rt", u - 3), 6 + u % 2)
        for key, b in (("rank", 0), ("count", 1), ("base", 2), ("eid", 3), ("idx", 4)):
            plan((key,), b)
        moe_idle = list(banks.freed)

        block = ctx.enter_context(nc.Block())

        @block.sync
        def _(sp):
            sp.dma_start(base, io["k_base"]).then_inc(consts_in, 16)
            for i, name in enumerate(("c", "c_ctx")):
                src = io[name] if name == "c_ctx" else io[name].rearrange("a d -> (a d)")
                sp.dma_start(c_col[:, i, :], src.rearrange("(p j) -> p j", j=KT)).then_inc(small_in, 16)
            sp.dma_start(b_ada, io["b_ada"].rearrange("a (m p j) -> (a p) m j", p=P, j=KT)).then_inc(small_in, 16)
            for i, name in enumerate(("norm_mix_pre", "norm_mix_post", "norm_ffn_pre", "norm_ffn_post")):
                sp.dma_start(gains[:, i, :], io[name].rearrange("a (p j) -> (a p) j", j=KT)).then_inc(small_in, 16)
            sp.dma_start(q_gain, io["q_gain_cols"]).then_inc(small_in, 16)
            sp.dma_start(kv_gain, io["mla_kv_norm"].rearrange("a (p j) -> (a p) j", j=1)).then_inc(small_in, 16)
            sp.dma_start(dn_gain, io["dn_norm"].rearrange("a (p j) -> (a p) j", j=1)).then_inc(small_in, 16)
            sp.dma_start(conv_w, io["conv_cols"].rearrange("p (n w) -> p n w", w=CONV)).then_inc(small_in, 16)
            sp.dma_start(neg_a, io["dn_A_log"].rearrange("a s h -> (a s h)").partition_broadcast(P)).then_inc(small_in, 16)
            sp.dma_start(dt_col, io["dn_dt_bias"].rearrange("a s h -> (a s h)").partition_broadcast(P)).then_inc(small_in, 16)
            sp.dma_start(rope, io["k_rope"]).then_inc(small_in, 16)

            def load_x(t):
                src = io["x"].rearrange("a t d -> (a t) d") if t < LT else io["ctx"].rearrange("a t d -> (a t) d")
                at = t if t < LT else t - LT
                if t >= 3:
                    banks.await_full(sp, ("xT", t - 3, 1))
                sp.dma_start(x_ring[:, t % 3, :], src[at * P:(at + 1) * P, :]).then_inc(x_in[t % 3], 16)

            ada = io["w_ada"].rearrange("a (p j) n -> (a p) j n", j=KT)

            def load_ada(q):
                m, half = q // 2, q % 2
                if q >= 2:
                    sp.wait_ge(ada_used, q - 1)
                sp.dma_start(w_ada[:, q % 2], ada[:, 4 * half:4 * half + 4, m * D:(m + 1) * D]).then_inc(ada_in[q % 2], 16)

            load_x(0)
            load_x(1)
            load_x(2)
            for q in range(4):
                load_ada(q)
            sp.dma_start(w_r, io["w_in_r"].rearrange("(p j) n -> p j n", j=KT)).then_inc(wr_in, 16)
            sp.dma_start(w_a, io["w_in_a"].rearrange("(p j) n -> p j n", j=KT)).then_inc(wa_in, 16)
            for t in range(3, TT):
                load_x(t)
            for q in range(4, 12):
                load_ada(q)
            banks.await_full(sp, ("A", TT - 1))
            sp.dma_start(w_z, io["w_in_z"].rearrange("(p j) n -> p j n", j=KT)).then_inc(wz_in, 16)
            banks.await_read(sp, ("gT",))
            sp.dma_start(gate_rows, gt_rows[0:2 * TT * DH, :]).then_inc(rows_out, 16)
            banks.await_full(sp, ("xT", TT - 1, 1))
            for n in range(12):
                if n >= 3:
                    banks.await_full(sp, ("qkv", n - 3, len(chans(n - 3)) - 1))
                sp.dma_start(w_c[:, n % 3], io["w_in_qkv"].rearrange("(p j) n -> p j n", j=KT)[:, :, n * P:(n + 1) * P])\
                  .then_inc(wc_in[n % 3], 16)
            sp.dma_start(masks, io["k_masks"].rearrange("p (a b) -> p a b", b=P)).then_inc(masks_in, 16)
            banks.await_full(sp, ("qkv", 11, 2))
            sp.wait_ge(rows_out, 16)
            sp.wait_ge(eps_set, 1)
            sp.dma_start(yb_dram[E * P:COLS * P, :].rearrange("(p r) (g c) -> p (r g) c", p=P, c=P),
                         mid(zero, (COLS - E) * KT)).then_inc(zero_out, 16)
            for i in range(TT):
                for d in range(2):
                    if i >= 1:
                        sp.wait_ge(lt_done[d], i)
                    r0 = gate_cols(d, chunk_of(i, d)).start
                    sp.dma_start(rows[:, d].rearrange("p h c -> p (h c)"),
                                 gate_rows[r0:r0 + DH, :].rearrange("h c -> (h c)").partition_broadcast(P)).then_inc(rows_in[d], 16)
            banks.await_full(sp, ("tv", TT - 1, 1))
            banks.await_full(sp, ("tv", TT - 1, 0))
            sp.dma_start(w_q, io["w_q_up4"].rearrange("(k p) n -> p k n", p=P)).then_inc(att_in, 16)
            sp.dma_start(w_k, io["w_k_up"]).then_inc(att_in, 16)
            sp.dma_start(w_v, io["w_v_up"]).then_inc(att_in, 16)
            w_out = io["w_out"].rearrange("a (k p) n -> (a p) k n", p=P)
            banks.await_full(sp, ("dt", LT - 1, 0))
            sp.dma_start(wo0, w_out[:, :, 0:512]).then_inc(wo_in, 16)
            banks.await_full(sp, ("pv", H - 1, 1, 0))
            sp.dma_start(wo1, w_out[:, :, 512:D]).then_inc(wo_in, 16)
            sp.dma_start(w_rt, io["w_router"].rearrange("(p j) n -> p j n", j=KT)).then_inc(rt_in, 16)
            sp.dma_start(b_rt, io["b_router"].partition_broadcast(P)).then_inc(rt_in, 16)
            sp.dma_start(route, io["k_route"]).then_inc(rt_in, 16)
            xs = io["x"].rearrange("a t d -> (a t) d")
            banks.await_read(sp, ("pv", H - 1, 1, 0))
            for t in range(2):
                sp.dma_start(xr[:, t], xs[t * P:(t + 1) * P, :]).then_inc(xr_in, 16)
                sp.wait_ge(xr_in, 16 * (t + 1))

            def load_expert(e, n, first):
                for w, at, k, read, landed in ((io["w_exp_gate"], 0, KT, g_full, gate_in), (io["w_exp_up"], UP_AT, KT, u_full, up_in),
                                               (io["w_exp_down"], DOWN_AT, FT, d_full, down_in)):
                    src = w[0][bass.ds(e, 1)].rearrange("a (p j) f -> (a p) (j f)", j=k)
                    dst = weights(n, at, 0, KT)
                    if not first:
                        sp.wait_ge(read, n - 1)
                        sp.sem_inc(sp_tick, 1)
                        sp.wait_ge(landed, 16 * n)
                        sp.sem_inc(sp_tick, 1)
                    sp.dma_start(dst, src).then_inc(landed, 16)

            load_expert(0, 0, True)
            for t in range(LT):
                sp.wait_ge(xn2_ready, t + 1)
                sp.dma_start(xn_dram[t * P:(t + 1) * P, :], xr[:, t % 2]).then_inc(xn_out, 16)
                if t + 2 < LT:
                    banks.await_full(sp, ("x2T", t, 1))
                    sp.wait_ge(xn_out, 16 * (t + 1))
                    sp.dma_start(xr[:, t % 2], xs[(t + 2) * P:(t + 3) * P, :]).then_inc(xr_in, 16)
                    sp.wait_ge(xr_in, 16 * (t + 3))
            banks.await_full(sp, ("y", LT - 1, 1))
            for landed in (gate_in, up_in, down_in):
                sp.wait_ge(landed, 16)
            load_expert(1, 1, True)
            sp.wait_ge(route_set, 1)
            blocks = sp.value_load(table[0:1, 60:61], min_val=E, max_val=COLS - 1)
            with sp.Fori(2, blocks) as n:
                load_expert(sp.value_load(table[0:1, bass.ds(n, 1)], min_val=0, max_val=E - 1), n, False)
            out = io["out"].rearrange("a t d -> (a t) d")
            for t in range(LT):
                sp.wait_ge(f_done, t + 1)
                sp.dma_start(out[t * P:(t + 1) * P, :], x2[:, t]).then_inc(all_in, 16)
            sp.wait_ge(all_in, 16 * LT)

        @block.tensor
        def _(pe):
            def mods(m):
                b = banks.acquire(pe, ("mod", m))
                for half in range(2):
                    q = 2 * m + half
                    pe.wait_ge(ada_in[q % 2], 16 * (q // 2 + 1))
                    for k in range(4):
                        for j in range(KT):
                            ins = pe.matmul(ps[:, b, 2 * j:2 * j + 2], w_ada[:, q % 2, k, j::KT], sc_col[:, 4 * half + k, :],
                                            start=(half == 0 and k == 0 and j == 0), stop=(half == 1 and k == 3),
                                            skip_group_check=True)
                    if half == 0:
                        ins.then_inc(ada_used, 1)
                banks.filled(ins, ("mod", m))

            def ada_slot_free(m):
                pe.wait_ge(banks.full_sem[banks.bank(("mod", m))], banks.jobs[("mod", m)][1])
                pe.sem_inc(ada_used, 1)

            pe.wait_ge(silu_c, 1)
            pe.wait_ge(consts_in, 16)
            for m in range(2):
                mods(m)
                ada_slot_free(m)
            for t in range(TT):
                pe.wait_ge(xn_ready, t + 1)
                for half in range(2):
                    b = banks.acquire(pe, ("xT", t, half))
                    for j in range(4):
                        ins = pe.transpose(ps[:, b, j * P:(j + 1) * P], x_ring[:, t % 3, 4 * half + j::KT], ident)
                    banks.filled(ins, ("xT", t, half))

            def await_h(t):
                banks.await_read(pe, ("xT", t, 0))
                banks.await_read(pe, ("xT", t, 1))

            pe.wait_ge(wr_in, 16)
            for n, (c0, cn) in enumerate(CHUNKS):
                for t in range(c0 // P, (c0 + cn) // P):
                    await_h(t)
                b = banks.acquire(pe, ("kr", n))
                for k in range(KT):
                    ins = pe.matmul(ps[:, b, 0:cn], w_r[:, k, :], hT[:, k, c0:c0 + cn], start=(k == 0), stop=(k == KT - 1))
                banks.filled(ins, ("kr", n))
            pe.wait_ge(wa_in, 16)
            for t in range(TT + 1):
                if t < TT:
                    b = banks.acquire(pe, ("A", t))
                    for k in range(KT):
                        ins = pe.matmul(ps[:, b, 0:WA], hT[:, k, t * P:(t + 1) * P], w_a[:, k, :], start=(k == 0), stop=(k == KT - 1))
                    banks.filled(ins, ("A", t))
                if t >= 1:
                    s = t - 1
                    pe.wait_ge(an_ready, s + 1)
                    b = banks.acquire(pe, ("AT", s))
                    for j in range(3):
                        ins = pe.transpose(ps[:, b, j * P:(j + 1) * P], an[:, s % 2, j * P:(j + 1) * P], ident)
                    banks.filled(ins, ("AT", s))
            for m in range(2, 6):
                mods(m)
                ada_slot_free(m)
            pe.wait_ge(gate_e, 1)
            b = banks.acquire(pe, ("gc",))
            n = TT * DH
            for d, tri in enumerate((tri_f, tri_b)):
                pe.matmul(ps[:, b, d * n:(d + 1) * n], tri, g_all[:, d * n:(d + 1) * n], start=(d == 0), stop=True, skip_group_check=True)
            banks.filled(pe.matmul(ps[:, b, P:P + 2 * n], ones, g_all, start=False, stop=True, skip_group_check=True), ("gc",))
            pe.wait_ge(gate_f, 1)
            b = banks.acquire(pe, ("gT",))
            pe.transpose(ps[0:2 * n, b, 0:P], gc, ident)
            banks.filled(pe.transpose(ps[0:2 * n, b, P:2 * P], beta, ident), ("gT",))
            pe.wait_ge(wz_in, 16)
            for t in range(LT):
                b = banks.acquire(pe, ("z", t))
                for k in range(KT):
                    ins = pe.matmul(ps[:, b, :], hT[:, k, t * P:(t + 1) * P], w_z[:, k, :], start=(k == 0), stop=(k == KT - 1))
                banks.filled(ins, ("z", t))
            for n in range(13):
                if n < 12:
                    pe.wait_ge(wc_in[n % 3], 16 * (n // 3 + 1))
                    for i, (c0, cn) in enumerate(chans(n)):
                        b = banks.acquire(pe, ("qkv", n, i))
                        for k in range(KT):
                            ins = pe.matmul(ps[:, b, 0:cn], w_c[:, n % 3, k, :], hT[:, k, c0:c0 + cn], start=(k == 0), stop=(k == KT - 1))
                        banks.filled(ins, ("qkv", n, i))
                if 1 <= n <= 8:
                    pe.wait_ge(sq_done, n)
                    for i, (c0, cn) in enumerate(chans(n - 1)):
                        b = banks.acquire(pe, ("ss", n - 1, i))
                        o = c0 if i < 2 else c0 + 2 * HALO
                        ins = pe.matmul(ps[:, b, 0:cn], ones, sq[:, o:o + cn], start=True, stop=True)
                        banks.filled(ins, ("ss", n - 1, i))

            pe.wait_ge(norm_done, 8)
            pe.wait_ge(silu_done, 12)

            def heads(key, lhsT, rhs, transpose=False):
                b = banks.acquire(pe, key)
                for h in range(DH):
                    out = ps[:, b, h * P:(h + 1) * P]
                    ins = pe.transpose(out, lhsT(h), ident) if transpose else pe.matmul(out, lhsT(h), rhs(h), start=True, stop=True)
                banks.filled(ins, key)

            for stage, i, d, level in dn_order:
                c, lat, par = chunk_of(i, d), i >= 2, i % 2
                tok = slice(c * P, (c + 1) * P)
                of = lambda buf: lambda h: buf[:, h * P:(h + 1) * P]
                kc, qc, vc = (lambda h: kT[:, h, tok]), (lambda h: qT[:, h, tok]), (lambda h: vT[:, h, tok])
                if stage == "gK":
                    heads(("gK", i, d), kc, kc)
                elif stage == "gQ" and lat:
                    heads(("gQ", i, d), kc, qc)
                elif stage == "tr":
                    heads(("tv", i, d), vc, None, transpose=True)
                    heads(("tk", i, d), kc, None, transpose=True)
                elif stage == "t2":
                    pe.wait_ge(u0_ready[d], i + 1)
                    heads(("t2", i, d), of(U[:, par, d]), None, transpose=True)
                elif stage == "Y":
                    pe.wait_ge(nlm_ready[d], 6 * i + level + 1)
                    banks.await_read(pe, ("t2", i, d) if level == 0 else ("T", i, d, level - 1))
                    heads(("Y", i, d, level), of(nlm[:, d, level]), of(T[:, d]))
                elif stage == "U":
                    banks.await_read(pe, ("Y", i, d, level))
                    heads(("U", i, d, level), of(Y[:, d]), of(U[:, par, d]))
                elif stage == "T":
                    banks.await_read(pe, ("U", i, d, level))
                    heads(("T", i, d, level), of(U[:, par, d]), None, transpose=True)
                elif stage == "KS":
                    if i == 0:
                        pe.wait_ge(s_zero, 1)
                    else:
                        banks.await_read(pe, ("SU", i - 1, d))
                    heads(("KS", i, d), kc, of(S[:, d]))
                    if lat:
                        heads(("QS", i, d), qc, of(S[:, d]))
                elif stage == "V":
                    banks.await_read(pe, ("U", i, d, 5))
                    pe.wait_ge(r_ready[d], i + 1)
                    heads(("V", i, d), of(U[:, par, d]), of(R[:, d]))
                elif stage == "OS":
                    banks.await_read(pe, ("V", i, d))
                    banks.await_read(pe, ("tk", i, d))
                    if i < TT - 1:
                        heads(("SU", i, d), of(kd[:, d]), of(Vn[:, d]))
                    if lat:
                        banks.await_read(pe, ("gQ", i, d))
                        heads(("I", i, d), of(intra[:, par, d]), of(Vn[:, d]))

            pe.wait_ge(att_in, 48)
            pe.wait_ge(att_set, 1)
            for b in (1, 2):
                pe.wait_ge(banks.free_sem[b], att_idle[b])
            for item in att:
                kind, h = item[0], item[1]
                par = h % 2
                if kind == "v":
                    b = banks.acquire(pe, item + (0,))
                    banks.filled(pe.matmul(ps[:, b, :], kvnT[:, h * P:(h + 1) * P], w_v, start=True, stop=True), item + (0,))
                elif kind == "ku":
                    for i, (c0, cn) in enumerate(CHUNKS):
                        b = banks.acquire(pe, item + (i,))
                        banks.filled(pe.matmul(ps[0:NOPE, b, 0:cn], w_k[:, h * NOPE:(h + 1) * NOPE], kvnT[:, c0:c0 + cn],
                                               start=True, stop=True), item + (i,))
                elif kind == "qu":
                    for i in range(2):
                        b = banks.acquire(pe, item + (i,))
                        for k in range(2):
                            ins = pe.matmul(ps[:, b, :], w_q[:, k, h * P:(h + 1) * P], qnT[:, k, i * 512:(i + 1) * 512],
                                            start=(k == 0), stop=(k == 1))
                        banks.filled(ins, item + (i,))
                elif kind == "mx":
                    j = item[2]
                    pe.wait_ge(qb_ready, 2 * h + 2)
                    banks.acquire(pe, item)
                    for i, (c0, cn) in enumerate(CHUNKS):
                        ins = pe.matmul(ps[:, i, 0:cn], qb[0:96, par * SEQ + j * P:par * SEQ + (j + 1) * P],
                                        kb[0:96, par * TOK + c0:par * TOK + c0 + cn], start=True, stop=True)
                    banks.filled(ins, item)
                elif kind == "nm":
                    i = item[2]
                    banks.await_read(pe, ("mx", h, 4 * i + 3))
                    b = banks.acquire(pe, item + (0,))
                    for j in range(4):
                        ins = pe.matmul(ps[96:97, b, j * P:(j + 1) * P], mx[:, par, 4 * i + j:4 * i + j + 1], ident, start=True, stop=True)
                    banks.filled(ins, item + (0,))
                elif kind == "sc":
                    i, k = item[2], item[3]
                    if k == 0:
                        banks.await_read(pe, ("nm", h, i, 0))
                        pe.wait_ge(q_rot, 2 * h + i + 1)
                        banks.await_read(pe, ("qu", h, i))
                        banks.await_read(pe, ("ku", h, 2))
                    b = banks.acquire(pe, item)
                    banks.filled(pe.matmul(ps[:, b, :], ka[0:97, par, k * P:(k + 1) * P], qa[0:97, par, i * 512:(i + 1) * 512],
                                           start=True, stop=True), item)
                elif kind == "pv":
                    i = item[2]
                    for k in range(TT - 3, TT):
                        banks.await_read(pe, ("sc", h, i, k))
                    if h == 0 and i == 0:
                        banks.await_read(pe, ("v", TT - 1, 0))
                        banks.await_read(pe, ("v", TT - 2, 0))
                    b = banks.acquire(pe, item + (0,))
                    for j in range(4):
                        for k in range(TT):
                            ins = pe.matmul(ps[:, b, j * (VD + 1):(j + 1) * (VD + 1)], PT[:, i, k, j * P:(j + 1) * P], V[:, k * H + h, :],
                                            start=(k == 0), stop=(k == TT - 1))
                    banks.filled(ins, item + (0,))
                elif kind == "dt":
                    pe.wait_ge(dn_out, h + 1)
                    b = banks.acquire(pe, item + (0,))
                    for j in range(DH):
                        ins = pe.transpose(ps[:, b, j * P:(j + 1) * P], oacc[:, h, j * P:(j + 1) * P], ident)
                    banks.filled(ins, item + (0,))
            for i in range(2):
                banks.await_read(pe, ("pv", H - 1, i, 0))
            for t in range(LT):
                b = banks.acquire(pe, ("at", t))
                for j in range(4):
                    ins = pe.transpose(ps[:, b, j * P:(j + 1) * P], atto[:, t, j * P:(j + 1) * P], ident)
                banks.filled(ins, ("at", t))

            for m in range(2):
                pe.wait_ge(diag_set, m + 1)
                for half in range(2):
                    b = banks.acquire(pe, ("gb", m, half))
                    for j in range(4):
                        ins = pe.matmul(ps[:, b, j * P:(j + 1) * P], ones, h2T[:, m, 4 * half + j, :], start=True, stop=True)
                    banks.filled(ins, ("gb", m, half))
            for t in range(LT):
                banks.await_read(pe, ("at", t))
                banks.await_read(pe, ("dt", t, 0))
            pe.wait_ge(wo_in, 32)
            for u in range(LT + 3):
                if u < LT:
                    for half, w in enumerate((wo0, wo1)):
                        b = banks.acquire(pe, ("y", u, half))
                        for k in range(KT):
                            ins = pe.matmul(ps[:, b, :], mixT[:, k, u * P:(u + 1) * P], w[:, k, :], start=(k == 0), stop=(k == KT - 1))
                        banks.filled(ins, ("y", u, half))
                if 0 <= u - 2 < LT:
                    t = u - 2
                    pe.wait_ge(xn2_ready, t + 1)
                    for half in range(2):
                        b = banks.acquire(pe, ("x2T", t, half))
                        for j in range(4):
                            ins = pe.transpose(ps[:, b, j * P:(j + 1) * P], xr[:, t % 2, 4 * half + j::KT], ident)
                        banks.filled(ins, ("x2T", t, half))
                if 0 <= u - 3 < LT:
                    t = u - 3
                    pe.wait_ge(rt_in, 48)
                    for half in range(2):
                        banks.await_read(pe, ("x2T", t, half))
                    b = banks.acquire(pe, ("rt", t))
                    for k in range(KT):
                        ins = pe.matmul(ps[:, b, 0:RW], h2T[:, t % 2, k, :], w_rt[:, k, :], start=(k == 0), stop=(k == KT - 1))
                    banks.filled(ins, ("rt", t))

            strict, iota = route[:, 0:P], route[:, P:2 * P]
            pe.wait_ge(marks_set, 1)
            b = banks.acquire(pe, ("rank",))
            pe.matmul(ps[:, b, 0:LT * E], strict, mark, start=True, stop=False)
            banks.filled(pe.matmul(ps[:, b, 0:LT * E], ones, before, start=False, stop=True), ("rank",))
            b = banks.acquire(pe, ("count",))
            banks.filled(pe.matmul(ps[0:E, b, 0:8], marks_all, ones[:, 0:8], start=True, stop=True), ("count",))
            pe.wait_ge(ext_set, 1)
            b = banks.acquire(pe, ("base",))
            pe.matmul(ps[:, b, 0:E], ext_b[0:E, :], strict[0:E, 0:E], start=True, stop=True, skip_group_check=True)
            pe.matmul(ps[:, b, E:E + 1], ext_b[0:E, :], ones[0:E, 0:1], start=False, stop=True, skip_group_check=True)
            banks.filled(pe.matmul(ps[0:E, b, 64:65], tri_f[0:E, 0:E], ext[0:E, :], start=False, stop=True, skip_group_check=True), ("base",))
            pe.wait_ge(flag_set, 1)
            b = banks.acquire(pe, ("eid",))
            banks.filled(pe.matmul(ps[0:1, b, 0:16], ones[0:E, 0:1], flags[0:E, :], start=True, stop=True), ("eid",))
            b = banks.acquire(pe, ("idx",))
            for n in range(TOPK * LT):
                pe.wait_ge(hot_set, n + 1)
                ins = pe.matmul(ps[:, b, 0:COLS + 2], hot_r[:, n % 4], hot_c[:, n % 4], start=(n == 0), stop=(n == TOPK * LT - 1))
                if n < TOPK * LT - 1:
                    ins.then_inc(idx_set, 1)
            banks.filled(ins, ("idx",))

            pe.wait_ge(route_set, 1)
            for b in range(8):
                if moe_idle[b]:
                    pe.wait_ge(banks.free_sem[b], moe_idle[b])

            def turn_tokens():
                for j in range(KT):
                    ins = pe.transpose(ps[:, j // 4, (j % 4) * P:(j % 4 + 1) * P], xg[:, j::KT], ident)
                ins.then_inc(xt_full, 1)

            def hidden(n, first):
                pe.wait_ge(xt_done, 2 * n + 2)
                if not first:
                    pe.wait_ge(hs_done, n)
                pe.wait_ge(gate_in, 16 * n + 16)
                for k in range(KT):
                    ins = pe.matmul(ps[:, 2, :], xT[:, k, :], weights(n, 0, k), start=(k == 0), stop=(k == KT - 1))
                ins.then_inc(g_full, 1)
                if not first:
                    pe.wait_ge(h_done, n)
                pe.wait_ge(up_in, 16 * n + 16)
                for k in range(KT):
                    ins = pe.matmul(ps[:, 3, :], xT[:, k, :], weights(n, UP_AT, k), start=(k == 0), stop=(k == KT - 1))
                ins.then_inc(u_full, 1)
                pe.wait_ge(tok_in, 16 * n + 32)
                turn_tokens()

            def down(n):
                pe.wait_ge(ht_done, n)
                pe.wait_ge(y_done, 2 * n + 1)
                pe.wait_ge(down_in, 16 * n)
                for half in range(2):
                    for j in range(FT):
                        ins = pe.matmul(ps[:, 5 + half, :], hidT[:, j, :], weights(n + 1, DOWN_AT, 2 * j + half), start=(j == 0), stop=(j == FT - 1))
                ins.then_inc(d_full, 1)

            def turn_hidden(n):
                pe.wait_ge(h_done, n + 1)
                for j in range(FT):
                    ins = pe.transpose(ps[:, 4, j * P:(j + 1) * P], hid[:, j::FT], ident)
                ins.then_inc(ht_full, 1)

            pe.wait_ge(tok_in, 16)
            turn_tokens()
            hidden(0, True)
            turn_hidden(0)
            blocks = pe.value_load(table[0:1, 60:61], min_val=E, max_val=COLS - 1)
            with pe.Fori(1, blocks) as n:
                hidden(n, False)
                down(n)
                turn_hidden(n)
            down(blocks)

        @block.scalar
        def _(act):
            step = Chain(act, act_step)
            act.wait_ge(small_in, 16 * 14)
            act.wait_ge(eps_set, 1)
            act.activation(sc_col.rearrange("p k w -> p w k"), c_col, ACT.Silu).then_inc(silu_c, 1)
            step(act.activation(neg_a, neg_a, ACT.Exp))

            def x_stats(t):
                act.wait_ge(x_in[t % 3], 16 * (t // 3 + 1))
                step(act.activation(junk, x_ring[:, t % 3, :], ACT.Square, scale=D ** -0.5, accum_out=ssx[:, t:t + 1]))
                act.activation(sdx[:, t:t + 1], ssx[:, t:t + 1], ACT.Sqrt, bias=eps_col).then_inc(x_sd, 1)

            x_stats(0)
            act.wait_ge(mix_mod, 1)
            for t in range(TT):
                if t + 1 < TT:
                    x_stats(t + 1)
                w = 0 if t < LT else 1
                b = banks.await_full(act, ("xT", t, 0))
                for j in range(4):
                    ins = act.activation(hT[:, j, t * P:(t + 1) * P], ps[:, b, j * P:(j + 1) * P], ACT.Identity,
                                         bias=modc[:, 0, w, j:j + 1], scale=mix_scale[:, w, j:j + 1])
                banks.release(ins, ("xT", t, 0))
            for t in range(TT):
                b = banks.await_full(act, ("A", t))
                step(act.activation(junk[:, 0:QR], ps[:, b, 0:QR], ACT.Square, scale=QR ** -0.5, accum_out=ss_a[:, t, 0:1]))
                step(act.activation(junk[:, 0:KVR], ps[:, b, QR:QR + KVR], ACT.Square, scale=KVR ** -0.5, accum_out=ss_a[:, t, 1:2]))
                act.activation(sd_a[:, t, :], ss_a[:, t, :], ACT.Sqrt, bias=eps_col).then_inc(a_sd, 1)
            act.wait_ge(gate_a, 1)
            act.activation(ba[:, :, 0:8], ba[:, :, 0:8], ACT.Exp, scale=-1.0).then_inc(gate_b, 1)
            act.wait_ge(gate_c, 1)
            step(act.activation(gtmp, gtmp, ACT.Exp))
            act.activation(gtmp, gtmp, ACT.Ln, bias=ones[:, 0:1]).then_inc(gate_d, 1)
            act.wait_ge(gate_f, 1)
            act.activation(egc, gc, ACT.Exp)
            act.activation(egl, egl, ACT.Exp)
            act.activation(kdc, kdc, ACT.Exp).then_inc(gate_g, 1)
            for t in range(LT):
                b = banks.await_full(act, ("z", t))
                banks.release(act.activation(z[:, t, :], ps[:, b, :], ACT.Silu), ("z", t))
            act.wait_ge(raw_edge, 1)
            for n in range(13):
                if n < 12:
                    if n >= 2:
                        act.wait_ge(conv_done, n - 1)
                    for i, (c0, cn) in enumerate(chans(n)):
                        b = banks.await_full(act, ("qkv", n, i))
                        o = HALO + c0 + (2 * HALO if i == 2 else 0)
                        banks.release(act.activation(raw[:, n % 2, o:o + cn], ps[:, b, 0:cn], ACT.Copy), ("qkv", n, i))
                if 1 <= n <= 8:
                    if n >= 2:
                        act.wait_ge(norm_done, n - 1)
                    for i, (c0, cn) in enumerate(chans(n - 1)):
                        b = banks.await_full(act, ("ss", n - 1, i))
                        o = c0 if i < 2 else c0 + 2 * HALO
                        banks.release(act.activation(rn[:, o:o + cn], ps[:, b, 0:cn], ACT.Sqrt, bias=eps_col), ("ss", n - 1, i))
                if n < 12:
                    act.wait_ge(conv_done, n + 1)
                    if n < 8:
                        width = SEQ if n < DH else CW
                        act.activation(acc[:, n % 2, 0:width], acc[:, n % 2, 0:width], ACT.Silu).then_inc(silu_done, 1)
                    else:
                        act.activation(vT[:, n - 8, 0:SEQ], acc[:, n % 2, 0:SEQ], ACT.Silu)
                        act.activation(vT[:, n - 8, SEQ:TOK], acc[:, n % 2, SEQ + 2 * HALO:CW], ACT.Silu).then_inc(silu_done, 1)

            for stage, i, d, level in dn_order:
                if stage == "gQ":
                    act.wait_ge(gm_ready[d], i + 1)
                    at = gate_cols(d, chunk_of(i, d)).start
                    for h in range(DH):
                        part = et[:, d, h * P:(h + 1) * P]
                        ins = act.activation(part, part, ACT.Exp, bias=ngc[:, at + h:at + h + 1])
                    ins.then_inc(et_ready[d], 1)
                elif stage == "tr":
                    b = banks.await_full(act, ("tk", i, d))
                    at = gate_cols(d, chunk_of(i, d)).start
                    for h in range(DH):
                        ins = act.activation(kd[:, d, h * P:(h + 1) * P], ps[:, b, h * P:(h + 1) * P], ACT.Copy, scale=kdc[:, at + h:at + h + 1])
                    banks.release(ins, ("tk", i, d))
                elif stage in ("t2", "Y", "T", "V"):
                    key = (stage, i, d) + ((level,) if stage in "YT" else ())
                    b = banks.await_full(act, key)
                    dst = {"t2": T, "T": T, "Y": Y, "V": Vn}[stage]
                    banks.release(act.activation(dst[:, d], ps[:, b, :], ACT.Copy), key)

            act.wait_ge(att_set, 1)
            for item in att:
                kind, h = item[0], item[1]
                par = h % 2
                if kind == "v":
                    b = banks.await_full(act, item + (0,))
                    banks.release(act.activation(V[:, h * H:(h + 1) * H, 0:VD], ps[:, b, :].rearrange("p (a b) -> p a b", b=VD), ACT.Copy), item + (0,))
                    if h == 0:
                        act.wait_ge(dn_ss, LT)
                        act.activation(rd, ssd, ACT.Sqrt, scale=1.0 / DK, bias=eps_col).then_inc(dn_sd, 1)
                elif kind == "ku":
                    for i, (c0, cn) in enumerate(CHUNKS):
                        b = banks.await_full(act, item + (i,))
                        banks.release(act.activation(ka[0:NOPE, par, c0:c0 + cn], ps[0:NOPE, b, 0:cn], ACT.Copy), item + (i,))
                elif kind == "qu":
                    for i in range(2):
                        b = banks.await_full(act, item + (i,))
                        banks.release(act.activation(qa[0:NOPE, par, i * 512:(i + 1) * 512], ps[0:NOPE, b, :], ACT.Copy), item + (i,))
                elif kind == "nm":
                    i = item[2]
                    b = banks.await_full(act, item + (0,))
                    banks.release(act.activation(qa[96:97, par, i * 512:(i + 1) * 512], ps[96:97, b, :], ACT.Copy, scale=-1.0), item + (0,))
                elif kind == "sc":
                    b = banks.await_full(act, item)
                    banks.release(act.activation(PT[:, item[2], item[3], :], ps[:, b, :], ACT.Exp, scale=SCALE), item)
                elif kind == "dt":
                    b = banks.await_full(act, item + (0,))
                    banks.release(act.activation(mixT[:, 4:8, h * P:(h + 1) * P], ps[:, b, :].rearrange("p (a b) -> p a b", b=P), ACT.Copy,
                                                 scale=dn_gain[:, 0:1]), item + (0,))
            for t in range(LT):
                b = banks.await_full(act, ("at", t))
                banks.release(act.activation(mixT[:, 0:4, t * P:(t + 1) * P], ps[:, b, :].rearrange("p (a b) -> p a b", b=P), ACT.Copy), ("at", t))
            for m, dst in enumerate((gate1, gate2)):
                for half in range(2):
                    b = banks.await_full(act, ("gb", m, half))
                    out = dst.rearrange("p (q j) -> p j q", j=KT)[:, 4 * half:4 * half + 4, :]
                    banks.release(act.activation(out, ps[:, b, :].rearrange("p (j q) -> p j q", q=P), ACT.Copy), ("gb", m, half))
            for u in range(LT + 3):
                if u < LT:
                    for half in range(2):
                        b = banks.await_full(act, ("y", u, half))
                        ins = act.activation(junk3[:, 0:512], ps[:, b, :], ACT.Square, scale=D ** -0.5, accum_out=ssy[:, u, half:half + 1])
                        if half == 0:
                            step(ins)
                    ins.then_inc(y_ss, 1)
                    act.wait_ge(y_sd, u + 1)
                    act.activation(ry[:, u:u + 1], ry[:, u:u + 1], ACT.Sqrt, bias=eps_col).then_inc(x2_sd, 1)
                    act.wait_ge(x2_ready, u + 1)
                    step(act.activation(junk3, x2[:, u], ACT.Square, scale=D ** -0.5, accum_out=ssz[:, u:u + 1]))
                    act.activation(rz[:, u:u + 1], ssz[:, u:u + 1], ACT.Sqrt, bias=eps_col).then_inc(x2_ss, 1)
                if 0 <= u - 2 < LT:
                    t = u - 2
                    b = banks.await_full(act, ("x2T", t, 0))
                    for j in range(4):
                        ins = act.activation(h2T[:, t % 2, j, :], ps[:, b, j * P:(j + 1) * P], ACT.Identity,
                                             bias=modc[:, 3, 0, j:j + 1], scale=ffn_scale[:, j:j + 1])
                    banks.release(ins, ("x2T", t, 0))
            act.wait_ge(r_exp, 1)
            act.activation(gx, gx, ACT.Exp).then_inc(r_expd, 1)
            act.wait_ge(r_exp2, 1)
            act.activation(small[1][:, 0:LT], small[0][:, 0:LT], ACT.Exp).then_inc(r_exp2d, 1)

            def modulate_half():
                for j in range(4):
                    ins = act.activation(xT[:, j, :], ps[:, 0, j * P:(j + 1) * P], ACT.Identity,
                                         bias=modc[:, 3, 0, j:j + 1], scale=ffn_scale[:, j:j + 1])
                ins.then_inc(xt_done, 1)

            def gate_and_next(n, first):
                act.wait_ge(g_full, n + 1)
                if not first:
                    act.wait_ge(h_done, n)
                act.activation(hh, ps[:, 2, :], ACT.Silu).then_inc(hs_done, 1)
                act.wait_ge(xt_full, n + 2)
                modulate_half()

            def copy_hidden(n):
                act.wait_ge(ht_full, n + 1)
                act.activation(hidT, ps[:, 4, :].rearrange("p (a b) -> p a b", b=P), ACT.Copy).then_inc(ht_done, 1)

            def copy_out(n):
                act.wait_ge(d_full, n)
                act.wait_ge(y_out, 16 * n)
                act.activation(yo[:, 0:512], ps[:, 5, :], ACT.Copy).then_inc(y_done, 1)

            def store_out(n):
                act.wait_ge(y_done, 2 * n + 3)
                act.dma_start(yb_dram[bass.ds((n - 1) * P, P), :], yo).then_inc(y_out, 16)

            def square_sum(t):
                act.wait_ge(f_sum, t + 1)
                step(act.activation(xg, f_at(t, 0), ACT.Square, scale=D ** -0.5, accum_out=ssf[:, t:t + 1]))
                act.activation(rf[:, t:t + 1], ssf[:, t:t + 1], ACT.Sqrt, bias=eps_col).then_inc(f_sd, 1)

            act.wait_ge(route_set, 1)
            act.wait_ge(zero_out, 16)
            act.sem_inc(y_done, 3)
            act.sem_inc(y_out, 16)
            act.wait_ge(xt_full, 1)
            modulate_half()
            gate_and_next(0, True)
            copy_hidden(0)
            blocks = act.value_load(table[0:1, 60:61], min_val=E, max_val=COLS - 1)
            with act.Fori(1, blocks) as n:
                gate_and_next(n, False)
                copy_out(n)
                copy_hidden(n)
                store_out(n)
            copy_out(blocks)
            store_out(blocks)
            for t in range(LT):
                act.wait_ge(f_in[t % 4], 16 * TOPK * (t // 4 + 1))
                act.activation(f_at(t, 0), f_at(t, 0), ACT.Copy, scale=cw[:, 0, t:t + 1]).then_inc(f_y0, 1)
                if t >= 1:
                    square_sum(t - 1)
            square_sum(LT - 1)

        @block.gpsimd
        def _(pool):
            step = Chain(pool, pool_step)
            pool.memset(zero, 0.0)
            pool.memset(eps_col, EPS).then_inc(eps_set, 1)
            banks.await_full(pool, ("mod", 5))
            step(pool.memset(raw.rearrange("p a b -> p (a b)"), 0.0))
            pool.sem_inc(raw_edge, 1)
            for n in range(8):
                width = SEQ if n < DH else CW
                pool.wait_ge(silu_done, n + 1)
                if n >= 1:
                    banks.await_full(pool, ("ss", n - 1, len(chans(n - 1)) - 1))
                pool.tensor_tensor(sq[:, 0:width], acc[:, n % 2, 0:width], acc[:, n % 2, 0:width], ALU.mult).then_inc(sq_done, 1)

            pool.wait_ge(silu_done, 12)
            pool.wait_ge(norm_done, 8)
            pool.wait_ge(conv_done, 12)
            banks.await_full(pool, ("qkv", 11, 2))
            pool.wait_ge(masks_in, 16)
            pool.memset(S.rearrange("p a b -> p (a b)"), 0.0).then_inc(s_zero, 1)
            for stage, i, d, level in dn_order:
                c, par = chunk_of(i, d), i % 2
                if stage == "gQ":
                    pool.wait_ge(rows_in[d], 16 * (i + 1))
                    if i >= 1:
                        pool.wait_ge(nlm_ready[d], 6 * i)
                    e3 = et[:, d].rearrange("p (h i) -> p h i", h=DH)
                    pool.tensor_tensor(e3, rows[:, d, :, 0:P], mid(masks[:, 14 + d, :], DH), ALU.add).then_inc(gm_ready[d], 1)
                elif stage == "gK":
                    e3 = et[:, d].rearrange("p (h i) -> p h i", h=DH)
                    banks.await_read(pool, ("gK", i, d))
                    pool.tensor_tensor(e3, e3, rows[:, d, :, P:2 * P], ALU.mult).then_inc(lt_done[d], 1)
                    pool.wait_ge(lt_done[d], i + 1)
                    if i >= 2:
                        banks.await_full(pool, ("V", i - 2, d))
                    u3 = U[:, par, d].rearrange("p (h i) -> p h i", h=DH)
                    step(pool.tensor_tensor(u3, e3, mid(masks[:, 7 * d, :], DH), ALU.mult))
                    pool.tensor_tensor(u3, u3, mid(ident, DH), ALU.add).then_inc(u0_ready[d], 1)
                elif stage == "nlm":
                    if i >= 1:
                        banks.await_full(pool, ("Y", i - 1, d, level))
                    pool.tensor_tensor(nlm[:, d, level].rearrange("p (h i) -> p h i", h=DH), et[:, d].rearrange("p (h i) -> p h i", h=DH),
                                       mid(masks[:, 7 * d + 1 + level, :], DH), ALU.mult).then_inc(nlm_ready[d], 1)
                elif stage == "OS" and i >= 2:
                    banks.await_read(pool, ("I", i, d))
                    first = (c < LT // 2) == (d == 0)
                    if first:
                        pool.tensor_copy(oacc[:, c], o1[:, d]).then_inc(o_used[d], 1)
                    else:
                        pool.wait_ge(o_used[1 - d], (11 - i) - 1)
                        pool.tensor_tensor(oacc[:, c], oacc[:, c], o1[:, d], ALU.add).then_inc(o_used[d], 1)

            for d in range(2):
                banks.await_read(pool, ("I", TT - 1, d))
                banks.await_read(pool, ("V", TT - 1, d))
                pool.wait_ge(o_used[d], LT)
            step(pool.memset(V[:, :, VD:VD + 1], 1.0))
            step(pool.memset(ka[96:97].rearrange("p a b -> p (a b)"), 1.0))
            for par in range(2):
                step(pool.tensor_copy(ka[64:96, par, :], krT[64:96, :]))
            pool.sem_inc(att_set, 1)
            for t in range(LT):
                if t >= 2:
                    pool.wait_ge(dn_ss, t - 1)
                pool.tensor_tensor(S[:, t % 2], oacc[:, t], oacc[:, t], ALU.mult).then_inc(dn_sq, 1)

            def cast(h):
                par = h % 2
                for i in range(2):
                    banks.await_read(pool, ("qu", h, i))
                pool.wait_ge(q_rot, 2 * h + 2)
                if h >= 2:
                    banks.await_full(pool, ("mx", h - 2, LT - 1))
                pool.tensor_copy(qb[0:96, par * SEQ:(par + 1) * SEQ], qa[0:96, par, :]).then_inc(qb_ready, 1)
                banks.await_read(pool, ("ku", h, 2))
                banks.await_read(pool, ("ku", h, 1))
                pool.tensor_copy(kb[0:96, par * TOK:(par + 1) * TOK], ka[0:96, par, :]).then_inc(qb_ready, 1)

            cast(0)
            for t in range(LT):
                pool.wait_ge(dn_rn, t + 1)
                pool.tensor_tensor(oacc[:, t], oacc[:, t], z[:, t], ALU.mult).then_inc(dn_out, 1)
            for h in range(1, H):
                cast(h)

            def gather(col, count):
                pool.tensor_copy(idx_cur, idx[:, col]).then_inc(idx_set, 1)
                pool.wait_ge(idx_set, count)
                pool.sem_inc(pool_tick, 1)
                pool.indirect_dma_start(out=xg, out_offset=None, in_=xn_dram,
                                        in_offset=bass.IndirectOffsetOnAxis(idx_cur, axis=0)).then_inc(tok_in, 16)

            made = TOPK * LT - 1
            pool.wait_ge(route_set, 1)
            pool.wait_ge(xn_out, 16 * LT)
            gather(slice(0, 1), made + 1)
            blocks = pool.value_load(table[0:1, 60:61], min_val=E, max_val=COLS - 1)
            with pool.Fori(1, blocks + 1) as n:
                pool.wait_ge(xt_full, n)
                pool.sem_inc(pool_tick, 1)
                gather(bass.ds(n, 1), n + (made + 1))
            pool.wait_ge(y_out, 16 * blocks + 16)
            pool.sem_inc(pool_tick, 1)
            for t in range(LT):
                if t >= 4:
                    pool.wait_ge(f_in[t % 4], 16 * TOPK * (t // 4))
                for k in range(TOPK):
                    pool.indirect_dma_start(out=f_at(t, k), out_offset=None, in_=yb_dram,
                                            in_offset=bass.IndirectOffsetOnAxis(dest[:, k * LT + t:k * LT + t + 1], axis=0)).then_inc(f_in[t % 4], 16)

        @block.vector
        def _(dve):
            step = Chain(dve, dve_step)

            def x_norm(t):
                dve.wait_ge(x_sd, t + 1)
                step(dve.reciprocal(rx[:, t:t + 1], sdx[:, t:t + 1]))
                dve.tensor_scalar(x_ring[:, t % 3, :], x_ring[:, t % 3, :], rx[:, t:t + 1], None, ALU.mult).then_inc(xn_ready, 1)

            def mod_out(m):
                b = banks.await_full(dve, ("mod", m))
                banks.release(dve.tensor_tensor(modc[:, m], ps[:, b, 0:2 * KT].rearrange("p (j w) -> p w j", w=2),
                                                mid(b_ada[:, m, :], 2), ALU.add), ("mod", m))

            x_norm(0)
            for m in range(2):
                mod_out(m)
            banks.await_read(dve, ("mod", 1))
            dve.scalar_tensor_tensor(mix_scale, modc[:, 1], 1.0, mid(gains[:, 0, :], 2), ALU.add, ALU.mult).then_inc(mix_mod, 1)
            dve.wait_ge(mix_mod, 1)
            for t in range(TT):
                if t + 1 < TT:
                    x_norm(t + 1)
                w = 0 if t < LT else 1
                b = banks.await_full(dve, ("xT", t, 1))
                for j in range(4):
                    ins = dve.tensor_scalar(hT[:, 4 + j, t * P:(t + 1) * P], ps[:, b, j * P:(j + 1) * P],
                                            mix_scale[:, w, 4 + j:5 + j], modc[:, 0, w, 4 + j:5 + j], ALU.mult, ALU.add)
                banks.release(ins, ("xT", t, 1))
            for n, (c0, cn) in enumerate(CHUNKS):
                b = banks.await_full(dve, ("kr", n))
                if n < 2:
                    step(dve.tensor_tensor(krT[64:96, c0:c0 + cn], ps[64:96, b, 0:cn], rope[64:96, c0:c0 + cn], ALU.mult))
                    banks.release(dve.tensor_tensor(rope_tmp[64:96, 0:cn], ps[96:128, b, 0:cn], rope[96:128, c0:c0 + cn], ALU.mult), ("kr", n))
                    banks.await_read(dve, ("kr", n))
                    step(dve.tensor_tensor(krT[64:96, c0:c0 + cn], krT[64:96, c0:c0 + cn], rope_tmp[64:96, 0:cn], ALU.add))
                else:
                    banks.release(dve.tensor_copy(krT[64:96, c0:c0 + cn], ps[64:96, b, 0:cn]), ("kr", n))
            for t in range(TT + 1):
                if t < TT:
                    b = banks.await_full(dve, ("A", t))
                    dve.wait_ge(a_sd, t + 1)
                    step(dve.reciprocal(r_a[:, t, :], sd_a[:, t, :]))
                    if t >= 2:
                        banks.await_full(dve, ("AT", t - 2))
                    dve.tensor_scalar(an[:, t % 2, 0:QR], ps[:, b, 0:QR], r_a[:, t, 0:1], None, ALU.mult)
                    dve.tensor_scalar(an[:, t % 2, QR:], ps[:, b, QR:QR + KVR], r_a[:, t, 1:2], None, ALU.mult).then_inc(an_ready, 1)
                    banks.release(dve.tensor_copy(ba[:, t, :], ps[:, b, QR + KVR:WA]), ("A", t))
                if t >= 1:
                    s = t - 1
                    b = banks.await_full(dve, ("AT", s))
                    if s < LT:
                        for j in range(2):
                            dve.tensor_scalar(qnT[:, j, s * P:(s + 1) * P], ps[:, b, j * P:(j + 1) * P], q_gain[:, j:j + 1], None, ALU.mult)
                    banks.release(dve.tensor_scalar(kvnT[:, s * P:(s + 1) * P], ps[:, b, QR:QR + KVR], kv_gain[:, 0:1], None, ALU.mult), ("AT", s))
            for m in range(2, 6):
                mod_out(m)
            banks.await_read(dve, ("A", TT - 1))
            by_dir = lambda ap: ap.rearrange("p t (s h) -> p s t h", s=2)
            flat4 = lambda ap: ap.rearrange("p (s t h) -> p s t h", s=2, h=DH)
            over_t = lambda ap: ap.rearrange("p (s h) -> p s h", s=2).unsqueeze(2).to_broadcast([P, 2, TT, DH])
            dve.tensor_tensor(flat4(g_all), by_dir(ba[:, :, 8:16]), over_t(dt_col), ALU.add).then_inc(gate_a, 1)
            dve.wait_ge(gate_a, 1)
            dve.scalar_tensor_tensor(gtmp, g_all, -1.0, g_all, ALU.mult, ALU.min).then_inc(gate_c, 1)
            dve.wait_ge(gate_c, 1)
            step(dve.tensor_scalar(g_all, g_all, 0.0, None, ALU.max))
            dve.wait_ge(gate_b, 1)
            step(dve.tensor_scalar(ba[:, :, 0:8], ba[:, :, 0:8], 1.0, None, ALU.add))
            step(dve.reciprocal(ba[:, :, 0:8], ba[:, :, 0:8]))
            step(dve.tensor_copy(flat4(beta), by_dir(ba[:, :, 0:8])))
            dve.wait_ge(gate_d, 1)
            step(dve.tensor_tensor(g_all, g_all, gtmp, ALU.add))
            step(dve.tensor_tensor(flat4(gtmp), flat4(g_all), over_t(neg_a), ALU.mult))
            dve.tensor_scalar(g_all, gtmp, -1.0, None, ALU.mult).then_inc(gate_e, 1)
            b = banks.await_full(dve, ("gc",))
            n80 = 2 * TT * DH
            step(dve.tensor_copy(gc, ps[:, b, 0:n80]))
            dve.tensor_scalar(ngc, ps[:, b, 0:n80], -1.0, None, ALU.mult)
            step(dve.tensor_copy(egl, ps[:, b, P:P + n80]))
            banks.release(dve.tensor_tensor(kdc, ps[:, b, P:P + n80], gc, ALU.subtract), ("gc",))
            banks.await_read(dve, ("gc",))
            dve.sem_inc(gate_f, 1)
            b = banks.await_full(dve, ("gT",))
            banks.release(dve.tensor_copy(gt_rows[0:n80, :], ps[0:n80, b, 0:2 * P]), ("gT",))
            dve.wait_ge(gate_g, 1)
            step(dve.tensor_tensor(bege, beta, egc, ALU.mult))
            dve.wait_ge(raw_edge, 1)
            for n in range(13):
                if n < 12:
                    width = SEQ if n < DH else CW
                    for i in range(len(chans(n))):
                        banks.await_read(dve, ("qkv", n, i))
                    if n >= 10:
                        dve.wait_ge(silu_done, n - 1)
                    step(dve.tensor_scalar(acc[:, n % 2, 0:width], raw[:, n % 2, 0:width], conv_w[:, n, 0:1], None, ALU.mult))
                    for o in range(1, CONV):
                        ins = dve.scalar_tensor_tensor(acc[:, n % 2, 0:width], raw[:, n % 2, o:o + width], conv_w[:, n, o:o + 1],
                                                       acc[:, n % 2, 0:width], ALU.mult, ALU.add)
                        if o < CONV - 1:
                            step(ins)
                    ins.then_inc(conv_done, 1)
                if 1 <= n <= 8:
                    s = n - 1
                    width = SEQ if s < DH else CW
                    for i in range(len(chans(s))):
                        banks.await_read(dve, ("ss", s, i))
                    if s >= DH:
                        if s == DH:
                            step(dve.memset(rn[:, SEQ:SEQ + 2 * HALO], 1.0))
                    step(dve.reciprocal(rn[:, 0:width], rn[:, 0:width]))
                    if s < DH:
                        dve.scalar_tensor_tensor(qT[:, s, :], acc[:, s % 2, 0:SEQ], DK ** -0.5, rn[:, 0:SEQ], ALU.mult, ALU.mult).then_inc(norm_done, 1)
                    else:
                        dve.tensor_tensor(kT[:, s - DH, 0:SEQ], acc[:, s % 2, 0:SEQ], rn[:, 0:SEQ], ALU.mult)
                        dve.tensor_tensor(kT[:, s - DH, SEQ:TOK], acc[:, s % 2, SEQ + 2 * HALO:CW], rn[:, SEQ + 2 * HALO:CW], ALU.mult).then_inc(norm_done, 1)
                    dve.wait_ge(norm_done, n)

            dve.wait_ge(silu_done, 12)
            h3 = lambda ap: ap.rearrange("p (h i) -> p h i", h=DH)
            for stage, i, d, level in dn_order:
                c, lat, par = chunk_of(i, d), i >= 2, i % 2
                cols = gate_cols(d, c)
                col4 = lambda g: bc(g[:, cols], [P, DH, P])
                if stage == "gQ" and lat:
                    dve.wait_ge(et_ready[d], i + 1)
                    b = banks.await_full(dve, ("gQ", i, d))
                    banks.release(dve.tensor_tensor(intra[:, par, d], ps[:, b, :], et[:, d], ALU.mult), ("gQ", i, d))
                elif stage == "gK":
                    dve.wait_ge(et_ready[d], i + 1)
                    if lat:
                        banks.await_read(dve, ("gQ", i, d))
                    b = banks.await_full(dve, ("gK", i, d))
                    banks.release(dve.tensor_tensor(et[:, d], ps[:, b, :], et[:, d], ALU.mult), ("gK", i, d))
                elif stage == "tr":
                    b = banks.await_full(dve, ("tv", i, d))
                    banks.release(dve.tensor_tensor(h3(R[:, d]), h3(ps[:, b, :]), col4(beta), ALU.mult), ("tv", i, d))
                elif stage == "U":
                    key = ("U", i, d, level)
                    b = banks.await_full(dve, key)
                    banks.release(dve.tensor_tensor(U[:, par, d], U[:, par, d], ps[:, b, :], ALU.add), key)
                elif stage == "KS":
                    b = banks.await_full(dve, ("KS", i, d))
                    if d == 1 or i >= 1:
                        dve.wait_ge(r_ready[1 - d], i + d)
                    banks.release(dve.tensor_tensor(h3(ks), h3(ps[:, b, :]), col4(bege), ALU.mult), ("KS", i, d))
                    banks.await_read(dve, ("KS", i, d))
                    banks.await_read(dve, ("tv", i, d))
                    dve.tensor_tensor(R[:, d], R[:, d], ks, ALU.subtract).then_inc(r_ready[d], 1)
                    if lat:
                        if i >= 3:
                            dve.wait_ge(o_used[d], i - 2)
                        b = banks.await_full(dve, ("QS", i, d))
                        banks.release(dve.tensor_tensor(h3(o1[:, d]), h3(ps[:, b, :]), col4(egc), ALU.mult), ("QS", i, d))
                elif stage == "OS":
                    if i < TT - 1:
                        b = banks.await_full(dve, ("SU", i, d))
                        for h in range(DH):
                            part = slice(h * P, (h + 1) * P)
                            ins = dve.scalar_tensor_tensor(S[:, d, part], S[:, d, part], egl[:, cols.start + h:cols.start + h + 1],
                                                           ps[:, b, part], ALU.mult, ALU.add)
                        banks.release(ins, ("SU", i, d))
                    if lat:
                        banks.await_read(dve, ("QS", i, d))
                        b = banks.await_full(dve, ("I", i, d))
                        banks.release(dve.tensor_tensor(o1[:, d], o1[:, d], ps[:, b, :], ALU.add), ("I", i, d))

            dve.wait_ge(att_set, 1)
            for t in range(LT):
                dve.wait_ge(dn_sq, t + 1)
                dve.tensor_reduce(ssd[:, t], h3(S[:, t % 2]), AX_X, ALU.add).then_inc(dn_ss, 1)
            dve.wait_ge(dn_sd, 1)
            step(dve.reciprocal(rd, rd))
            for t in range(LT):
                dve.tensor_tensor(h3(oacc[:, t]), h3(oacc[:, t]), bc(rd[:, t], [P, DH, P]), ALU.mult).then_inc(dn_rn, 1)
            for item in att:
                kind, h = item[0], item[1]
                par = h % 2
                if kind == "qu":
                    for i in range(2):
                        run = slice(i * 512, (i + 1) * 512)
                        b = banks.await_full(dve, item + (i,))
                        step(dve.tensor_tensor(qa[64:96, par, run], ps[64:96, b, :], rope[64:96, run], ALU.mult))
                        banks.release(dve.tensor_tensor(rot[64:96, :], ps[96:128, b, :], rope[96:128, run], ALU.mult), item + (i,))
                        banks.await_read(dve, item + (i,))
                        dve.tensor_tensor(qa[64:96, par, run], qa[64:96, par, run], rot[64:96, :], ALU.add).then_inc(q_rot, 1)
                        dve.wait_ge(q_rot, 2 * h + i + 1)
                elif kind == "mx":
                    banks.await_full(dve, item)
                    banks.release(dve.tensor_reduce(mx[:, par, item[2]:item[2] + 1],
                                                    ps[:, 0:3, :].rearrange("p a b -> p (a b)")[:, 0:TOK], AX_X, ALU.max), item)
                elif kind == "pv":
                    i = item[2]
                    if h == 0 and i == 0:
                        dve.wait_ge(dn_out, LT)
                    b = banks.await_full(dve, item + (0,))
                    o3 = ps[:, b, 0:4 * (VD + 1)].rearrange("p (a b) -> p a b", b=VD + 1)
                    step(dve.reciprocal(rden[:, 2 * par + i, :], o3[:, :, VD]))
                    banks.release(dve.tensor_tensor(atto[:, 4 * i:4 * i + 4, h * VD:(h + 1) * VD], o3[:, :, 0:VD],
                                                    bc(rden[:, 2 * par + i, :], [P, 4, VD]), ALU.mult), item + (0,))

            step(dve.scalar_tensor_tensor(ffn_scale, modc[:, 4, 0], 1.0, gains[:, 2, :], ALU.add, ALU.mult))
            for m, (row, gain) in enumerate(((2, 1), (5, 3))):
                step(dve.tensor_tensor(modc[:, row, 0], modc[:, row, 0], gains[:, gain, :], ALU.mult))
                for j in range(KT):
                    ins = dve.tensor_scalar(h2T[:, m, j, :], ident, modc[:, row, 0, j:j + 1], None, ALU.mult)
                ins.then_inc(diag_set, 1)
            banks.await_read(dve, ("gb", 1, 1))
            banks.await_read(dve, ("gb", 1, 0))
            for u in range(LT + 3):
                if u < LT:
                    dve.wait_ge(y_ss, u + 1)
                    dve.tensor_tensor(ry[:, u:u + 1], ssy[:, u, 0:1], ssy[:, u, 1:2], ALU.add).then_inc(y_sd, 1)
                    dve.wait_ge(x2_sd, u + 1)
                    step(dve.reciprocal(ry[:, u:u + 1], ry[:, u:u + 1]))
                    for half in range(2):
                        b = banks.await_full(dve, ("y", u, half))
                        banks.release(dve.scalar_tensor_tensor(x2[:, u, half * 512:(half + 1) * 512], ps[:, b, :], ry[:, u:u + 1],
                                                               gate1[:, half * 512:(half + 1) * 512], ALU.mult, ALU.mult), ("y", u, half))
                    for half in range(2):
                        banks.await_read(dve, ("y", u, half))
                    dve.wait_ge(xr_in, 16 * (u + 1))
                    dve.tensor_tensor(x2[:, u], x2[:, u], xr[:, u % 2], ALU.add).then_inc(x2_ready, 1)
                    dve.wait_ge(x2_ready, u + 1)
                    dve.wait_ge(x2_ss, u + 1)
                    step(dve.reciprocal(rz[:, u:u + 1], rz[:, u:u + 1]))
                    dve.tensor_scalar(xr[:, u % 2], x2[:, u], rz[:, u:u + 1], None, ALU.mult).then_inc(xn2_ready, 1)
                if 0 <= u - 2 < LT:
                    t = u - 2
                    b = banks.await_full(dve, ("x2T", t, 1))
                    for j in range(4, KT):
                        ins = dve.tensor_scalar(h2T[:, t % 2, j, :], ps[:, b, (j - 4) * P:(j - 3) * P], ffn_scale[:, j:j + 1],
                                                modc[:, 3, 0, j:j + 1], ALU.mult, ALU.add)
                    banks.release(ins, ("x2T", t, 1))
                if 0 <= u - 3 < LT:
                    t = u - 3
                    b = banks.await_full(dve, ("rt", t))
                    banks.release(dve.tensor_tensor(logits[:, t], ps[:, b, 0:RW], b_rt, ALU.add), ("rt", t))
            for t in (LT - 2, LT - 1):
                banks.await_read(dve, ("rt", t))
            dve.wait_ge(xn_out, 16 * LT)

            iota, steps, falling = route[:, P:2 * P], route[:, 2 * P + LT:2 * P + LT + 8], route[:, 2 * P + LT + 8:2 * P + LT + 8 + E]
            tok_id = route[:, 2 * P:2 * P + LT]
            v3 = lambda ap, b: ap.rearrange("p (a b) -> p a b", b=b)

            def first_max(top, hot, values, width):
                v, hv = v3(values, width), v3(hot, width)
                step(dve.tensor_reduce(top, v, AX_X, ALU.max))
                step(dve.tensor_tensor(hv, v, bc(top, [P, LT, width]), ALU.is_equal))
                step(dve.tensor_tensor(hv, hv, mid(falling[:, E - width:E], LT), ALU.mult))
                step(dve.tensor_reduce(ktop, hv, AX_X, ALU.max))
                step(dve.tensor_tensor(hv, hv, bc(ktop, [P, LT, width]), ALU.is_equal))

            step(dve.tensor_copy(v3(gx, G), logits[:, :, 0:G]))
            first_max(gsum, og, gx, G)
            dve.tensor_tensor(v3(gx, G), v3(gx, G), bc(gsum, [P, LT, G]), ALU.subtract).then_inc(r_exp, 1)
            eg = lambda ap: ap.rearrange("p (t g e) -> p t g e", g=G, e=EG)
            og4 = v3(og, G).unsqueeze(3).to_broadcast([P, LT, G, EG])
            step(dve.tensor_tensor(eg(em), logits[:, :, G:RW].rearrange("p t (g e) -> p t g e", g=G), og4, ALU.mult))
            step(dve.tensor_scalar(og, og, 1e30, -1e30, ALU.mult, ALU.add))
            step(dve.tensor_tensor(eg(em), eg(em), og4, ALU.add))
            first_max(vtop[:, 0], oh[:, 0], em, E)
            step(dve.scalar_tensor_tensor(em, oh[:, 0], -1e30, em, ALU.mult, ALU.add))
            first_max(vtop[:, 1], oh[:, 1], em, E)
            step(dve.tensor_tensor(mark, oh[:, 0], oh[:, 1], ALU.add))
            step(dve.memset(before[:, 0:E], 0.0))
            for t in range(1, LT):
                step(dve.tensor_tensor(before[:, t * E:(t + 1) * E], before[:, (t - 1) * E:t * E], mark[:, (t - 1) * E:t * E], ALU.add))
            dve.tensor_tensor(marks_all, before[:, (LT - 1) * E:], mark[:, (LT - 1) * E:], ALU.add).then_inc(marks_set, 1)
            d8, e8, s8 = small[0][:, 0:LT], small[1][:, 0:LT], small[2][:, 0:LT]
            dve.tensor_tensor(d8, vtop[:, 1], vtop[:, 0], ALU.subtract).then_inc(r_exp2, 1)
            dve.wait_ge(r_expd, 1)
            step(dve.tensor_reduce(gsum, v3(gx, G), AX_X, ALU.add))
            dve.wait_ge(r_exp2d, 1)
            step(dve.tensor_scalar(s8, e8, 1.0, None, ALU.add))
            step(dve.tensor_tensor(s8, s8, gsum, ALU.mult))
            step(dve.reciprocal(cw[:, 0], s8))
            step(dve.tensor_tensor(cw[:, 1], cw[:, 0], e8, ALU.mult))
            b = banks.await_full(dve, ("count",))
            step(dve.tensor_tensor(cmp8[0:E, 0], ps[0:E, b, 0:8], steps[0:E, :], ALU.is_gt))
            step(dve.tensor_reduce(ext[0:E, :], cmp8[0:E, 0], AX_X, ALU.add))
            banks.release(dve.tensor_copy(ext_b[0:E, :], ext[0:E, :].to_broadcast([E, P])), ("count",))
            banks.await_read(dve, ("count",))
            dve.sem_inc(ext_set, 1)
            b = banks.await_full(dve, ("base",))
            dve.tensor_copy(base_row, ps[:, b, 0:E])
            dve.tensor_copy(n_ext, ps[:, b, E:E + 1])
            banks.release(dve.tensor_copy(end_col[0:E, :], ps[0:E, b, 64:65]), ("base",))
            banks.await_read(dve, ("base",))
            dve.tensor_scalar(flags[0:E, :], iota[0:E, 0:16], end_col[0:E, :], None, ALU.is_ge).then_inc(flag_set, 1)
            rank, expert, base_k, q, r, pos, col = small[0], small[1], small[2], small[3], small[4], small[5], small[6]
            oh4 = oh.rearrange("p k (t e) -> p (k t) e", e=E)
            b = banks.await_full(dve, ("rank",))
            t3 = v3(tmp, LT * E)
            banks.release(dve.tensor_tensor(t3, oh, mid(ps[:, b, 0:LT * E], TOPK), ALU.mult), ("rank",))
            banks.await_read(dve, ("rank",))
            step(dve.tensor_reduce(rank, v3(tmp, E), AX_X, ALU.add))
            for dst, row in ((expert, iota[:, 0:E]), (base_k, base_row)):
                step(dve.tensor_tensor(v3(tmp, E), oh4, mid(row, TOPK * LT), ALU.mult))
                step(dve.tensor_reduce(dst, v3(tmp, E), AX_X, ALU.add))
            step(dve.tensor_tensor(cmp8, bc(rank, [P, TOPK * LT, 8]), mid(steps, TOPK * LT), ALU.is_ge))
            step(dve.tensor_reduce(q, cmp8, AX_X, ALU.add))
            step(dve.scalar_tensor_tensor(r, q, -float(P), rank, ALU.mult, ALU.add))
            step(dve.tensor_scalar(pos, q, 0.0, None, ALU.is_gt))
            step(dve.scalar_tensor_tensor(col, base_k, float(E - 1), q, ALU.add, ALU.add))
            step(dve.tensor_tensor(col, col, expert, ALU.subtract))
            step(dve.tensor_tensor(col, col, pos, ALU.mult))
            step(dve.tensor_tensor(col, col, expert, ALU.add))
            step(dve.scalar_tensor_tensor(dest, col, float(P), r, ALU.mult, ALU.add))
            for n in range(TOPK * LT):
                if n >= 4:
                    dve.wait_ge(idx_set, n - 3)
                step(dve.tensor_scalar(hot_r[:, n % 4], iota, r[:, n:n + 1], None, ALU.is_equal))
                dve.tensor_scalar(hot_c[:, n % 4], iota[:, 0:COLS + 2], col[:, n:n + 1], tok_id[:, n % LT:n % LT + 1],
                                  ALU.is_equal, ALU.mult).then_inc(hot_set, 1)
            b = banks.await_full(dve, ("eid",))
            step(dve.memset(table[0:1, :], 0))
            step(dve.tensor_copy(table[0:1, 0:E], iota[0:1, 0:E]))
            banks.release(dve.tensor_scalar(table[0:1, E:COLS], ps[0:1, b, 0:16], float(E - 1), None, ALU.min), ("eid",))
            step(dve.tensor_scalar(table[0:1, 60:61], n_ext[0:1, :], float(E), None, ALU.add))
            b = banks.await_full(dve, ("idx",))
            banks.release(dve.tensor_copy(idx, ps[:, b, 0:COLS + 2]), ("idx",))
            banks.await_read(dve, ("idx",))
            dve.sem_inc(route_set, 1)

            def modulate_half():
                for j in range(4, KT):
                    ins = dve.tensor_scalar(xT[:, j, :], ps[:, 1, (j - 4) * P:(j - 3) * P], ffn_scale[:, j:j + 1],
                                            modc[:, 3, 0, j:j + 1], ALU.mult, ALU.add)
                ins.then_inc(xt_done, 1)

            def hidden_and_next(n, first):
                dve.wait_ge(u_full, n + 1)
                dve.wait_ge(hs_done, n + 1)
                if not first:
                    dve.wait_ge(ht_full, n)
                dve.tensor_tensor(hid, hh, ps[:, 3, :], ALU.mult).then_inc(h_done, 1)
                dve.wait_ge(xt_full, n + 2)
                modulate_half()

            def copy_out(n):
                dve.wait_ge(d_full, n)
                dve.wait_ge(y_out, 16 * n)
                dve.tensor_copy(yo[:, 512:D], ps[:, 6, :]).then_inc(y_done, 1)

            dve.wait_ge(route_set, 1)
            dve.wait_ge(xt_full, 1)
            modulate_half()
            hidden_and_next(0, True)
            blocks = dve.value_load(table[0:1, 60:61], min_val=E, max_val=COLS - 1)
            with dve.Fori(1, blocks) as n:
                hidden_and_next(n, False)
                copy_out(n)
            copy_out(blocks)

            def combine(t):
                dve.wait_ge(f_y0, t + 1)
                dve.scalar_tensor_tensor(f_at(t, 0), f_at(t, 1), cw[:, 1, t:t + 1], f_at(t, 0), ALU.mult, ALU.add).then_inc(f_sum, 1)

            combine(0)
            for t in range(LT):
                if t + 1 < LT:
                    combine(t + 1)
                dve.wait_ge(f_sd, t + 1)
                step(dve.reciprocal(rf[:, t:t + 1], rf[:, t:t + 1]))
                step(dve.scalar_tensor_tensor(f_at(t, 0), f_at(t, 0), rf[:, t:t + 1], gate2, ALU.mult, ALU.mult))
                dve.tensor_tensor(x2[:, t], x2[:, t], f_at(t, 0), ALU.add).then_inc(f_done, 1)



def lay_out(inputs):
    a = {k: np.ascontiguousarray(v) for k, v in inputs.items()}
    a["q_gain_cols"] = a.pop("mla_q_norm")[0].reshape(2, 128).T
    w_in = a.pop("w_in")[0]
    q, kv, kr, qkv, zz, b, g = np.split(w_in, np.cumsum([256, 128, 32, 1536, 512, 8, 8])[:-1].tolist(), axis=1)
    swap = np.arange(32) ^ 1
    a["w_in_a"] = np.concatenate([q, kv, b, g], axis=1)
    a["w_in_r"] = np.concatenate([kr, kr[:, swap]] * 2, axis=1)
    a["w_in_z"], a["w_in_qkv"] = zz, qkv
    a["conv_cols"] = a.pop("dn_conv")[0].reshape(5, 12, 128).transpose(2, 1, 0).reshape(128, 60)
    wq = a.pop("w_q_up")[0].reshape(256, 8, 96)
    a["w_q_up4"] = np.concatenate([wq, wq[:, :, 64 + swap]], axis=2).reshape(256, 1024)
    wkv = a.pop("w_kv_up")[0].reshape(128, 8, 128)
    a["w_k_up"] = wkv[:, :, :64].reshape(128, 512)
    a["w_v_up"] = wkv[:, :, 64:].reshape(128, 512)
    a["w_router"] = np.concatenate([a.pop("w_router_group")[0], a.pop("w_router_expert")[0].transpose(1, 0, 2).reshape(1024, 32)], axis=1)
    a["b_router"] = np.concatenate([a.pop("b_router_group")[0], a.pop("b_router_expert")[0].reshape(32)])
    return {k: np.ascontiguousarray(v) for k, v in a.items()}


def kernel(**inputs):
    import concourse.bacc as bacc
    from concourse.bass_utils import run_bass_kernel_spmd

    nc = bacc.Bacc("TRN2", target_bir_lowering=False, num_devices=1)
    arrays = lay_out(inputs)
    arrays.update({f"k_{k}": v for k, v in shape_constants().items()})
    io, feed = {}, {}
    for name, a in arrays.items():
        feed[f"in_{name}"] = a
        io[name] = nc.dram_tensor(f"in_{name}", a.shape, mybir.dt.from_np(a.dtype), kind="ExternalInput").ap()
    io["out"] = nc.dram_tensor("out", (1, SEQ, D), F32, kind="ExternalOutput").ap()
    hybrid_block_kernel(nc, io)
    result = run_bass_kernel_spmd(nc, [feed], core_ids=[0])
    return result.results[0]["out"]
```

```python
from contextlib import ExitStack

import numpy as np

import concourse.bass as bass
from concourse import mybir

ALU = mybir.AluOpType
ACT = mybir.ActivationFunctionType
AX_X = mybir.AxisListType.X
F32 = mybir.dt.float32
BF16 = mybir.dt.bfloat16
I32 = mybir.dt.int32
U32 = mybir.dt.uint32

P = 128
D = 1024
KT = D // P
SEQ = 1024
CTX = 256
TOK = SEQ + CTX
TT = TOK // P
LT = SEQ // P
EPS = 1e-6
CHUNKS = [(0, 512), (512, 512), (1024, 256)]

H = 8
NOPE, ROPE, VD = 64, 32, 64
QR, KVR = 256, 128
SCALE = (NOPE + ROPE) ** -0.5
WA = QR + KVR + 16
DH = 4
DK = 128
CONV = 5
HALO = CONV // 2
CW = SEQ + CTX + 2 * HALO
RAW = CW + 2 * HALO
LEVELS = [2, 4, 8, 16, 32, 64]

E = 32
EG = 8
G = 4
TOPK = 2
FF = 512
FT = FF // P
EXTRA = TOPK * SEQ // P - 1
COLS = 48
RW = G + E


def shape_constants():
    i = np.arange(P)
    c = {}
    ident = np.eye(P)
    tri_f = (i[:, None] <= i[None, :]).astype(float)
    tri_b = (i[:, None] >= i[None, :]).astype(float)
    strict = (i[:, None] < i[None, :]).astype(float)
    iota = np.tile(i[None, :], (P, 1)).astype(float)
    tok = (i[:, None] + P * np.arange(LT)[None, :]).astype(float)
    c["base"] = np.concatenate([ident, np.ones((P, P)), tri_f, tri_b], axis=1)
    steps = np.tile(P * np.arange(1.0, 9.0)[None, :], (P, 1))
    falling = np.tile(E - np.arange(float(E))[None, :], (P, 1))
    c["route"] = np.concatenate([strict, iota, tok, steps, falling], axis=1)
    low, neg = [], []
    for back in (False, True):
        for s in [1] + LEVELS:
            bi, bj = i[None, :] // s, i[:, None] // s
            m = (bi % 2 == 0) & (bj == bi + 1) if back else (bi % 2 == 1) & (bj == bi - 1)
            low.append(-m.astype(float))
        keep = i[:, None] >= i[None, :] if back else i[:, None] <= i[None, :]
        neg.append(np.where(keep, 0.0, -1e30))
    c["masks"] = np.concatenate(low + neg, axis=1)
    half = ROPE // 2
    inv = (10000.0 ** (-np.arange(0, half, 2, dtype=np.float32) / half)).astype(np.float32)
    rows, cols = np.arange(SEQ) // 64, np.arange(SEQ) % 64
    ang = np.concatenate([rows[:, None].astype(np.float32) * inv, cols[:, None].astype(np.float32) * inv], axis=1)
    cos, sin = np.cos(ang), np.sin(ang)
    rope = np.zeros((P, SEQ))
    rope[64:96] = np.repeat(cos, 2, axis=1).T
    rope[96:128] = np.stack([-sin, sin], axis=-1).reshape(SEQ, ROPE).T
    c["rope"] = rope
    return {k: np.ascontiguousarray(v.astype(np.float32)) for k, v in c.items()}


class Banks:

    def __init__(self, full, free):
        self.full_sem, self.free_sem = full, free
        self.uses = [0] * 8
        self.freed = [0] * 8
        self.jobs, self.parts = {}, {}

    def plan(self, key, bank, parts=1):
        self.jobs[key] = (bank, self.uses[bank] + 1, self.freed[bank])
        self.parts[key] = parts
        self.uses[bank] += 1
        self.freed[bank] += parts

    def bank(self, key):
        return self.jobs[key][0]

    def acquire(self, pe, key):
        bank, _, before = self.jobs[key]
        if before:
            pe.wait_ge(self.free_sem[bank], before)
        return bank

    def filled(self, ins, key):
        ins.then_inc(self.full_sem[self.jobs[key][0]], 1)

    def await_full(self, eng, key):
        bank, use, _ = self.jobs[key]
        eng.wait_ge(self.full_sem[bank], use)
        return bank

    def release(self, ins, key):
        ins.then_inc(self.free_sem[self.jobs[key][0]], 1)

    def await_read(self, eng, key):
        bank, _, before = self.jobs[key]
        eng.wait_ge(self.free_sem[bank], before + self.parts[key])


class Chain:

    def __init__(self, eng, sem):
        self.eng, self.sem, self.count = eng, sem, 0

    def __call__(self, ins):
        ins.then_inc(self.sem, 1)
        self.count += 1
        self.eng.wait_ge(self.sem, self.count)


class Arena:

    def __init__(self, tensor, size):
        self.tensor, self.size, self.top = tensor, size, 0

    def take(self, *dims):
        n = int(np.prod(dims))
        v = self.tensor[:, self.top:self.top + n]
        self.top += n
        assert self.top <= self.size, self.top
        if len(dims) == 2:
            v = v.rearrange("p (a b) -> p a b", b=dims[1])
        elif len(dims) == 3:
            v = v.rearrange("p (a b c) -> p a b c", b=dims[1], c=dims[2])
        return v


def bc(ap, shape):
    return ap.unsqueeze(2).to_broadcast(shape)


def mid(ap, n):
    return ap.unsqueeze(1).to_broadcast([P, n, ap.shape[-1]])


def hybrid_block_kernel(nc, io):
    with ExitStack() as ctx:
        sem = lambda name: ctx.enter_context(nc.semaphore(name))
        size = 53200
        arena = Arena(ctx.enter_context(nc.sbuf_tensor("arena", [P, size], F32)), size)
        ps = ctx.enter_context(nc.psum_tensor("ps", [P, 8, 512], F32))
        banks = Banks([sem(f"bank_full{b}") for b in range(8)], [sem(f"bank_read{b}") for b in range(8)])
        dram = lambda name, *shape: nc.dram_tensor(name, shape, F32, kind="Internal").ap()

        take = arena.take
        ident, ones, tri_f, tri_b = (take(P) for _ in range(4))
        base = arena.tensor[:, 0:4 * P]
        b_ada = take(6, KT)
        gains = take(4, KT)
        q_gain, kv_gain, dn_gain = take(2), take(1), take(1)
        conv_w = take(12, CONV)
        c_col = take(2, KT)
        sc_col = take(KT, 2)
        modc = take(6, 2, KT)
        mix_scale = take(2, KT)
        ffn_scale = take(KT)
        eps_col = take(1)
        neg_a, dt_col = take(8), take(8)
        ssx, sdx, rx = take(TT), take(TT), take(TT)
        ss_a, sd_a, r_a = take(TT, 2), take(TT, 2), take(TT, 2)
        ba = take(TT, 16)
        rope_at = arena.top
        rope = take(SEQ)
        zero = take(P)
        gate = [take(2 * TT * DH) for _ in range(9)]
        g_all, beta, gc, ngc, egc, bege, egl, kdc, gtmp = gate
        persistent_top = arena.top

        z = take(LT, DH * DK)
        qT = take(DH, SEQ)
        kT = take(DH, TOK)
        vT = take(DH, TOK)
        qnT = take(2, SEQ)
        kvnT = take(TOK)
        krT = take(TOK)
        w_ada_of = lambda at: arena.tensor[:, at:at + KT * D].rearrange("p (a b) -> p a b", b=D)
        w_ada_1, w_ada_2 = w_ada_of(persistent_top), w_ada_of(persistent_top + KT * D)
        mod_rows_at = persistent_top + 2 * KT * D
        mod_rows = arena.tensor[:, mod_rows_at:mod_rows_at + 2 * D].rearrange("p (a b) -> p a b", b=D)
        assert mod_rows_at + 2 * D <= persistent_top + LT * DH * DK + DH * (SEQ + 2 * TOK)
        mixer_top = arena.top

        hT = take(KT, TOK)
        w_a = take(KT, WA)
        after_wa = arena.top
        arena.top = mixer_top + KT * TOK
        w_z = take(KT, DH * DK)
        arena.top = max(arena.top, after_wa)
        ring_top = arena.top
        x_ring = take(3, D)
        arena.top = ring_top
        w_c = take(3, KT, P)
        w_r = w_c[:, 2]
        ada_top = arena.top
        w_ada_0 = take(KT, D)
        arena.top = ada_top
        w_ada = [w_ada_0, w_ada_1, w_ada_2]
        raw = take(2, RAW)
        acc = take(2, CW)
        sq, rn = take(CW), take(CW)
        raw_end = arena.top
        arena.top = max(ada_top + 8 * D, raw_end)
        an = take(2, QR + KVR)
        rope_tmp = an.rearrange("p a b -> p (a b)")
        junk = take(D // 2).bitcast(BF16)
        in_proj_top = arena.top
        gt_rows = rope_tmp[:, 0:2 * P]

        arena.top = mixer_top
        nlm = take(2, 6, DH * P)
        intra = take(2, 2, DH * P)
        T = take(2, DH * P)
        Y = take(2, DH * P)
        assert arena.top == mixer_top + KT * TOK
        masks = take(16, P)
        rows = take(2, DH, 2 * P)
        assert arena.top == ring_top
        et = take(2, DH * P)
        U = take(2, 2, DH * P)
        R, kd, Vn, o1, S = (take(2, DH * P) for _ in range(5))
        ks = take(DH * P)
        dn_squares = arena.tensor[:, arena.top - 5 * DH * P:arena.top].rearrange("p (a b) -> p a b", b=DH * P)
        oacc = take(LT, DH * DK)
        dn_top = arena.top

        z_at, qk_at, v_at = persistent_top, persistent_top + LT * DH * DK, persistent_top + LT * DH * DK + DH * (SEQ + TOK)
        arena.top = z_at
        atto = take(LT, H * VD)
        assert arena.top == qk_at
        mixT = take(KT, SEQ)
        arena.top = v_at
        w_q = take(2, H * P)
        w_k, w_v = take(H * NOPE), take(H * VD)
        qa = take(2, SEQ)
        assert arena.top == v_at + DH * TOK
        arena.top = mixer_top
        ka = take(2, TOK)
        V = take(TT * H, VD + 1)
        qb = take(SEQ).bitcast(BF16)
        kb = take(TOK).bitcast(BF16)
        PT = take(2, TT, 512)
        mx, rden = take(2, LT), take(LT, 4)
        ssd, rd = take(LT, DH), take(LT, DH)
        gates_at = persistent_top - 9 * 2 * TT * DH
        rot = arena.tensor[:, gates_at:gates_at + 512]
        assert arena.top <= dn_top - 4096 - 1536, arena.top

        WB = 3 * KT * FF
        wbuf = [arena.tensor[:, v_at:v_at + WB], arena.tensor[:, z_at:z_at + WB]]
        UP_AT, DOWN_AT = KT * FF, 2 * KT * FF

        def slot_of(n):
            return v_at - (n % 2) * (v_at - z_at)

        def weights(n, at, row, rows=1):
            return arena.tensor[:, bass.ds(slot_of(n) + (at + row * 512), rows * 512)]
        arena.top = v_at + WB
        wo1_at = arena.top
        wo1 = take(KT, 512)
        x2 = take(LT, D)
        gate2 = take(D)
        w_rt, b_rt, logits = take(KT, RW), take(RW), take(LT, RW)
        route = take(2 * P + LT + 8 + E)
        cw = take(TOPK, LT)
        dest = take(TOPK * LT).bitcast(I32)
        idx = take(COLS + 2).bitcast(I32)
        table = take(64).bitcast(I32)
        idx_cur = take(1).bitcast(I32)
        ssf, rf = take(LT), take(LT)
        tmp_at = arena.top
        h2T = take(2, KT, P)
        xr = take(2, D)
        gate1 = take(D)
        junk3 = take(512).bitcast(BF16)
        ssy, ry = take(LT, 2), take(LT)
        ssz, rz = take(LT), take(LT)
        y_top = arena.top
        arena.top = tmp_at
        tmp = take(TOPK * LT * E)
        small = [take(TOPK * LT) for _ in range(8)]
        cmp8 = take(TOPK * LT, 8)
        ext_b, base_row, flags = take(P), take(E), take(16)
        ext, end_col, n_ext = take(1), take(1), take(1)
        hot_r, hot_c = take(TOPK * LT, P), take(TOPK * LT, COLS + 2)
        assert arena.top <= y_top, (arena.top, y_top)
        arena.top = gates_at
        before = take(LT * E)
        arena.top = rope_at
        oh = take(TOPK, LT * E)
        mark = take(LT * E)
        marks_all = take(E)
        og, em = take(G), take(E)
        gx = take(LT * G)
        gsum, vtop, ktop = take(LT), take(TOPK, LT), take(LT)
        assert arena.top <= rope_at + SEQ
        oacc_at = dn_top - LT * DH * DK
        assert y_top <= oacc_at
        arena.top = oacc_at
        wo0 = take(KT, 512)
        arena.top = oacc_at
        xg, yo = take(D), take(D)
        arena.top = wo1_at
        xT = take(KT, P)
        hh, hid, hidT = take(FF), take(FF), take(FT, P)

        def f_at(t, k):
            n = TOPK * t + k
            return wbuf[1][:, n * D:(n + 1) * D] if n < 12 else wbuf[0][:, (n - 12) * D:(n - 11) * D]

        dve_step, act_step, pool_step = sem("dve_step"), sem("act_step"), sem("pool_step")
        consts_in, small_in = sem("consts_in"), sem("small_in")
        x_in = [sem(f"x_in{i}") for i in range(3)]
        ada_in = [sem(f"ada_in{i}") for i in range(8)]
        c_in, ada_summed = sem("c_in"), [sem(f"ada_summed{m}") for m in range(2, 6)]
        wr_in, wa_in, wz_in = sem("wr_in"), sem("wa_in"), sem("wz_in")
        wc_in = [sem(f"wc_in{i}") for i in range(3)]
        silu_c = sem("silu_c")
        x_sd, xn_ready, mix_mod = sem("x_sd"), sem("xn_ready"), sem("mix_mod")
        a_sd, an_ready = sem("a_sd"), sem("an_ready")
        raw_edge, conv_done, silu_done, sq_done, norm_done = (
            sem("raw_edge"), sem("conv_done"), sem("silu_done"), sem("sq_done"), sem("norm_done"))
        eps_set = sem("eps_set")
        gate_a, gate_b, gate_c, gate_d, gate_e, gate_f, gate_g = (sem(f"gate_{x}") for x in "abcdefg")
        rows_out, masks_in, dn_start, s_zero = sem("rows_out"), sem("masks_in"), sem("dn_start"), sem("s_zero")
        two = lambda name: [sem(name + x) for x in ("_fwd", "_bwd")]
        rows_in, gm_ready, et_ready, lt_done, u0_ready, nlm_ready, r_ready, o_used = (
            two(x) for x in ("rows_in", "gm_ready", "et_ready", "lt_done", "u0_ready", "nlm_ready", "r_ready", "o_used"))
        ka_set = sem("ka_set")
        att_in, att_set, dn_sq, dn_ss, dn_sd, dn_rn, dn_out = (
            sem(x) for x in ("att_in", "att_set", "dn_sq", "dn_ss", "dn_sd", "dn_rn", "dn_out"))
        q_rot, qb_ready, rden_step = sem("q_rot"), sem("qb_ready"), sem("rden_step")
        wo_in, xr_in, y_sd, y_ss, x2_ss, x2_sd, xn_out, xn2_ready, rt_in, gate1_set, diag_set = (
            sem(x) for x in ("wo_in", "xr_in", "y_sd", "y_ss", "x2_ss", "x2_sd", "xn_out", "xn2_ready", "rt_in", "gate1_set", "diag_set"))
        x2_ready, r_exp, r_expd, r_exp2, r_exp2d, marks_set, ext_set, flag_set, route_set = (
            sem(x) for x in ("x2_ready", "r_exp", "r_expd", "r_exp2", "r_exp2d", "marks_set", "ext_set", "flag_set",
                             "route_set"))
        gate_in, up_in, down_in, tok_in, y_out = (sem(x) for x in ("gate_in", "up_in", "down_in", "tok_in", "y_out"))
        xt_full, xt_done, g_full, u_full, hs_done, h_done, ht_full, ht_done, d_full, y_done, idx_set = (
            sem(x) for x in ("xt_full", "xt_done", "g_full", "u_full", "hs_done", "h_done", "ht_full", "ht_done", "d_full", "y_done", "idx_set"))
        zero_out = sem("zero_out")
        col_set, hot_set = sem("col_set"), [sem("hot_set0"), sem("hot_set1")]
        f_in = [sem(f"f_in{i}") for i in range(4)]
        pool_tick, sp_tick, f_y0, f_sum, f_ss, f_sd, f_done, all_in = (
            sem(x) for x in ("pool_tick", "sp_tick", "f_y0", "f_sum", "f_ss", "f_sd", "f_done", "all_in"))
        xn_dram, yb_dram = dram("xn_dram", SEQ, D), dram("yb_dram", COLS * P, D)
        gate_rows = dram("gate_rows", 2 * TT * DH, 2 * P)
        out_done = sem("out_done")

        def chans(n):
            return CHUNKS[:2] if n < DH else CHUNKS

        def chunk_of(i, d):
            order = [8, 9] + list(range(LT)) if d == 0 else [9, 8] + list(range(LT - 1, -1, -1))
            return order[i]

        def gate_cols(d, c):
            at = (d * TT + c) * DH
            return slice(at, at + DH)

        dn_order = []
        dn_early = [(stage, 0, d, 0) for stage in ("gQ", "gK") for d in range(2)]
        for i in range(TT + 1):
            def both(stage, step, level=0):
                if 0 <= step < TT:
                    dn_order.extend((stage, step, d, level) for d in range(2))
            if i == 0:
                for level in range(6):
                    both("nlm", 0, level)
            both("tr", i - 1)
            both("t2", i)
            for level in range(6):
                both("Y", i, level)
                if level in (0, 1, 2):
                    both(("KS", "V", "OS")[level], i - 1)
                both("U", i, level)
                if level == 2:
                    both("gQ", i + 1)
                if level == 3:
                    both("gK", i + 1)
                    for lv in range(6):
                        both("nlm", i + 1, lv)
                if level < 5:
                    both("T", i, level)

        dn_decays_first = []
        for item in dn_order:
            if item[0] == "gQ":
                at = next(n for n, x in enumerate(dn_decays_first) if x[0:2] == ("OS", item[1] - 2)) if item[1] >= 2 else len(dn_decays_first)
                dn_decays_first.insert(at + item[2] * (item[1] >= 2), item)
            else:
                dn_decays_first.append(item)

        M2_AT = 4
        plan = banks.plan
        def plan_x(t):
            for half in range(2):
                plan(("xT", t, half), 2 * (t % 2) + half)
        for m in range(2):
            for half in range(2):
                plan(("row", m, half), 4 + 2 * m + half)
        plan_x(0)
        plan_x(1)
        for m in range(2):
            plan(("mod", m), 4 + m)
        for t in range(TT + 1):
            if t + 2 < TT:
                plan_x(t + 2)
            if t < TT:
                plan(("A", t), 6 + t % 2)
            if t >= 1:
                plan(("AT", t - 1), 4 + (t - 1) % 2)
            if t == M2_AT:
                plan(("mod", 2), 4)
        for n in range(3):
            plan(("kr", n), n)
        for m in range(3, 6):
            plan(("mod", m), (m + 1) % 4 + 4 * (m == 3))
        for t in range(LT):
            plan(("z", t), 4 + t % 4)
            if t == 3:
                plan(("gc",), 0)
            if t == 5:
                plan(("gT",), 1)
        for n in range(13):
            if n == 11:
                for d in range(2):
                    plan(("gK", 0, d), 6 + d)
            if n < 12:
                for i in range(len(chans(n))):
                    plan(("qkv", n, i), i + 3 * (n % 2))
            if 1 <= n <= 8:
                for i in range(len(chans(n - 1))):
                    plan(("ss", n - 1, i), 6 + i % 2)

        for stage, i, d, level in dn_order:
            lat = i >= 2
            key, b = (stage, i, d), 4 * d
            if stage == "gK":
                plan(key, b + 3)
            elif stage == "gQ":
                if lat:
                    plan(key, b + 3)
            elif stage == "tr":
                plan(("tv", i, d), b + 3)
                plan(("tk", i, d), b + 2)
            elif stage == "t2":
                plan(key, b + 1)
            elif stage == "Y":
                plan(key + (level,), b)
            elif stage == "T":
                plan(key + (level,), b + 1)
            elif stage == "U":
                plan(key + (level,), b + 2)
            elif stage == "KS":
                plan(key, b + 3)
                if lat:
                    plan(("QS", i, d), b + 2)
            elif stage == "V":
                plan(key, b + 3)
            elif stage == "OS":
                if i < TT - 1:
                    plan(("SU", i, d), b + 3)
                if lat:
                    plan(("I", i, d), b + 1)

        att = [("ku", 0), ("qu", 0)] + [("v", k) for k in range(TT)] + [("ku", 1), ("qu", 1)] + [("mx", 0, j) for j in range(LT)] + [("nm", 0, 0)]
        max_bank = lambda item: 3 * (item[2] % 2) if item[1] == 0 else 0
        spread = {5 + 2 * j: j for j in range(LT)}
        for h in range(H):
            for n in range(2 * TT):
                att.append(("sc", h, n // TT, n % TT))
                if h + 1 < H:
                    if n == 0 and h > 0:
                        att.append(("ku", h + 1))
                        att.append(("qu", h + 1))
                    if n in spread:
                        att.append(("mx", h + 1, spread[n]))
                    if n == 15:
                        att.append(("nm", h + 1, 0))
                if n == 1 and h > 0:
                    att.append(("pv", h - 1, 1))
                if n == 2:
                    att.append(("nm", h, 1))
                if n == (12 if h else 19):
                    att.append(("pv", h, 0))
                if h == 1 and n % 2 == 1 and n < 2 * LT:
                    att.append(("dt", n // 2))
        att.append(("pv", H - 1, 1))
        att_idle = list(banks.freed)
        misc = 0
        for item in att:
            if item[0] == "mx":
                plan(item, max_bank(item))
            elif item[0] == "sc":
                plan(item, 3 + (item[2] * TT + item[3]) % 3)
            else:
                for i in range({"ku": 3, "qu": 2}.get(item[0], 1)):
                    plan(item + (i,), 6 + misc % 2, parts=2 if item[0] == "qu" else 1)
                    misc += 1
        for t in range(LT):
            plan(("at", t), 6 + t % 2)
        for m in range(2):
            for half in range(2):
                plan(("gb", m, half), 4 + half)
        for u in range(LT + 2):
            if u < LT:
                plan(("y", u, 0), 2 * (u % 2))
            if 0 <= u - 2 < LT:
                plan(("rt", u - 2), 6 + u % 2)
            if u < LT:
                plan(("y", u, 1), 2 * (u % 2) + 1)
            if 0 <= u - 1 < LT:
                for half in range(2):
                    plan(("x2T", u - 1, half), 4 + half)
        for key, b in (("rank", 0), ("count", 1), ("base", 2), ("eid", 3), ("idx", 4)):
            plan((key,), b)
        moe_idle = list(banks.freed)

        block = ctx.enter_context(nc.Block())

        @block.sync
        def _(sp):
            for i, name in enumerate(("c", "c_ctx")):
                src = io[name] if name == "c_ctx" else io[name].rearrange("a d -> (a d)")
                sp.dma_start(c_col[:, i, :], src.rearrange("(p j) -> p j", j=KT)).then_inc(c_in, 16)

            def load_x(t):
                src = io["x"].rearrange("a t d -> (a t) d") if t < LT else io["ctx"].rearrange("a t d -> (a t) d")
                at = t if t < LT else t - LT
                if t >= 3:
                    banks.await_full(sp, ("xT", t - 3, 1))
                sp.dma_start(x_ring[:, t % 3, :], src[at * P:(at + 1) * P, :]).then_inc(x_in[t % 3], 16)

            ada = io["w_ada"].rearrange("a (p j) n -> (a p) j n", j=KT)

            for q in range(4):
                m, half = q // 2, q % 2
                sp.dma_start(w_ada[m][:, 4 * half:4 * half + 4, :], ada[:, 4 * half:4 * half + 4, m * D:(m + 1) * D]).then_inc(ada_in[q], 16)
            sp.dma_start(base, io["k_base"]).then_inc(consts_in, 16)
            load_x(0)
            sp.dma_start(b_ada, io["b_ada"].rearrange("a (m p j) -> (a p) m j", p=P, j=KT)).then_inc(small_in, 16)
            for i, name in enumerate(("norm_mix_pre", "norm_mix_post", "norm_ffn_pre", "norm_ffn_post")):
                sp.dma_start(gains[:, i, :], io[name].rearrange("a (p j) -> (a p) j", j=KT)).then_inc(small_in, 16)
            load_x(1)
            sp.dma_start(q_gain, io["q_gain_cols"]).then_inc(small_in, 16)
            sp.dma_start(kv_gain, io["mla_kv_norm"].rearrange("a (p j) -> (a p) j", j=1)).then_inc(small_in, 16)
            sp.dma_start(dn_gain, io["dn_norm"].rearrange("a (p j) -> (a p) j", j=1)).then_inc(small_in, 16)
            sp.dma_start(conv_w, io["conv_cols"].rearrange("p (n w) -> p n w", w=CONV)).then_inc(small_in, 16)
            sp.dma_start(neg_a, io["dn_A_log"].rearrange("a s h -> (a s h)").partition_broadcast(P)).then_inc(small_in, 16)
            sp.dma_start(dt_col, io["dn_dt_bias"].rearrange("a s h -> (a s h)").partition_broadcast(P)).then_inc(small_in, 16)
            sp.dma_start(rope, io["k_rope"]).then_inc(small_in, 16)
            load_x(2)
            sp.dma_start(w_a, io["w_in_a"].rearrange("(p j) n -> p j n", j=KT)).then_inc(wa_in, 16)
            sp.dma_start(w_ada[2], ada[:, :, 2 * D:3 * D]).then_inc(ada_in[4], 16)

            def load_ada(m):
                sp.dma_start(w_ada[m % 3], ada[:, :, m * D:(m + 1) * D]).then_inc(ada_in[m + 2], 16)

            for t in range(3, TT):
                load_x(t)
                if t in (4, 7):
                    m = (t - 4) // 3
                    banks.await_full(sp, ("row", m, 1))
                    load_ada(m + 3)
                if t - 3 == M2_AT + 1:
                    banks.await_full(sp, ("mod", 2))
                    load_ada(5)
            banks.await_full(sp, ("xT", TT - 2, 1))
            sp.dma_start(w_r, io["w_in_r"].rearrange("(p j) n -> p j n", j=KT)).then_inc(wr_in, 16)
            banks.await_full(sp, ("A", TT - 1))
            sp.dma_start(w_z, io["w_in_z"].rearrange("(p j) n -> p j n", j=KT)).then_inc(wz_in, 16)
            banks.await_full(sp, ("xT", TT - 1, 1))
            for n in range(12):
                if n == 2:
                    banks.await_full(sp, ("kr", 2))
                if n >= 3:
                    banks.await_full(sp, ("qkv", n - 3, len(chans(n - 3)) - 1))
                sp.dma_start(w_c[:, n % 3], io["w_in_qkv"].rearrange("(p j) n -> p j n", j=KT)[:, :, n * P:(n + 1) * P])\
                  .then_inc(wc_in[n % 3], 16)
                if n == 2:
                    banks.await_read(sp, ("gT",))
                    sp.dma_start(gate_rows, gt_rows[0:2 * TT * DH, :]).then_inc(rows_out, 16)
            for t in range(LT - 4, LT):
                banks.await_full(sp, ("z", t))
            sp.dma_start(masks, io["k_masks"].rearrange("p (a b) -> p a b", b=P)).then_inc(masks_in, 16)
            sp.wait_ge(rows_out, 16)
            for i in range(TT):
                for d in range(2):
                    if i >= 1:
                        sp.wait_ge(lt_done[d], i)
                    r0 = gate_cols(d, chunk_of(i, d)).start
                    sp.dma_start(rows[:, d].rearrange("p h c -> p (h c)"),
                                 gate_rows[r0:r0 + DH, :].rearrange("h c -> (h c)").partition_broadcast(P)).then_inc(rows_in[d], 16)
                if i == 1:
                    sp.wait_ge(eps_set, 1)
                    sp.dma_start(yb_dram[E * P:COLS * P, :].rearrange("(p r) (g c) -> p (r g) c", p=P, c=P),
                                 mid(zero, (COLS - E) * KT)).then_inc(zero_out, 16)
            banks.await_full(sp, ("tv", TT - 1, 1))
            banks.await_full(sp, ("tv", TT - 1, 0))
            sp.dma_start(w_q, io["w_q_up4"].rearrange("(k p) n -> p k n", p=P)).then_inc(att_in, 16)
            sp.dma_start(w_k, io["w_k_up"]).then_inc(att_in, 16)
            sp.dma_start(w_v, io["w_v_up"]).then_inc(att_in, 16)
            w_out = io["w_out"].rearrange("a (k p) n -> (a p) k n", p=P)
            banks.await_full(sp, ("dt", LT - 1, 0))
            sp.dma_start(wo0, w_out[:, :, 0:512]).then_inc(wo_in, 16)
            banks.await_full(sp, ("pv", H - 1, 1, 0))
            sp.dma_start(wo1, w_out[:, :, 512:D]).then_inc(wo_in, 16)
            sp.dma_start(w_rt, io["w_router"].rearrange("(p j) n -> p j n", j=KT)).then_inc(rt_in, 16)
            sp.dma_start(b_rt, io["b_router"].partition_broadcast(P)).then_inc(rt_in, 16)
            sp.dma_start(route, io["k_route"]).then_inc(rt_in, 16)
            xs = io["x"].rearrange("a t d -> (a t) d")
            banks.await_read(sp, ("pv", H - 1, 1, 0))
            for t in range(2):
                sp.dma_start(xr[:, t], xs[t * P:(t + 1) * P, :]).then_inc(xr_in, 16)
                sp.wait_ge(xr_in, 16 * (t + 1))

            def load_expert(e, n, first):
                for w, at, k, read, landed in ((io["w_exp_gate"], 0, KT, g_full, gate_in), (io["w_exp_up"], UP_AT, KT, u_full, up_in),
                                               (io["w_exp_down"], DOWN_AT, FT, d_full, down_in)):
                    src = w[0][bass.ds(e, 1)].rearrange("a (p j) f -> (a p) (j f)", j=k)
                    dst = weights(n, at, 0, KT)
                    if not first:
                        sp.wait_ge(read, n - 1)
                        sp.sem_inc(sp_tick, 1)
                        sp.wait_ge(landed, 16 * n)
                        sp.sem_inc(sp_tick, 1)
                    sp.dma_start(dst, src).then_inc(landed, 16)

            load_expert(0, 0, True)
            for t in range(LT):
                sp.wait_ge(xn2_ready, t + 1)
                sp.dma_start(xn_dram[t * P:(t + 1) * P, :], xr[:, t % 2]).then_inc(xn_out, 16)
                if t + 2 < LT:
                    banks.await_full(sp, ("x2T", t, 1))
                    sp.wait_ge(xn_out, 16 * (t + 1))
                    sp.dma_start(xr[:, t % 2], xs[(t + 2) * P:(t + 3) * P, :]).then_inc(xr_in, 16)
                    sp.wait_ge(xr_in, 16 * (t + 3))
            banks.await_full(sp, ("y", LT - 1, 1))
            for landed in (gate_in, up_in, down_in):
                sp.wait_ge(landed, 16)
            load_expert(1, 1, True)
            sp.wait_ge(route_set, 1)
            blocks = sp.value_load(table[0:1, 60:61], min_val=E, max_val=COLS - 1)
            with sp.Fori(2, blocks) as n:
                load_expert(sp.value_load(table[0:1, bass.ds(n, 1)], min_val=0, max_val=E - 1), n, False)
            out = io["out"].rearrange("a t d -> (a t) d")
            for t in range(LT):
                sp.wait_ge(f_done, t + 1)
                sp.dma_start(out[t * P:(t + 1) * P, :], x2[:, t]).then_inc(all_in, 16)
            sp.wait_ge(all_in, 16 * LT)

        @block.tensor
        def _(pe):
            def mod_rows_of(m):
                for half in range(2):
                    banks.acquire(pe, ("row", m, half))
                for k in range(KT):
                    if k % 4 == 0:
                        pe.wait_ge(ada_in[2 * m + k // 4], 16)
                    for half in range(2):
                        ins = pe.matmul(ps[0:2, 4 + 2 * m + half, :], sc_col[:, k, :], w_ada[m][:, k, half * 512:(half + 1) * 512],
                                        start=(k == 0), stop=(k == KT - 1))
                        if k == KT - 1:
                            banks.filled(ins, ("row", m, half))

            def mod_cols(m):
                for half in range(2):
                    banks.await_read(pe, ("row", m, half))
                b = banks.acquire(pe, ("mod", m))
                for j in range(KT):
                    ins = pe.matmul(ps[:, b, 2 * j:2 * j + 2], mod_rows[0:2, m, j::KT], ident[0:2, 0:2],
                                    start=(j == 0), stop=True, skip_group_check=True)
                banks.filled(ins, ("mod", m))

            def mod_sum(m):
                pe.wait_ge(ada_summed[m - 2], 1)
                b = banks.acquire(pe, ("mod", m))
                for j in range(KT):
                    ins = pe.matmul(ps[:, b, 2 * j:2 * j + 2], w_ada[m % 3][:, 0, j::KT], ones[:, 0:2],
                                    start=(j == 0), stop=True, skip_group_check=True)
                banks.filled(ins, ("mod", m))

            def turn_x(t):
                pe.wait_ge(xn_ready, t + 1)
                for half in range(2):
                    b = banks.acquire(pe, ("xT", t, half))
                    for j in range(4):
                        ins = pe.transpose(ps[:, b, j * P:(j + 1) * P], x_ring[:, t % 3, 4 * half + j::KT], ident)
                    banks.filled(ins, ("xT", t, half))

            pe.wait_ge(silu_c, 1)
            for m in range(2):
                mod_rows_of(m)
            pe.wait_ge(consts_in, 16)
            turn_x(0)
            turn_x(1)
            for m in range(2):
                mod_cols(m)
            for t in range(TT + 1):
                if t + 2 < TT:
                    turn_x(t + 2)
                if t < TT:
                    if t == 0:
                        pe.wait_ge(wa_in, 16)
                    for half in range(2):
                        banks.await_read(pe, ("xT", t, half))
                    b = banks.acquire(pe, ("A", t))
                    for k in range(KT):
                        ins = pe.matmul(ps[:, b, 0:WA], hT[:, k, t * P:(t + 1) * P], w_a[:, k, :], start=(k == 0), stop=(k == KT - 1))
                    banks.filled(ins, ("A", t))
                if t >= 1:
                    s = t - 1
                    pe.wait_ge(an_ready, s + 1)
                    b = banks.acquire(pe, ("AT", s))
                    for j in range(3):
                        ins = pe.transpose(ps[:, b, j * P:(j + 1) * P], an[:, s % 2, j * P:(j + 1) * P], ident)
                    banks.filled(ins, ("AT", s))
                if t == M2_AT:
                    mod_sum(2)
            pe.wait_ge(wr_in, 16)
            for n, (c0, cn) in enumerate(CHUNKS):
                b = banks.acquire(pe, ("kr", n))
                for k in range(KT):
                    ins = pe.matmul(ps[:, b, 0:cn], w_r[:, k, :], hT[:, k, c0:c0 + cn], start=(k == 0), stop=(k == KT - 1))
                banks.filled(ins, ("kr", n))
            for m in range(3, 6):
                mod_sum(m)
            pe.wait_ge(wz_in, 16)
            for t in range(LT):
                b = banks.acquire(pe, ("z", t))
                for k in range(KT):
                    ins = pe.matmul(ps[:, b, :], hT[:, k, t * P:(t + 1) * P], w_z[:, k, :], start=(k == 0), stop=(k == KT - 1))
                banks.filled(ins, ("z", t))
                n = TT * DH
                if t == 3:
                    pe.wait_ge(gate_e, 1)
                    b = banks.acquire(pe, ("gc",))
                    for d, tri in enumerate((tri_f, tri_b)):
                        pe.matmul(ps[:, b, d * n:(d + 1) * n], tri, g_all[:, d * n:(d + 1) * n], start=(d == 0), stop=True, skip_group_check=True)
                    banks.filled(pe.matmul(ps[:, b, P:P + 2 * n], ones, g_all, start=False, stop=True, skip_group_check=True), ("gc",))
                if t == 5:
                    pe.wait_ge(gate_f, 1)
                    b = banks.acquire(pe, ("gT",))
                    pe.transpose(ps[0:2 * n, b, 0:P], gc, ident)
                    banks.filled(pe.transpose(ps[0:2 * n, b, P:2 * P], beta, ident), ("gT",))
            def heads(key, lhsT, rhs, transpose=False):
                b = banks.acquire(pe, key)
                for h in range(DH):
                    out = ps[:, b, h * P:(h + 1) * P]
                    ins = pe.transpose(out, lhsT(h), ident) if transpose else pe.matmul(out, lhsT(h), rhs(h), start=True, stop=True)
                banks.filled(ins, key)

            def dn_stage(stage, i, d, level):
                c, lat, par = chunk_of(i, d), i >= 2, i % 2
                tok = slice(c * P, (c + 1) * P)
                of = lambda buf: lambda h: buf[:, h * P:(h + 1) * P]
                kc, qc, vc = (lambda h: kT[:, h, tok]), (lambda h: qT[:, h, tok]), (lambda h: vT[:, h, tok])
                if stage == "gK":
                    heads(("gK", i, d), kc, kc)
                elif stage == "gQ" and lat:
                    heads(("gQ", i, d), kc, qc)
                elif stage == "tr":
                    if i == 0:
                        pe.wait_ge(silu_done, 12)
                    heads(("tv", i, d), vc, None, transpose=True)
                    heads(("tk", i, d), kc, None, transpose=True)
                elif stage == "t2":
                    pe.wait_ge(u0_ready[d], i + 1)
                    heads(("t2", i, d), of(U[:, par, d]), None, transpose=True)
                elif stage == "Y":
                    pe.wait_ge(nlm_ready[d], 6 * i + level + 1)
                    banks.await_read(pe, ("t2", i, d) if level == 0 else ("T", i, d, level - 1))
                    heads(("Y", i, d, level), of(nlm[:, d, level]), of(T[:, d]))
                elif stage == "U":
                    banks.await_read(pe, ("Y", i, d, level))
                    heads(("U", i, d, level), of(Y[:, d]), of(U[:, par, d]))
                elif stage == "T":
                    banks.await_read(pe, ("U", i, d, level))
                    heads(("T", i, d, level), of(U[:, par, d]), None, transpose=True)
                elif stage == "KS":
                    if i == 0:
                        pe.wait_ge(s_zero, 1)
                    else:
                        banks.await_read(pe, ("SU", i - 1, d))
                    heads(("KS", i, d), kc, of(S[:, d]))
                    if lat:
                        heads(("QS", i, d), qc, of(S[:, d]))
                elif stage == "V":
                    banks.await_read(pe, ("U", i, d, 5))
                    pe.wait_ge(r_ready[d], i + 1)
                    heads(("V", i, d), of(U[:, par, d]), of(R[:, d]))
                elif stage == "OS":
                    banks.await_read(pe, ("V", i, d))
                    banks.await_read(pe, ("tk", i, d))
                    if i < TT - 1:
                        heads(("SU", i, d), of(kd[:, d]), of(Vn[:, d]))
                    if lat:
                        banks.await_read(pe, ("gQ", i, d))
                        heads(("I", i, d), of(intra[:, par, d]), of(Vn[:, d]))

            for n in range(13):
                if n == 11:
                    pe.wait_ge(norm_done, 8)
                    for item in dn_early:
                        dn_stage(*item)
                if n < 12:
                    pe.wait_ge(wc_in[n % 3], 16 * (n // 3 + 1))
                    for i, (c0, cn) in enumerate(chans(n)):
                        b = banks.acquire(pe, ("qkv", n, i))
                        for k in range(KT):
                            ins = pe.matmul(ps[:, b, 0:cn], w_c[:, n % 3, k, :], hT[:, k, c0:c0 + cn], start=(k == 0), stop=(k == KT - 1))
                        banks.filled(ins, ("qkv", n, i))
                if 1 <= n <= 8:
                    pe.wait_ge(sq_done, n)
                    for i, (c0, cn) in enumerate(chans(n - 1)):
                        b = banks.acquire(pe, ("ss", n - 1, i))
                        o = c0 if i < 2 else c0 + 2 * HALO
                        ins = pe.matmul(ps[:, b, 0:cn], ones, sq[:, o:o + cn], start=True, stop=True)
                        banks.filled(ins, ("ss", n - 1, i))


            for item in dn_order:
                dn_stage(*item)

            pe.wait_ge(att_in, 48)
            for item in att:
                kind, h = item[0], item[1]
                par = h % 2
                if item == ("mx", 0, 0):
                    for b in (1, 2, 4, 5):
                        pe.wait_ge(banks.free_sem[b], att_idle[b])
                if kind == "v":
                    b = banks.acquire(pe, item + (0,))
                    banks.filled(pe.matmul(ps[:, b, :], kvnT[:, h * P:(h + 1) * P], w_v, start=True, stop=True), item + (0,))
                elif kind == "ku":
                    for i, (c0, cn) in enumerate(CHUNKS):
                        b = banks.acquire(pe, item + (i,))
                        banks.filled(pe.matmul(ps[0:NOPE, b, 0:cn], w_k[:, h * NOPE:(h + 1) * NOPE], kvnT[:, c0:c0 + cn],
                                               start=True, stop=True), item + (i,))
                elif kind == "qu":
                    for i in range(2):
                        b = banks.acquire(pe, item + (i,))
                        for k in range(2):
                            ins = pe.matmul(ps[:, b, :], w_q[:, k, h * P:(h + 1) * P], qnT[:, k, i * 512:(i + 1) * 512],
                                            start=(k == 0), stop=(k == 1))
                        banks.filled(ins, item + (i,))
                elif kind == "mx":
                    j = item[2]
                    pe.wait_ge(qb_ready, 2 * h + 2)
                    banks.acquire(pe, item)
                    g = max_bank(item)
                    for i, (c0, cn) in enumerate(CHUNKS):
                        ins = pe.matmul(ps[:, g + i, 0:cn], qb[0:96, par * SEQ + j * P:par * SEQ + (j + 1) * P],
                                        kb[0:96, par * TOK + c0:par * TOK + c0 + cn], start=True, stop=True)
                    banks.filled(ins, item)
                elif kind == "nm":
                    i = item[2]
                    banks.await_read(pe, ("mx", h, 4 * i + 3))
                    b = banks.acquire(pe, item + (0,))
                    for j in range(4):
                        ins = pe.matmul(ps[96:97, b, j * P:(j + 1) * P], mx[:, par, 4 * i + j:4 * i + j + 1], ident, start=True, stop=True)
                    banks.filled(ins, item + (0,))
                elif kind == "sc":
                    i, k = item[2], item[3]
                    if k == 0:
                        banks.await_read(pe, ("nm", h, i, 0))
                        pe.wait_ge(q_rot, 2 * h + i + 1)
                        banks.await_read(pe, ("qu", h, i))
                        banks.await_read(pe, ("ku", h, 2))
                    b = banks.acquire(pe, item)
                    banks.filled(pe.matmul(ps[:, b, :], ka[0:97, par, k * P:(k + 1) * P], qa[0:97, par, i * 512:(i + 1) * 512],
                                           start=True, stop=True), item)
                elif kind == "pv":
                    i = item[2]
                    for k in range(TT - 3, TT):
                        banks.await_read(pe, ("sc", h, i, k))
                    if h == 0 and i == 0:
                        banks.await_read(pe, ("v", TT - 1, 0))
                        banks.await_read(pe, ("v", TT - 2, 0))
                    b = banks.acquire(pe, item + (0,))
                    for j in range(4):
                        for k in range(TT):
                            ins = pe.matmul(ps[:, b, j * (VD + 1):(j + 1) * (VD + 1)], PT[:, i, k, j * P:(j + 1) * P], V[:, k * H + h, :],
                                            start=(k == 0), stop=(k == TT - 1))
                    banks.filled(ins, item + (0,))
                elif kind == "dt":
                    pe.wait_ge(dn_out, LT)
                    b = banks.acquire(pe, item + (0,))
                    for j in range(DH):
                        ins = pe.transpose(ps[:, b, j * P:(j + 1) * P], oacc[:, h, j * P:(j + 1) * P], ident)
                    banks.filled(ins, item + (0,))
            for i in range(2):
                banks.await_read(pe, ("pv", H - 1, i, 0))
            for t in range(LT):
                b = banks.acquire(pe, ("at", t))
                for j in range(4):
                    ins = pe.transpose(ps[:, b, j * P:(j + 1) * P], atto[:, t, j * P:(j + 1) * P], ident)
                banks.filled(ins, ("at", t))

            for m in range(2):
                pe.wait_ge(diag_set, m + 1)
                for half in range(2):
                    b = banks.acquire(pe, ("gb", m, half))
                    for j in range(4):
                        ins = pe.matmul(ps[:, b, j * P:(j + 1) * P], ones, h2T[:, m, 4 * half + j, :], start=True, stop=True)
                    banks.filled(ins, ("gb", m, half))
            for t in range(LT):
                banks.await_read(pe, ("at", t))
                banks.await_read(pe, ("dt", t, 0))
            pe.wait_ge(wo_in, 32)
            def project(u, half, w):
                b = banks.acquire(pe, ("y", u, half))
                for k in range(KT):
                    ins = pe.matmul(ps[:, b, :], mixT[:, k, u * P:(u + 1) * P], w[:, k, :], start=(k == 0), stop=(k == KT - 1))
                banks.filled(ins, ("y", u, half))

            for u in range(LT + 2):
                if u < LT:
                    project(u, 0, wo0)
                if 0 <= u - 2 < LT:
                    t = u - 2
                    pe.wait_ge(rt_in, 48)
                    for half in range(2):
                        banks.await_read(pe, ("x2T", t, half))
                    b = banks.acquire(pe, ("rt", t))
                    for k in range(KT):
                        ins = pe.matmul(ps[:, b, 0:RW], h2T[:, t % 2, k, :], w_rt[:, k, :], start=(k == 0), stop=(k == KT - 1))
                    banks.filled(ins, ("rt", t))
                if u < LT:
                    project(u, 1, wo1)
                if 0 <= u - 1 < LT:
                    t = u - 1
                    pe.wait_ge(xn2_ready, t + 1)
                    for half in range(2):
                        b = banks.acquire(pe, ("x2T", t, half))
                        for j in range(4):
                            ins = pe.transpose(ps[:, b, j * P:(j + 1) * P], xr[:, t % 2, 4 * half + j::KT], ident)
                        banks.filled(ins, ("x2T", t, half))

            strict, iota = route[:, 0:P], route[:, P:2 * P]
            pe.wait_ge(marks_set, 1)
            b = banks.acquire(pe, ("rank",))
            pe.matmul(ps[:, b, 0:LT * E], strict, mark, start=True, stop=False)
            banks.filled(pe.matmul(ps[:, b, 0:LT * E], ones, before, start=False, stop=True), ("rank",))
            b = banks.acquire(pe, ("count",))
            banks.filled(pe.matmul(ps[0:E, b, 0:8], marks_all, ones[:, 0:8], start=True, stop=True), ("count",))
            pe.wait_ge(ext_set, 1)
            b = banks.acquire(pe, ("base",))
            pe.matmul(ps[:, b, 0:E], ext_b[0:E, :], strict[0:E, 0:E], start=True, stop=True, skip_group_check=True)
            pe.matmul(ps[:, b, E:E + 1], ext_b[0:E, :], ones[0:E, 0:1], start=False, stop=True, skip_group_check=True)
            banks.filled(pe.matmul(ps[0:E, b, 64:65], tri_f[0:E, 0:E], ext[0:E, :], start=False, stop=True, skip_group_check=True), ("base",))
            pe.wait_ge(flag_set, 1)
            b = banks.acquire(pe, ("eid",))
            banks.filled(pe.matmul(ps[0:1, b, 0:16], ones[0:E, 0:1], flags[0:E, :], start=True, stop=True), ("eid",))
            b = banks.acquire(pe, ("idx",))
            for n in range(TOPK * LT):
                if n == 0:
                    pe.wait_ge(col_set, 1)
                if n % LT == 0:
                    pe.wait_ge(hot_set[n // LT], 1)
                ins = pe.matmul(ps[:, b, 0:COLS + 2], hot_r[:, n], hot_c[:, n], start=(n == 0), stop=(n == TOPK * LT - 1))
            banks.filled(ins, ("idx",))

            pe.wait_ge(route_set, 1)
            for b in range(8):
                if moe_idle[b]:
                    pe.wait_ge(banks.free_sem[b], moe_idle[b])

            def turn_tokens():
                for j in range(KT):
                    ins = pe.transpose(ps[:, j // 4, (j % 4) * P:(j % 4 + 1) * P], xg[:, j::KT], ident)
                ins.then_inc(xt_full, 1)

            def hidden(n, first):
                pe.wait_ge(xt_done, 2 * n + 2)
                if not first:
                    pe.wait_ge(hs_done, n)
                pe.wait_ge(gate_in, 16 * n + 16)
                for k in range(KT):
                    ins = pe.matmul(ps[:, 2, :], xT[:, k, :], weights(n, 0, k), start=(k == 0), stop=(k == KT - 1))
                ins.then_inc(g_full, 1)
                if not first:
                    pe.wait_ge(h_done, n)
                pe.wait_ge(up_in, 16 * n + 16)
                for k in range(KT):
                    ins = pe.matmul(ps[:, 3, :], xT[:, k, :], weights(n, UP_AT, k), start=(k == 0), stop=(k == KT - 1))
                ins.then_inc(u_full, 1)
                pe.wait_ge(tok_in, 16 * n + 32)
                turn_tokens()

            def down(n):
                pe.wait_ge(ht_done, n)
                pe.wait_ge(y_done, 2 * n + 1)
                pe.wait_ge(down_in, 16 * n)
                for half in range(2):
                    for j in range(FT):
                        ins = pe.matmul(ps[:, 5 + half, :], hidT[:, j, :], weights(n + 1, DOWN_AT, 2 * j + half), start=(j == 0), stop=(j == FT - 1))
                ins.then_inc(d_full, 1)

            def turn_hidden(n):
                pe.wait_ge(h_done, n + 1)
                for j in range(FT):
                    ins = pe.transpose(ps[:, 4, j * P:(j + 1) * P], hid[:, j::FT], ident)
                ins.then_inc(ht_full, 1)

            pe.wait_ge(tok_in, 16)
            turn_tokens()
            hidden(0, True)
            turn_hidden(0)
            blocks = pe.value_load(table[0:1, 60:61], min_val=E, max_val=COLS - 1)
            with pe.Fori(1, blocks) as n:
                hidden(n, False)
                down(n)
                turn_hidden(n)
            down(blocks)

        @block.scalar
        def _(act):
            step = Chain(act, act_step)
            act.wait_ge(c_in, 32)
            act.wait_ge(eps_set, 1)
            act.activation(sc_col.rearrange("p k w -> p w k"), c_col, ACT.Silu).then_inc(silu_c, 1)

            def x_stats(t):
                act.wait_ge(x_in[t % 3], 16 * (t // 3 + 1))
                step(act.activation(junk, x_ring[:, t % 3, :], ACT.Square, scale=D ** -0.5, accum_out=ssx[:, t:t + 1]))
                act.activation(sdx[:, t:t + 1], ssx[:, t:t + 1], ACT.Sqrt, bias=eps_col).then_inc(x_sd, 1)

            x_stats(0)
            x_stats(1)
            for m in range(2):
                b = banks.await_full(act, ("row", m, 0))
                banks.release(act.activation(mod_rows[0:2, m, 0:512], ps[0:2, b, :], ACT.Copy), ("row", m, 0))
            act.wait_ge(mix_mod, 1)
            for t in range(TT + 1):
                if t + 2 < TT:
                    x_stats(t + 2)
                if t < TT:
                    w = 0 if t < LT else 1
                    b = banks.await_full(act, ("xT", t, 0))
                    for j in range(4):
                        ins = act.activation(hT[:, j, t * P:(t + 1) * P], ps[:, b, j * P:(j + 1) * P], ACT.Identity,
                                             bias=modc[:, 0, w, j:j + 1], scale=mix_scale[:, w, j:j + 1])
                    banks.release(ins, ("xT", t, 0))
                if t >= 1:
                    s = t - 1
                    b = banks.await_full(act, ("A", s))
                    step(act.activation(junk[:, 0:QR], ps[:, b, 0:QR], ACT.Square, scale=QR ** -0.5, accum_out=ss_a[:, s, 0:1]))
                    step(act.activation(junk[:, 0:KVR], ps[:, b, QR:QR + KVR], ACT.Square, scale=KVR ** -0.5, accum_out=ss_a[:, s, 1:2]))
                    act.activation(sd_a[:, s, :], ss_a[:, s, :], ACT.Sqrt, bias=eps_col).then_inc(a_sd, 1)
            act.wait_ge(small_in, 16 * 12)
            step(act.activation(neg_a, neg_a, ACT.Exp))
            act.wait_ge(gate_a, 1)
            act.activation(ba[:, :, 0:8], ba[:, :, 0:8], ACT.Exp, scale=-1.0).then_inc(gate_b, 1)
            act.wait_ge(gate_c, 1)
            step(act.activation(gtmp, gtmp, ACT.Exp))
            act.activation(gtmp, gtmp, ACT.Ln, bias=ones[:, 0:1]).then_inc(gate_d, 1)
            for m in range(3, 6):
                banks.await_full(act, ("mod", m))
            for t in range(LT):
                b = banks.await_full(act, ("z", t))
                banks.release(act.activation(z[:, t, :], ps[:, b, :], ACT.Silu), ("z", t))
            act.wait_ge(gate_f, 1)
            act.activation(egc, gc, ACT.Exp)
            act.activation(egl, egl, ACT.Exp)
            act.activation(kdc, kdc, ACT.Exp).then_inc(gate_g, 1)
            def dn_stage(stage, i, d, level):
                if stage == "gQ":
                    act.wait_ge(gm_ready[d], i + 1)
                    at = gate_cols(d, chunk_of(i, d)).start
                    for h in range(DH):
                        part = et[:, d, h * P:(h + 1) * P]
                        ins = act.activation(part, part, ACT.Exp, bias=ngc[:, at + h:at + h + 1])
                    ins.then_inc(et_ready[d], 1)
                elif stage == "tr":
                    b = banks.await_full(act, ("tk", i, d))
                    at = gate_cols(d, chunk_of(i, d)).start
                    for h in range(DH):
                        ins = act.activation(kd[:, d, h * P:(h + 1) * P], ps[:, b, h * P:(h + 1) * P], ACT.Copy, scale=kdc[:, at + h:at + h + 1])
                    banks.release(ins, ("tk", i, d))
                elif stage in ("t2", "Y", "T", "V"):
                    key = (stage, i, d) + ((level,) if stage in "YT" else ())
                    b = banks.await_full(act, key)
                    dst = {"t2": T, "T": T, "Y": Y, "V": Vn}[stage]
                    banks.release(act.activation(dst[:, d], ps[:, b, :], ACT.Copy), key)

            act.wait_ge(raw_edge, 1)
            for n in range(13):
                if n == 11:
                    for item in dn_early:
                        dn_stage(*item)
                if n < 12:
                    if n >= 2:
                        act.wait_ge(conv_done, n - 1)
                    for i, (c0, cn) in enumerate(chans(n)):
                        b = banks.await_full(act, ("qkv", n, i))
                        o = HALO + c0 + (2 * HALO if i == 2 else 0)
                        banks.release(act.activation(raw[:, n % 2, o:o + cn], ps[:, b, 0:cn], ACT.Copy), ("qkv", n, i))
                if 1 <= n <= 8:
                    if n >= 2:
                        act.wait_ge(norm_done, n - 1)
                    for i, (c0, cn) in enumerate(chans(n - 1)):
                        b = banks.await_full(act, ("ss", n - 1, i))
                        o = c0 if i < 2 else c0 + 2 * HALO
                        banks.release(act.activation(rn[:, o:o + cn], ps[:, b, 0:cn], ACT.Sqrt, bias=eps_col), ("ss", n - 1, i))
                if n == 11:
                    for item in dn_decays_first[0:16]:
                        dn_stage(*item)
                if n < 12:
                    act.wait_ge(conv_done, n + 1)
                    if n < 8:
                        width = SEQ if n < DH else CW
                        act.activation(acc[:, n % 2, 0:width], acc[:, n % 2, 0:width], ACT.Silu).then_inc(silu_done, 1)
                    else:
                        act.activation(vT[:, n - 8, 0:SEQ], acc[:, n % 2, 0:SEQ], ACT.Silu)
                        act.activation(vT[:, n - 8, SEQ:TOK], acc[:, n % 2, SEQ + 2 * HALO:CW], ACT.Silu).then_inc(silu_done, 1)

            for item in dn_decays_first[16:]:
                dn_stage(*item)

            act.wait_ge(ka_set, 1)
            for item in att:
                kind, h = item[0], item[1]
                par = h % 2
                if item == ("v", 0):
                    act.wait_ge(att_set, 1)
                    banks.await_read(act, ("ku", 0, 2))
                    banks.await_read(act, ("ku", 0, 1))
                    act.activation(kb[0:96, 0:TOK], ka[0:96, 0, :], ACT.Copy).then_inc(qb_ready, 1)
                if item == ("sc", 0, 1, 0):
                    act.wait_ge(dn_ss, LT)
                    act.activation(rd, ssd, ACT.Sqrt, scale=1.0 / DK, bias=eps_col).then_inc(dn_sd, 1)
                if kind == "v":
                    b = banks.await_full(act, item + (0,))
                    banks.release(act.activation(V[:, h * H:(h + 1) * H, 0:VD], ps[:, b, :].rearrange("p (a b) -> p a b", b=VD), ACT.Copy), item + (0,))
                elif kind == "ku":
                    for i, (c0, cn) in enumerate(CHUNKS):
                        b = banks.await_full(act, item + (i,))
                        banks.release(act.activation(ka[0:NOPE, par, c0:c0 + cn], ps[0:NOPE, b, 0:cn], ACT.Copy), item + (i,))
                elif kind == "qu":
                    for i in range(2):
                        b = banks.await_full(act, item + (i,))
                        banks.release(act.activation(qa[0:NOPE, par, i * 512:(i + 1) * 512], ps[0:NOPE, b, :], ACT.Copy), item + (i,))
                elif kind == "nm":
                    i = item[2]
                    b = banks.await_full(act, item + (0,))
                    banks.release(act.activation(qa[96:97, par, i * 512:(i + 1) * 512], ps[96:97, b, :], ACT.Copy, scale=-1.0), item + (0,))
                elif kind == "sc":
                    b = banks.await_full(act, item)
                    banks.release(act.activation(PT[:, item[2], item[3], :], ps[:, b, :], ACT.Exp, scale=SCALE), item)
                elif kind == "dt":
                    b = banks.await_full(act, item + (0,))
                    banks.release(act.activation(mixT[:, 4:8, h * P:(h + 1) * P], ps[:, b, :].rearrange("p (a b) -> p a b", b=P), ACT.Copy,
                                                 scale=dn_gain[:, 0:1]), item + (0,))
            for t in range(LT):
                b = banks.await_full(act, ("at", t))
                banks.release(act.activation(mixT[:, 0:4, t * P:(t + 1) * P], ps[:, b, :].rearrange("p (a b) -> p a b", b=P), ACT.Copy), ("at", t))
            for m, dst in enumerate((gate1, gate2)):
                for half in range(2):
                    b = banks.await_full(act, ("gb", m, half))
                    out = dst.rearrange("p (q j) -> p j q", j=KT)[:, 4 * half:4 * half + 4, :]
                    banks.release(act.activation(out, ps[:, b, :].rearrange("p (j q) -> p j q", q=P), ACT.Copy), ("gb", m, half))
            for u in range(LT + 1):
                if u < LT:
                    for half in range(2):
                        b = banks.await_full(act, ("y", u, half))
                        ins = act.activation(junk3[:, 0:512], ps[:, b, :], ACT.Square, scale=D ** -0.5, accum_out=ssy[:, u, half:half + 1])
                        if half == 0:
                            step(ins)
                    ins.then_inc(y_ss, 1)
                if u >= 1:
                    t = u - 1
                    b = banks.await_full(act, ("x2T", t, 0))
                    for j in range(4):
                        ins = act.activation(h2T[:, t % 2, j, :], ps[:, b, j * P:(j + 1) * P], ACT.Identity,
                                             bias=modc[:, 3, 0, j:j + 1], scale=ffn_scale[:, j:j + 1])
                    banks.release(ins, ("x2T", t, 0))
                if u < LT:
                    act.wait_ge(y_sd, u + 1)
                    act.activation(ry[:, u:u + 1], ry[:, u:u + 1], ACT.Sqrt, bias=eps_col).then_inc(x2_sd, 1)
                    act.wait_ge(x2_ready, u + 1)
                    step(act.activation(junk3, x2[:, u], ACT.Square, scale=D ** -0.5, accum_out=ssz[:, u:u + 1]))
                    act.activation(rz[:, u:u + 1], ssz[:, u:u + 1], ACT.Sqrt, bias=eps_col).then_inc(x2_ss, 1)
            act.wait_ge(r_exp, 1)
            act.activation(gx, gx, ACT.Exp)
            act.activation(small[7][:, LT:2 * LT], small[7][:, 0:LT], ACT.Exp).then_inc(r_expd, 1)

            def modulate_half():
                for j in range(4):
                    ins = act.activation(xT[:, j, :], ps[:, 0, j * P:(j + 1) * P], ACT.Identity,
                                         bias=modc[:, 3, 0, j:j + 1], scale=ffn_scale[:, j:j + 1])
                ins.then_inc(xt_done, 1)

            def gate_and_next(n, first):
                act.wait_ge(g_full, n + 1)
                if not first:
                    act.wait_ge(h_done, n)
                act.activation(hh, ps[:, 2, :], ACT.Silu).then_inc(hs_done, 1)
                act.wait_ge(xt_full, n + 2)
                modulate_half()

            def copy_hidden(n):
                act.wait_ge(ht_full, n + 1)
                act.activation(hidT, ps[:, 4, :].rearrange("p (a b) -> p a b", b=P), ACT.Copy).then_inc(ht_done, 1)

            def copy_out(n):
                act.wait_ge(d_full, n)
                act.wait_ge(y_out, 16 * n)
                act.activation(yo[:, 0:512], ps[:, 5, :], ACT.Copy).then_inc(y_done, 1)

            def store_out(n):
                act.wait_ge(y_done, 2 * n + 3)
                act.dma_start(yb_dram[bass.ds((n - 1) * P, P), :], yo).then_inc(y_out, 16)

            def square_sum(t):
                act.wait_ge(f_sum, t + 1)
                step(act.activation(xg, f_at(t, 0), ACT.Square, scale=D ** -0.5, accum_out=ssf[:, t:t + 1]))
                act.activation(rf[:, t:t + 1], ssf[:, t:t + 1], ACT.Sqrt, bias=eps_col).then_inc(f_sd, 1)

            act.wait_ge(route_set, 1)
            act.wait_ge(zero_out, 16)
            act.sem_inc(y_done, 3)
            act.sem_inc(y_out, 16)
            act.wait_ge(xt_full, 1)
            modulate_half()
            gate_and_next(0, True)
            copy_hidden(0)
            blocks = act.value_load(table[0:1, 60:61], min_val=E, max_val=COLS - 1)
            with act.Fori(1, blocks) as n:
                gate_and_next(n, False)
                copy_out(n)
                copy_hidden(n)
                store_out(n)
            copy_out(blocks)
            store_out(blocks)
            for t in range(LT):
                act.wait_ge(f_in[t % 4], 16 * TOPK * (t // 4 + 1))
                act.activation(f_at(t, 0), f_at(t, 0), ACT.Copy, scale=cw[:, 0, t:t + 1]).then_inc(f_y0, 1)
                if t >= 1:
                    square_sum(t - 1)
            square_sum(LT - 1)

        @block.gpsimd
        def _(pool):
            step = Chain(pool, pool_step)
            pool.memset(zero, 0.0)
            pool.memset(eps_col, EPS).then_inc(eps_set, 1)
            pool.wait_ge(silu_c, 1)
            w = w_ada[4 % 3]
            pool.wait_ge(ada_in[4 + 2], 16)
            for k in range(KT):
                step(pool.tensor_scalar(w[:, k, :], w[:, k, :], sc_col[:, k, 0:1], None, ALU.mult))
                if k >= 1:
                    ins = pool.tensor_tensor(w[:, 0, :], w[:, 0, :], w[:, k, :], ALU.add)
                    if k < KT - 1:
                        step(ins)
            ins.then_inc(ada_summed[4 - 2], 1)
            def dn_stage(stage, i, d, level):
                c, par = chunk_of(i, d), i % 2
                if stage == "gQ":
                    pool.wait_ge(rows_in[d], 16 * (i + 1))
                    if i >= 1:
                        pool.wait_ge(nlm_ready[d], 6 * i)
                    e3 = et[:, d].rearrange("p (h i) -> p h i", h=DH)
                    pool.tensor_tensor(e3, rows[:, d, :, 0:P], mid(masks[:, 14 + d, :], DH), ALU.add).then_inc(gm_ready[d], 1)
                elif stage == "gK":
                    e3 = et[:, d].rearrange("p (h i) -> p h i", h=DH)
                    banks.await_read(pool, ("gK", i, d))
                    pool.tensor_tensor(e3, e3, rows[:, d, :, P:2 * P], ALU.mult).then_inc(lt_done[d], 1)
                    pool.wait_ge(lt_done[d], i + 1)
                    if i >= 2:
                        banks.await_full(pool, ("V", i - 2, d))
                    u3 = U[:, par, d].rearrange("p (h i) -> p h i", h=DH)
                    step(pool.tensor_tensor(u3, e3, mid(masks[:, 7 * d, :], DH), ALU.mult))
                    pool.tensor_tensor(u3, u3, mid(ident, DH), ALU.add).then_inc(u0_ready[d], 1)
                elif stage == "nlm":
                    if i >= 1:
                        banks.await_full(pool, ("Y", i - 1, d, level))
                    pool.tensor_tensor(nlm[:, d, level].rearrange("p (h i) -> p h i", h=DH), et[:, d].rearrange("p (h i) -> p h i", h=DH),
                                       mid(masks[:, 7 * d + 1 + level, :], DH), ALU.mult).then_inc(nlm_ready[d], 1)
                elif stage == "OS" and i >= 2:
                    banks.await_read(pool, ("I", i, d))
                    first = (c < LT // 2) == (d == 0)
                    if first:
                        pool.tensor_copy(oacc[:, c], o1[:, d]).then_inc(o_used[d], 1)
                    else:
                        pool.wait_ge(o_used[1 - d], (11 - i) - 1)
                        pool.tensor_tensor(oacc[:, c], oacc[:, c], o1[:, d], ALU.add).then_inc(o_used[d], 1)

            banks.await_full(pool, ("mod", 5))
            step(pool.memset(raw.rearrange("p a b -> p (a b)"), 0.0))
            pool.sem_inc(raw_edge, 1)
            for n in range(8):
                width = SEQ if n < DH else CW
                pool.wait_ge(silu_done, n + 1)
                if n >= 1:
                    banks.await_full(pool, ("ss", n - 1, len(chans(n - 1)) - 1))
                pool.tensor_tensor(sq[:, 0:width], acc[:, n % 2, 0:width], acc[:, n % 2, 0:width], ALU.mult).then_inc(sq_done, 1)

            pool.wait_ge(masks_in, 16)
            banks.await_full(pool, ("qkv", 9, 2))
            for item in dn_early[0:2]:
                dn_stage(*item)
            banks.await_full(pool, ("qkv", 10, 2))
            for item in dn_early[2:4]:
                dn_stage(*item)
            banks.await_full(pool, ("qkv", 11, 2))
            for item in dn_decays_first[0:12]:
                dn_stage(*item)
            pool.wait_ge(silu_done, 12)
            pool.wait_ge(norm_done, 8)
            pool.wait_ge(conv_done, 12)
            pool.memset(S.rearrange("p a b -> p (a b)"), 0.0).then_inc(s_zero, 1)
            for item in dn_decays_first[12:-2]:
                dn_stage(*item)
            for d in range(2):
                pool.wait_ge(o_used[d], LT - 1)
            banks.await_full(pool, ("Y", TT - 1, 0, 5))
            step(pool.memset(ka[96:97].rearrange("p a b -> p (a b)"), 1.0))
            pool.tensor_copy(ka[64:96, 0, :], krT[64:96, :]).then_inc(ka_set, 1)
            for d in range(2):
                banks.await_full(pool, ("I", TT - 1, d))
                banks.await_read(pool, ("V", TT - 1, d))
            pool.wait_ge(ka_set, 1)
            pool.memset(V[:, :, VD:VD + 1], 1.0).then_inc(att_set, 1)
            pool.wait_ge(att_set, 1)
            for item in dn_decays_first[-2:]:
                dn_stage(*item)
                pool.wait_ge(o_used[item[2]], LT)

            def cast(h):
                par = h % 2
                for i in range(2):
                    banks.await_read(pool, ("qu", h, i))
                pool.wait_ge(q_rot, 2 * h + 2)
                if h >= 2:
                    banks.await_full(pool, ("mx", h - 2, LT - 1))
                pool.tensor_copy(qb[0:96, par * SEQ:(par + 1) * SEQ], qa[0:96, par, :]).then_inc(qb_ready, 1)
                banks.await_read(pool, ("ku", h, 2))
                banks.await_read(pool, ("ku", h, 1))
                pool.tensor_copy(kb[0:96, par * TOK:(par + 1) * TOK], ka[0:96, par, :]).then_inc(qb_ready, 1)

            step(pool.tensor_copy(ka[64:96, 1, :], krT[64:96, :]))
            cast(1)
            pool.wait_ge(qb_ready, 4)
            for t in range(LT):
                if t >= 5:
                    pool.wait_ge(dn_ss, t - 4)
                pool.tensor_tensor(dn_squares[:, t % 5], oacc[:, t], oacc[:, t], ALU.mult).then_inc(dn_sq, 1)
            for t in range(LT // 2):
                pool.wait_ge(dn_rn, t + 1)
                pool.tensor_tensor(oacc[:, t], oacc[:, t], z[:, t], ALU.mult).then_inc(dn_out, 1)
            pool.wait_ge(dn_out, LT)
            for h in range(2, H):
                cast(h)

            def gather(col, count):
                pool.tensor_copy(idx_cur, idx[:, col]).then_inc(idx_set, 1)
                pool.wait_ge(idx_set, count)
                pool.sem_inc(pool_tick, 1)
                pool.indirect_dma_start(out=xg, out_offset=None, in_=xn_dram,
                                        in_offset=bass.IndirectOffsetOnAxis(idx_cur, axis=0)).then_inc(tok_in, 16)

            made = 0
            pool.wait_ge(route_set, 1)
            pool.wait_ge(xn_out, 16 * LT)
            gather(slice(0, 1), made + 1)
            blocks = pool.value_load(table[0:1, 60:61], min_val=E, max_val=COLS - 1)
            with pool.Fori(1, blocks + 1) as n:
                pool.wait_ge(xt_full, n)
                pool.sem_inc(pool_tick, 1)
                gather(bass.ds(n, 1), n + (made + 1))
            pool.wait_ge(y_out, 16 * blocks + 16)
            pool.sem_inc(pool_tick, 1)
            for t in range(LT):
                if t >= 4:
                    pool.wait_ge(f_in[t % 4], 16 * TOPK * (t // 4))
                for k in range(TOPK):
                    pool.indirect_dma_start(out=f_at(t, k), out_offset=None, in_=yb_dram,
                                            in_offset=bass.IndirectOffsetOnAxis(dest[:, k * LT + t:k * LT + t + 1], axis=0)).then_inc(f_in[t % 4], 16)

        @block.vector
        def _(dve):
            step = Chain(dve, dve_step)

            def x_norm(t):
                dve.wait_ge(x_sd, t + 1)
                step(dve.reciprocal(rx[:, t:t + 1], sdx[:, t:t + 1]))
                dve.tensor_scalar(x_ring[:, t % 3, :], x_ring[:, t % 3, :], rx[:, t:t + 1], None, ALU.mult).then_inc(xn_ready, 1)

            def mod_out(m):
                b = banks.await_full(dve, ("mod", m))
                banks.release(dve.tensor_tensor(modc[:, m], ps[:, b, 0:2 * KT].rearrange("p (j w) -> p w j", w=2),
                                                mid(b_ada[:, m, :], 2), ALU.add), ("mod", m))

            x_norm(0)
            x_norm(1)
            for m in range(2):
                b = banks.await_full(dve, ("row", m, 1))
                banks.release(dve.tensor_copy(mod_rows[0:2, m, 512:D], ps[0:2, b, :]), ("row", m, 1))
            dve.wait_ge(small_in, 16 * 12)
            for m in range(2):
                mod_out(m)
            banks.await_read(dve, ("mod", 1))
            dve.scalar_tensor_tensor(mix_scale, modc[:, 1], 1.0, mid(gains[:, 0, :], 2), ALU.add, ALU.mult).then_inc(mix_mod, 1)
            dve.wait_ge(mix_mod, 1)
            for t in range(TT + 2):
                if t + 2 < TT:
                    x_norm(t + 2)
                if t < TT:
                    w = 0 if t < LT else 1
                    b = banks.await_full(dve, ("xT", t, 1))
                    for j in range(4):
                        ins = dve.tensor_scalar(hT[:, 4 + j, t * P:(t + 1) * P], ps[:, b, j * P:(j + 1) * P],
                                                mix_scale[:, w, 4 + j:5 + j], modc[:, 0, w, 4 + j:5 + j], ALU.mult, ALU.add)
                    banks.release(ins, ("xT", t, 1))
                if 0 <= t - 1 < TT:
                    s = t - 1
                    b = banks.await_full(dve, ("A", s))
                    dve.wait_ge(a_sd, s + 1)
                    step(dve.reciprocal(r_a[:, s, :], sd_a[:, s, :]))
                    if s >= 2:
                        banks.await_full(dve, ("AT", s - 2))
                    dve.tensor_scalar(an[:, s % 2, 0:QR], ps[:, b, 0:QR], r_a[:, s, 0:1], None, ALU.mult)
                    dve.tensor_scalar(an[:, s % 2, QR:], ps[:, b, QR:QR + KVR], r_a[:, s, 1:2], None, ALU.mult).then_inc(an_ready, 1)
                    banks.release(dve.tensor_copy(ba[:, s, :], ps[:, b, QR + KVR:WA]), ("A", s))
                if t >= 2:
                    s = t - 2
                    b = banks.await_full(dve, ("AT", s))
                    if s < LT:
                        for j in range(2):
                            dve.tensor_scalar(qnT[:, j, s * P:(s + 1) * P], ps[:, b, j * P:(j + 1) * P], q_gain[:, j:j + 1], None, ALU.mult)
                    banks.release(dve.tensor_scalar(kvnT[:, s * P:(s + 1) * P], ps[:, b, QR:QR + KVR], kv_gain[:, 0:1], None, ALU.mult), ("AT", s))
                if t == M2_AT + 1:
                    mod_out(2)
                if t < 11:
                    m, t0 = (2, 0) if t < 4 else (3, 4) if t < 7 else (5, 7)
                    per = 3 if m == 3 else 2
                    w = w_ada[m % 3]
                    for k in range(per * (t - t0), min(per * (t - t0 + 1), KT)):
                        if k == 0:
                            dve.wait_ge(ada_in[m + 2], 16)
                            ins = dve.tensor_scalar(w[:, 0, :], w[:, 0, :], sc_col[:, 0, 0:1], None, ALU.mult)
                        else:
                            ins = dve.scalar_tensor_tensor(w[:, 0, :], w[:, k, :], sc_col[:, k, 0:1], w[:, 0, :], ALU.mult, ALU.add)
                        if k < KT - 1:
                            step(ins)
                        else:
                            ins.then_inc(ada_summed[m - 2], 1)
            banks.await_read(dve, ("A", TT - 1))
            by_dir = lambda ap: ap.rearrange("p t (s h) -> p s t h", s=2)
            flat4 = lambda ap: ap.rearrange("p (s t h) -> p s t h", s=2, h=DH)
            over_t = lambda ap: ap.rearrange("p (s h) -> p s h", s=2).unsqueeze(2).to_broadcast([P, 2, TT, DH])
            dve.tensor_tensor(flat4(g_all), by_dir(ba[:, :, 8:16]), over_t(dt_col), ALU.add).then_inc(gate_a, 1)
            dve.wait_ge(gate_a, 1)
            dve.scalar_tensor_tensor(gtmp, g_all, -1.0, g_all, ALU.mult, ALU.min).then_inc(gate_c, 1)
            dve.wait_ge(gate_c, 1)
            step(dve.tensor_scalar(g_all, g_all, 0.0, None, ALU.max))
            dve.wait_ge(gate_b, 1)
            step(dve.tensor_scalar(ba[:, :, 0:8], ba[:, :, 0:8], 1.0, None, ALU.add))
            step(dve.reciprocal(ba[:, :, 0:8], ba[:, :, 0:8]))
            step(dve.tensor_copy(flat4(beta), by_dir(ba[:, :, 0:8])))
            dve.wait_ge(gate_d, 1)
            step(dve.tensor_tensor(g_all, g_all, gtmp, ALU.add))
            step(dve.tensor_tensor(flat4(gtmp), flat4(g_all), over_t(neg_a), ALU.mult))
            dve.tensor_scalar(g_all, gtmp, -1.0, None, ALU.mult).then_inc(gate_e, 1)
            for n, (c0, cn) in enumerate(CHUNKS):
                b = banks.await_full(dve, ("kr", n))
                if n < 2:
                    step(dve.tensor_tensor(krT[64:96, c0:c0 + cn], ps[64:96, b, 0:cn], rope[64:96, c0:c0 + cn], ALU.mult))
                    banks.release(dve.tensor_tensor(rope_tmp[64:96, 0:cn], ps[96:128, b, 0:cn], rope[96:128, c0:c0 + cn], ALU.mult), ("kr", n))
                    banks.await_read(dve, ("kr", n))
                    step(dve.tensor_tensor(krT[64:96, c0:c0 + cn], krT[64:96, c0:c0 + cn], rope_tmp[64:96, 0:cn], ALU.add))
                else:
                    banks.release(dve.tensor_copy(krT[64:96, c0:c0 + cn], ps[64:96, b, 0:cn]), ("kr", n))
            for m in range(3, 6):
                mod_out(m)
            b = banks.await_full(dve, ("gc",))
            n80 = 2 * TT * DH
            step(dve.tensor_copy(gc, ps[:, b, 0:n80]))
            dve.tensor_scalar(ngc, ps[:, b, 0:n80], -1.0, None, ALU.mult)
            step(dve.tensor_copy(egl, ps[:, b, P:P + n80]))
            banks.release(dve.tensor_tensor(kdc, ps[:, b, P:P + n80], gc, ALU.subtract), ("gc",))
            banks.await_read(dve, ("gc",))
            dve.sem_inc(gate_f, 1)
            b = banks.await_full(dve, ("gT",))
            banks.release(dve.tensor_copy(gt_rows[0:n80, :], ps[0:n80, b, 0:2 * P]), ("gT",))
            dve.wait_ge(gate_g, 1)
            step(dve.tensor_tensor(bege, beta, egc, ALU.mult))
            h3 = lambda ap: ap.rearrange("p (h i) -> p h i", h=DH)
            def dn_stage(stage, i, d, level):
                c, lat, par = chunk_of(i, d), i >= 2, i % 2
                cols = gate_cols(d, c)
                col4 = lambda g: bc(g[:, cols], [P, DH, P])
                if stage == "gQ" and lat:
                    dve.wait_ge(et_ready[d], i + 1)
                    b = banks.await_full(dve, ("gQ", i, d))
                    banks.release(dve.tensor_tensor(intra[:, par, d], ps[:, b, :], et[:, d], ALU.mult), ("gQ", i, d))
                elif stage == "gK":
                    dve.wait_ge(et_ready[d], i + 1)
                    if lat:
                        banks.await_read(dve, ("gQ", i, d))
                    b = banks.await_full(dve, ("gK", i, d))
                    banks.release(dve.tensor_tensor(et[:, d], ps[:, b, :], et[:, d], ALU.mult), ("gK", i, d))
                elif stage == "tr":
                    if i == 0:
                        dve.wait_ge(silu_done, 12)
                    b = banks.await_full(dve, ("tv", i, d))
                    banks.release(dve.tensor_tensor(h3(R[:, d]), h3(ps[:, b, :]), col4(beta), ALU.mult), ("tv", i, d))
                elif stage == "U":
                    key = ("U", i, d, level)
                    b = banks.await_full(dve, key)
                    banks.release(dve.tensor_tensor(U[:, par, d], U[:, par, d], ps[:, b, :], ALU.add), key)
                elif stage == "KS":
                    b = banks.await_full(dve, ("KS", i, d))
                    if d == 1 or i >= 1:
                        dve.wait_ge(r_ready[1 - d], i + d)
                    banks.release(dve.tensor_tensor(h3(ks), h3(ps[:, b, :]), col4(bege), ALU.mult), ("KS", i, d))
                    banks.await_read(dve, ("KS", i, d))
                    banks.await_read(dve, ("tv", i, d))
                    dve.tensor_tensor(R[:, d], R[:, d], ks, ALU.subtract).then_inc(r_ready[d], 1)
                    if lat:
                        if i >= 3:
                            dve.wait_ge(o_used[d], i - 2)
                        b = banks.await_full(dve, ("QS", i, d))
                        banks.release(dve.tensor_tensor(h3(o1[:, d]), h3(ps[:, b, :]), col4(egc), ALU.mult), ("QS", i, d))
                elif stage == "OS":
                    if i < TT - 1:
                        b = banks.await_full(dve, ("SU", i, d))
                        for h in range(DH):
                            part = slice(h * P, (h + 1) * P)
                            ins = dve.scalar_tensor_tensor(S[:, d, part], S[:, d, part], egl[:, cols.start + h:cols.start + h + 1],
                                                           ps[:, b, part], ALU.mult, ALU.add)
                        banks.release(ins, ("SU", i, d))
                    if lat:
                        banks.await_read(dve, ("QS", i, d))
                        b = banks.await_full(dve, ("I", i, d))
                        banks.release(dve.tensor_tensor(o1[:, d], o1[:, d], ps[:, b, :], ALU.add), ("I", i, d))

            dve.wait_ge(raw_edge, 1)
            for n in range(13):
                if n == 11:
                    for item in dn_early:
                        dn_stage(*item)
                if n < 12:
                    width = SEQ if n < DH else CW
                    for i in range(len(chans(n))):
                        banks.await_read(dve, ("qkv", n, i))
                    if n >= 10:
                        dve.wait_ge(silu_done, n - 1)
                    step(dve.tensor_scalar(acc[:, n % 2, 0:width], raw[:, n % 2, 0:width], conv_w[:, n, 0:1], None, ALU.mult))
                    for o in range(1, CONV):
                        ins = dve.scalar_tensor_tensor(acc[:, n % 2, 0:width], raw[:, n % 2, o:o + width], conv_w[:, n, o:o + 1],
                                                       acc[:, n % 2, 0:width], ALU.mult, ALU.add)
                        if o < CONV - 1:
                            step(ins)
                    ins.then_inc(conv_done, 1)
                if 1 <= n <= 8:
                    s = n - 1
                    width = SEQ if s < DH else CW
                    for i in range(len(chans(s))):
                        banks.await_read(dve, ("ss", s, i))
                    if s >= DH:
                        if s == DH:
                            step(dve.memset(rn[:, SEQ:SEQ + 2 * HALO], 1.0))
                    step(dve.reciprocal(rn[:, 0:width], rn[:, 0:width]))
                    if s < DH:
                        dve.scalar_tensor_tensor(qT[:, s, :], acc[:, s % 2, 0:SEQ], DK ** -0.5, rn[:, 0:SEQ], ALU.mult, ALU.mult).then_inc(norm_done, 1)
                    else:
                        dve.tensor_tensor(kT[:, s - DH, 0:SEQ], acc[:, s % 2, 0:SEQ], rn[:, 0:SEQ], ALU.mult)
                        dve.tensor_tensor(kT[:, s - DH, SEQ:TOK], acc[:, s % 2, SEQ + 2 * HALO:CW], rn[:, SEQ + 2 * HALO:CW], ALU.mult).then_inc(norm_done, 1)
                    dve.wait_ge(norm_done, n)

            for item in dn_order:
                dn_stage(*item)

            def dn_square_sums(tiles):
                for t in tiles:
                    dve.wait_ge(dn_sq, t + 1)
                    dve.tensor_reduce(ssd[:, t], h3(dn_squares[:, t % 5]), AX_X, ALU.add).then_inc(dn_ss, 1)

            def dn_norm(tiles):
                if tiles[0] == 0:
                    dve.wait_ge(dn_sd, 1)
                    step(dve.reciprocal(rd, rd))
                for t in tiles:
                    dve.tensor_tensor(h3(oacc[:, t]), h3(oacc[:, t]), bc(rd[:, t], [P, DH, P]), ALU.mult).then_inc(dn_rn, 1)

            def dn_gate():
                for t in range(LT // 2, LT):
                    dve.wait_ge(dn_rn, t + 1)
                    dve.tensor_tensor(oacc[:, t], oacc[:, t], z[:, t], ALU.mult).then_inc(dn_out, 1)

            dve.wait_ge(att_set, 1)
            for item in att:
                kind, h = item[0], item[1]
                par = h % 2
                if kind == "qu":
                    for i in range(2):
                        run = slice(i * 512, (i + 1) * 512)
                        b = banks.await_full(dve, item + (i,))
                        step(dve.tensor_tensor(qa[64:96, par, run], ps[64:96, b, :], rope[64:96, run], ALU.mult))
                        banks.release(dve.tensor_tensor(rot[64:96, :], ps[96:128, b, :], rope[96:128, run], ALU.mult), item + (i,))
                        banks.await_read(dve, item + (i,))
                        if h == 0:
                            banks.await_read(dve, item + (i,))
                        dve.tensor_tensor(qa[64:96, par, run], qa[64:96, par, run], rot[64:96, :], ALU.add).then_inc(q_rot, 1)
                        dve.wait_ge(q_rot, 2 * h + i + 1)
                    if h == 0:
                        dve.tensor_copy(qb[0:96, 0:SEQ], qa[0:96, 0, :]).then_inc(qb_ready, 1)
                elif kind == "mx":
                    g = banks.await_full(dve, item)
                    banks.release(dve.tensor_reduce(mx[:, par, item[2]:item[2] + 1],
                                                    ps[:, g:g + 3, :].rearrange("p a b -> p (a b)")[:, 0:TOK], AX_X, ALU.max), item)
                    if item == ("mx", 0, LT - 1):
                        dn_square_sums(range(0, 5))
                    elif item == ("mx", 1, 1):
                        dn_square_sums(range(5, LT))
                    elif h == 1 and 3 <= item[2] < 7:
                        dn_norm(range(2 * item[2] - 6, 2 * item[2] - 4))
                    elif item == ("mx", 1, 7):
                        dn_gate()
                elif kind == "pv":
                    i = item[2]
                    if h == 0 and i == 0:
                        dve.wait_ge(dn_out, LT)
                    b = banks.await_full(dve, item + (0,))
                    o3 = ps[:, b, 0:4 * (VD + 1)].rearrange("p (a b) -> p a b", b=VD + 1)
                    step(dve.reciprocal(rden[:, 2 * par + i, :], o3[:, :, VD]))
                    banks.release(dve.tensor_tensor(atto[:, 4 * i:4 * i + 4, h * VD:(h + 1) * VD], o3[:, :, 0:VD],
                                                    bc(rden[:, 2 * par + i, :], [P, 4, VD]), ALU.mult), item + (0,))

            step(dve.scalar_tensor_tensor(ffn_scale, modc[:, 4, 0], 1.0, gains[:, 2, :], ALU.add, ALU.mult))
            for m, (row, gain) in enumerate(((2, 1), (5, 3))):
                step(dve.tensor_tensor(modc[:, row, 0], modc[:, row, 0], gains[:, gain, :], ALU.mult))
                for j in range(KT):
                    ins = dve.tensor_scalar(h2T[:, m, j, :], ident, modc[:, row, 0, j:j + 1], None, ALU.mult)
                ins.then_inc(diag_set, 1)
            banks.await_read(dve, ("gb", 1, 1))
            banks.await_read(dve, ("gb", 1, 0))
            iota, steps, falling = route[:, P:2 * P], route[:, 2 * P + LT:2 * P + LT + 8], route[:, 2 * P + LT + 8:2 * P + LT + 8 + E]
            tok_id = route[:, 2 * P:2 * P + LT]
            v3 = lambda ap, b: ap.rearrange("p (a b) -> p a b", b=b)

            def first_max(top, key, hot, values, width):
                step(dve.tensor_reduce(top, values, AX_X, ALU.max))
                step(dve.scalar_tensor_tensor(hot, values, top, falling[:, E - width:E], ALU.is_equal, ALU.mult))
                step(dve.tensor_reduce(key, hot, AX_X, ALU.max))
                step(dve.tensor_scalar(hot, hot, key, None, ALU.is_equal))

            def select(t):
                at, row = slice(t, t + 1), slice(t * E, (t + 1) * E)
                if t == 0:
                    dve.wait_ge(rt_in, 48)
                    step(dve.memset(before[:, 0:E], 0.0))
                first_max(gsum[:, at], ktop[:, at], og, logits[:, t, 0:G], G)
                dve.tensor_scalar(gx[:, t * G:(t + 1) * G], logits[:, t, 0:G], gsum[:, at], None, ALU.subtract)
                og3, em3 = og.unsqueeze(2).to_broadcast([P, G, EG]), v3(em, EG)
                step(dve.tensor_tensor(em3, v3(logits[:, t, G:RW], EG), og3, ALU.mult))
                step(dve.tensor_scalar(og, og, 1e30, -1e30, ALU.mult, ALU.add))
                step(dve.tensor_tensor(em3, em3, og3, ALU.add))
                first_max(vtop[:, 0, at], ktop[:, at], oh[:, 0, row], em, E)
                step(dve.scalar_tensor_tensor(em, oh[:, 0, row], -1e30, em, ALU.mult, ALU.add))
                first_max(vtop[:, 1, at], ktop[:, at], oh[:, 1, row], em, E)
                step(dve.tensor_tensor(mark[:, row], oh[:, 0, row], oh[:, 1, row], ALU.add))
                if t < LT - 1:
                    step(dve.tensor_tensor(before[:, (t + 1) * E:(t + 2) * E], before[:, row], mark[:, row], ALU.add))
                else:
                    dve.tensor_tensor(marks_all, before[:, row], mark[:, row], ALU.add).then_inc(marks_set, 1)

            def route_tile(t):
                b = banks.await_full(dve, ("rt", t))
                banks.release(dve.tensor_tensor(logits[:, t], ps[:, b, 0:RW], b_rt, ALU.add), ("rt", t))
                banks.await_read(dve, ("rt", t))
                select(t)

            def modulate_tile(t):
                b = banks.await_full(dve, ("x2T", t, 1))
                for j in range(4, KT):
                    ins = dve.tensor_scalar(h2T[:, t % 2, j, :], ps[:, b, (j - 4) * P:(j - 3) * P], ffn_scale[:, j:j + 1],
                                            modc[:, 3, 0, j:j + 1], ALU.mult, ALU.add)
                banks.release(ins, ("x2T", t, 1))

            for u in range(LT + 2):
                if 2 <= u < LT:
                    route_tile(u - 2)
                if 1 <= u <= LT:
                    modulate_tile(u - 1)
                if u >= LT:
                    route_tile(u - 2)
                if u < LT:
                    dve.wait_ge(y_ss, u + 1)
                    dve.tensor_tensor(ry[:, u:u + 1], ssy[:, u, 0:1], ssy[:, u, 1:2], ALU.add).then_inc(y_sd, 1)
                    dve.wait_ge(x2_sd, u + 1)
                    step(dve.reciprocal(ry[:, u:u + 1], ry[:, u:u + 1]))
                    for half in range(2):
                        b = banks.await_full(dve, ("y", u, half))
                        banks.release(dve.scalar_tensor_tensor(x2[:, u, half * 512:(half + 1) * 512], ps[:, b, :], ry[:, u:u + 1],
                                                               gate1[:, half * 512:(half + 1) * 512], ALU.mult, ALU.mult), ("y", u, half))
                    for half in range(2):
                        banks.await_read(dve, ("y", u, half))
                    dve.wait_ge(xr_in, 16 * (u + 1))
                    dve.tensor_tensor(x2[:, u], x2[:, u], xr[:, u % 2], ALU.add).then_inc(x2_ready, 1)
                    dve.wait_ge(x2_ready, u + 1)
                    dve.wait_ge(x2_ss, u + 1)
                    step(dve.reciprocal(rz[:, u:u + 1], rz[:, u:u + 1]))
                    dve.tensor_scalar(xr[:, u % 2], x2[:, u], rz[:, u:u + 1], None, ALU.mult).then_inc(xn2_ready, 1)
            dve.wait_ge(xn_out, 16 * LT)

            rank, expert, base_k, q, r, pos, col = small[0], small[1], small[2], small[3], small[4], small[5], small[6]
            oh4 = oh.rearrange("p k (t e) -> p (k t) e", e=E)
            t3 = v3(tmp, LT * E)

            def look_up(dst, row):
                step(dve.tensor_tensor(v3(tmp, E), oh4, mid(row, TOPK * LT), ALU.mult))
                step(dve.tensor_reduce(dst, v3(tmp, E), AX_X, ALU.add))

            look_up(expert, iota[:, 0:E])
            b = banks.await_full(dve, ("count",))
            step(dve.tensor_tensor(cmp8[0:E, 0], ps[0:E, b, 0:8], steps[0:E, :], ALU.is_gt))
            step(dve.tensor_reduce(ext[0:E, :], cmp8[0:E, 0], AX_X, ALU.add))
            banks.release(dve.tensor_copy(ext_b[0:E, :], ext[0:E, :].to_broadcast([E, P])), ("count",))
            banks.await_read(dve, ("count",))
            dve.sem_inc(ext_set, 1)
            b = banks.await_full(dve, ("base",))
            dve.tensor_copy(base_row, ps[:, b, 0:E])
            dve.tensor_copy(n_ext, ps[:, b, E:E + 1])
            banks.release(dve.tensor_copy(end_col[0:E, :], ps[0:E, b, 64:65]), ("base",))
            banks.await_read(dve, ("base",))
            dve.tensor_scalar(flags[0:E, :], iota[0:E, 0:16], end_col[0:E, :], None, ALU.is_ge).then_inc(flag_set, 1)
            b = banks.await_full(dve, ("rank",))
            banks.release(dve.tensor_tensor(t3, oh, mid(ps[:, b, 0:LT * E], TOPK), ALU.mult), ("rank",))
            banks.await_read(dve, ("rank",))
            step(dve.tensor_reduce(rank, v3(tmp, E), AX_X, ALU.add))
            step(dve.tensor_tensor(cmp8, bc(rank, [P, TOPK * LT, 8]), mid(steps, TOPK * LT), ALU.is_ge))
            step(dve.tensor_reduce(q, cmp8, AX_X, ALU.add))
            step(dve.scalar_tensor_tensor(r, q, -float(P), rank, ALU.mult, ALU.add))
            look_up(base_k, base_row)
            step(dve.tensor_scalar(pos, q, 0.0, None, ALU.is_gt))
            step(dve.scalar_tensor_tensor(col, base_k, float(E - 1), q, ALU.add, ALU.add))
            step(dve.tensor_tensor(col, col, expert, ALU.subtract))
            step(dve.tensor_tensor(col, col, pos, ALU.mult))
            step(dve.tensor_tensor(col, col, expert, ALU.add))
            step(dve.scalar_tensor_tensor(dest, col, float(P), r, ALU.mult, ALU.add))
            step(dve.tensor_tensor(hot_c, mid(iota[:, 0:COLS + 2], TOPK * LT), bc(col, [P, TOPK * LT, COLS + 2]), ALU.is_equal))
            def row_ones(k):
                part = slice(k * LT, (k + 1) * LT)
                dve.tensor_tensor(hot_r[:, part], mid(iota, LT), bc(r[:, part], [P, LT, P]), ALU.is_equal).then_inc(hot_set[k], 1)

            hot4 = hot_c.rearrange("p (k t) c -> p k t c", t=LT)
            dve.tensor_tensor(hot4, hot4, tok_id.unsqueeze(1).unsqueeze(3).to_broadcast([P, TOPK, LT, COLS + 2]), ALU.mult).then_inc(col_set, 1)
            row_ones(0)
            row_ones(1)
            b = banks.await_full(dve, ("eid",))
            step(dve.memset(table[0:1, :], 0))
            step(dve.tensor_copy(table[0:1, 0:E], iota[0:1, 0:E]))
            banks.release(dve.tensor_scalar(table[0:1, E:COLS], ps[0:1, b, 0:16], float(E - 1), None, ALU.min), ("eid",))
            step(dve.tensor_scalar(table[0:1, 60:61], n_ext[0:1, :], float(E), None, ALU.add))
            b = banks.await_full(dve, ("idx",))
            banks.release(dve.tensor_copy(idx, ps[:, b, 0:COLS + 2]), ("idx",))
            banks.await_read(dve, ("idx",))
            dve.sem_inc(route_set, 1)

            def modulate_half():
                for j in range(4, KT):
                    ins = dve.tensor_scalar(xT[:, j, :], ps[:, 1, (j - 4) * P:(j - 3) * P], ffn_scale[:, j:j + 1],
                                            modc[:, 3, 0, j:j + 1], ALU.mult, ALU.add)
                ins.then_inc(xt_done, 1)

            def hidden_and_next(n, first):
                dve.wait_ge(u_full, n + 1)
                dve.wait_ge(hs_done, n + 1)
                if not first:
                    dve.wait_ge(ht_full, n)
                dve.tensor_tensor(hid, hh, ps[:, 3, :], ALU.mult).then_inc(h_done, 1)
                dve.wait_ge(xt_full, n + 2)
                modulate_half()

            def copy_out(n):
                dve.wait_ge(d_full, n)
                dve.wait_ge(y_out, 16 * n)
                dve.tensor_copy(yo[:, 512:D], ps[:, 6, :]).then_inc(y_done, 1)

            d8, e8, s8 = small[7][:, 0:LT], small[7][:, LT:2 * LT], ktop
            dve.wait_ge(route_set, 1)
            dve.tensor_tensor(d8, vtop[:, 1], vtop[:, 0], ALU.subtract).then_inc(r_exp, 1)
            dve.wait_ge(r_expd, 1)
            step(dve.tensor_reduce(gsum, v3(gx, G), AX_X, ALU.add))
            step(dve.tensor_scalar(s8, e8, 1.0, None, ALU.add))
            step(dve.tensor_tensor(s8, s8, gsum, ALU.mult))
            step(dve.reciprocal(cw[:, 0], s8))
            step(dve.tensor_tensor(cw[:, 1], cw[:, 0], e8, ALU.mult))
            dve.wait_ge(xt_full, 1)
            modulate_half()
            hidden_and_next(0, True)
            blocks = dve.value_load(table[0:1, 60:61], min_val=E, max_val=COLS - 1)
            with dve.Fori(1, blocks) as n:
                hidden_and_next(n, False)
                copy_out(n)
            copy_out(blocks)

            def combine(t):
                dve.wait_ge(f_y0, t + 1)
                dve.scalar_tensor_tensor(f_at(t, 0), f_at(t, 1), cw[:, 1, t:t + 1], f_at(t, 0), ALU.mult, ALU.add).then_inc(f_sum, 1)

            combine(0)
            for t in range(LT):
                if t + 1 < LT:
                    combine(t + 1)
                dve.wait_ge(f_sd, t + 1)
                step(dve.reciprocal(rf[:, t:t + 1], rf[:, t:t + 1]))
                step(dve.scalar_tensor_tensor(f_at(t, 0), f_at(t, 0), rf[:, t:t + 1], gate2, ALU.mult, ALU.mult))
                dve.tensor_tensor(x2[:, t], x2[:, t], f_at(t, 0), ALU.add).then_inc(f_done, 1)



def lay_out(inputs):
    a = {k: np.ascontiguousarray(v) for k, v in inputs.items()}
    a["q_gain_cols"] = a.pop("mla_q_norm")[0].reshape(2, 128).T
    w_in = a.pop("w_in")[0]
    q, kv, kr, qkv, zz, b, g = np.split(w_in, np.cumsum([256, 128, 32, 1536, 512, 8, 8])[:-1].tolist(), axis=1)
    swap = np.arange(32) ^ 1
    a["w_in_a"] = np.concatenate([q, kv, b, g], axis=1)
    a["w_in_r"] = np.concatenate([kr, kr[:, swap]] * 2, axis=1)
    a["w_in_z"], a["w_in_qkv"] = zz, qkv
    a["conv_cols"] = a.pop("dn_conv")[0].reshape(5, 12, 128).transpose(2, 1, 0).reshape(128, 60)
    wq = a.pop("w_q_up")[0].reshape(256, 8, 96)
    a["w_q_up4"] = np.concatenate([wq, wq[:, :, 64 + swap]], axis=2).reshape(256, 1024)
    wkv = a.pop("w_kv_up")[0].reshape(128, 8, 128)
    a["w_k_up"] = wkv[:, :, :64].reshape(128, 512)
    a["w_v_up"] = wkv[:, :, 64:].reshape(128, 512)
    a["w_router"] = np.concatenate([a.pop("w_router_group")[0], a.pop("w_router_expert")[0].transpose(1, 0, 2).reshape(1024, 32)], axis=1)
    a["b_router"] = np.concatenate([a.pop("b_router_group")[0], a.pop("b_router_expert")[0].reshape(32)])
    return {k: np.ascontiguousarray(v) for k, v in a.items()}


def kernel(**inputs):
    import concourse.bacc as bacc
    from concourse.bass_utils import run_bass_kernel_spmd

    nc = bacc.Bacc("TRN2", target_bir_lowering=False, num_devices=1)
    arrays = lay_out(inputs)
    arrays.update({f"k_{k}": v for k, v in shape_constants().items()})
    io, feed = {}, {}
    for name, a in arrays.items():
        feed[f"in_{name}"] = a
        io[name] = nc.dram_tensor(f"in_{name}", a.shape, mybir.dt.from_np(a.dtype), kind="ExternalInput").ap()
    io["out"] = nc.dram_tensor("out", (1, SEQ, D), F32, kind="ExternalOutput").ap()
    hybrid_block_kernel(nc, io)
    result = run_bass_kernel_spmd(nc, [feed], core_ids=[0])
    return result.results[0]["out"]
```
